# Optimizing a Trainium2 kernel written in Bass

```python
import math
import jax
import jax.numpy as jnp
from jax import lax
import numpy as np

D_MODEL = 1024
BATCH = 1
SEQ = 256
DEPTH = 2
DEC_BATCH = 1
DEC_SEQ = 512
PAST_LEN = 128

N_MIXERS = 2
N_A_LAYERS = (DEPTH + 1) // 2
N_B_LAYERS = DEPTH // 2

HA = 16
Q_LORA = 384
KV_LORA = 256
DN = 64
DR = 32
DV = 64
ROPE_THETA_A = 10000.0

HB = 16
KVB = 8
HD = 128
ROPE_THETA_B = 10000.0
GRID_W = 64

N_EXPERTS = 16
EXPERT_FF = 1024
EC_CAPACITY_FACTOR = 2

Q_BLOCK = 128
RMS_EPS = 1e-6

kernel_name = "hybrid_mla_axialgqa_ec_moe_encoder"

def _rms(x, g):
    xf = x.astype(jnp.float32)
    y = xf * lax.rsqrt(jnp.mean(xf * xf, axis=-1, keepdims=True) + RMS_EPS)
    return y.astype(x.dtype) * g

def _rope(x, pos, theta):
    d = x.shape[-1]
    half = d // 2
    inv = theta ** (-(jnp.arange(half, dtype=jnp.float32) * 2.0 / d))
    ang = pos[:, None] * inv[None, :]
    cos = jnp.cos(ang)[:, None, :]
    sin = jnp.sin(ang)[:, None, :]
    xf = x.astype(jnp.float32)
    x1, x2 = xf[..., :half], xf[..., half:]
    out = jnp.concatenate([x1 * cos - x2 * sin, x1 * sin + x2 * cos], axis=-1)
    return out.astype(x.dtype)

def _axial_rope(x, row, col):
    half = x.shape[-1] // 2
    return jnp.concatenate([_rope(x[..., :half], row, ROPE_THETA_B),
                            _rope(x[..., half:], col, ROPE_THETA_B)], axis=-1)

def _block_attention(q, k, v, scale):
    b, s, h, dk = q.shape
    hk = k.shape[2]
    g = h // hk
    nb = s // Q_BLOCK
    qb = q.reshape(b, nb, Q_BLOCK, hk, g, dk).transpose(1, 0, 2, 3, 4, 5)

    def one_block(qi):
        sc = jnp.einsum('bqkgd,bskd->bkgqs', qi, k,
                        preferred_element_type=jnp.float32) * scale
        p = jax.nn.softmax(sc, axis=-1).astype(v.dtype)
        return jnp.einsum('bkgqs,bskd->bqkgd', p, v)

    out = lax.map(one_block, qb)
    return out.transpose(1, 0, 2, 3, 4, 5).reshape(b, s, h, v.shape[-1])

def _mla(h, w_in, g_q, w_uq, g_kv, w_ukv, w_o, pos):
    b, s, _ = h.shape
    proj = h @ w_in
    c_q = proj[..., :Q_LORA]
    c_kv = proj[..., Q_LORA:Q_LORA + KV_LORA]
    k_r = proj[..., Q_LORA + KV_LORA:]
    q = (_rms(c_q, g_q) @ w_uq).reshape(b, s, HA, DN + DR)
    q = jnp.concatenate([q[..., :DN], _rope(q[..., DN:], pos, ROPE_THETA_A)], axis=-1)
    k_r = _rope(k_r[:, :, None, :], pos, ROPE_THETA_A)
    kv = (_rms(c_kv, g_kv) @ w_ukv).reshape(b, s, HA, DN + DV)
    k = jnp.concatenate([kv[..., :DN], jnp.broadcast_to(k_r, (b, s, HA, DR))], axis=-1)
    v = kv[..., DN:]
    o = _block_attention(q, k, v, (DN + DR) ** -0.5)
    return o.reshape(b, s, HA * DV) @ w_o

def _gqa_axial(h, w_qkv, g_qn, g_kn, w_o, row, col):
    b, s, _ = h.shape
    proj = h @ w_qkv
    q = proj[..., :HB * HD].reshape(b, s, HB, HD)
    k = proj[..., HB * HD:(HB + KVB) * HD].reshape(b, s, KVB, HD)
    v = proj[..., (HB + KVB) * HD:].reshape(b, s, KVB, HD)
    q = _axial_rope(_rms(q, g_qn), row, col)
    k = _axial_rope(_rms(k, g_kn), row, col)
    o = _block_attention(q, k, v, HD ** -0.5)
    return o.reshape(b, s, HB * HD) @ w_o

def _ec_moe(h, w_r, w_g, w_u, w_d):
    b, s, d = h.shape
    n = b * s
    cap = EC_CAPACITY_FACTOR * n // N_EXPERTS
    t = h.reshape(n, d)
    aff = jax.nn.softmax((t @ w_r).astype(jnp.float32), axis=-1)
    gate, idx = lax.top_k(aff.T, cap)
    xe = t[idx]
    hid = jax.nn.silu(jnp.einsum('ecd,edf->ecf', xe, w_g)) * jnp.einsum('ecd,edf->ecf', xe, w_u)
    ye = jnp.einsum('ecf,efd->ecd', hid, w_d) * gate[..., None].astype(t.dtype)
    out = jnp.zeros_like(t).at[idx.reshape(-1)].add(ye.reshape(-1, d))
    return out.reshape(b, s, d)

def _trunk(x, g_attn_a, w_in_a, g_q_a, w_uq_a, g_kv_a, w_ukv_a, w_o_a,
           g_attn_b, w_qkv_b, g_qn_b, g_kn_b, w_o_b,
           g_ffn, w_router, w_gate, w_up, w_down, g_final):
    s = x.shape[1]
    rows = s // GRID_W
    pos = jnp.arange(s, dtype=jnp.float32)
    row = jnp.repeat(jnp.arange(rows, dtype=jnp.float32), GRID_W)
    col = jnp.tile(jnp.arange(GRID_W, dtype=jnp.float32), rows)
    for i in range(DEPTH):
        j = i // N_MIXERS
        if i % N_MIXERS == 0:
            x = x + _mla(_rms(x, g_attn_a[j]), w_in_a[j], g_q_a[j], w_uq_a[j],
                         g_kv_a[j], w_ukv_a[j], w_o_a[j], pos)
        else:
            x = x + _gqa_axial(_rms(x, g_attn_b[j]), w_qkv_b[j], g_qn_b[j], g_kn_b[j],
                               w_o_b[j], row, col)
        x = x + _ec_moe(_rms(x, g_ffn[i]), w_router[i], w_gate[i], w_up[i], w_down[i])
    return _rms(x, g_final)

def setup_inputs(seed: int = 0) -> dict:
    key = jax.random.key(seed)
    ks = jax.random.split(key, 24)

    def nrm(k, shape, scale):
        return jax.random.normal(k, shape, dtype=jnp.float32) * scale

    def gain(k, shape):
        return 1.0 + 0.01 * jax.random.normal(k, shape, dtype=jnp.float32)

    D = D_MODEL
    return {
        "x_prompt": nrm(ks[0], (BATCH, SEQ, D), 1.0),
        "x_sample": nrm(ks[1], (DEC_BATCH, DEC_SEQ, D), 1.0),
        "g_attn_a": gain(ks[2], (N_A_LAYERS, D)),
        "w_in_a": nrm(ks[3], (N_A_LAYERS, D, Q_LORA + KV_LORA + DR), D ** -0.5),
        "g_q_a": gain(ks[4], (N_A_LAYERS, Q_LORA)),
        "w_uq_a": nrm(ks[5], (N_A_LAYERS, Q_LORA, HA * (DN + DR)), Q_LORA ** -0.5),
        "g_kv_a": gain(ks[6], (N_A_LAYERS, KV_LORA)),
        "w_ukv_a": nrm(ks[7], (N_A_LAYERS, KV_LORA, HA * (DN + DV)), KV_LORA ** -0.5),
        "w_o_a": nrm(ks[8], (N_A_LAYERS, HA * DV, D), (HA * DV) ** -0.5),
        "g_attn_b": gain(ks[9], (N_B_LAYERS, D)),
        "w_qkv_b": nrm(ks[10], (N_B_LAYERS, D, (HB + 2 * KVB) * HD), D ** -0.5),
        "g_qn_b": gain(ks[11], (N_B_LAYERS, HD)),
        "g_kn_b": gain(ks[12], (N_B_LAYERS, HD)),
        "w_o_b": nrm(ks[13], (N_B_LAYERS, HB * HD, D), (HB * HD) ** -0.5),
        "g_ffn": gain(ks[14], (DEPTH, D)),
        "w_router": nrm(ks[15], (DEPTH, D, N_EXPERTS), D ** -0.5),
        "w_gate": nrm(ks[16], (DEPTH, N_EXPERTS, D, EXPERT_FF), D ** -0.5),
        "w_up": nrm(ks[17], (DEPTH, N_EXPERTS, D, EXPERT_FF), D ** -0.5),
        "w_down": nrm(ks[18], (DEPTH, N_EXPERTS, EXPERT_FF, D), EXPERT_FF ** -0.5),
        "g_final": gain(ks[19], (D,)),
    }

def reference(x_prompt, x_sample, g_attn_a, w_in_a, g_q_a, w_uq_a, g_kv_a, w_ukv_a, w_o_a,
              g_attn_b, w_qkv_b, g_qn_b, g_kn_b, w_o_b,
              g_ffn, w_router, w_gate, w_up, w_down, g_final):
    y_prompt = _trunk(x_prompt, g_attn_a, w_in_a, g_q_a, w_uq_a, g_kv_a, w_ukv_a, w_o_a,
                      g_attn_b, w_qkv_b, g_qn_b, g_kn_b, w_o_b,
                      g_ffn, w_router, w_gate, w_up, w_down, g_final)
    y_sample = _trunk(x_sample, g_attn_a, w_in_a, g_q_a, w_uq_a, g_kv_a, w_ukv_a, w_o_a,
                      g_attn_b, w_qkv_b, g_qn_b, g_kn_b, w_o_b,
                      g_ffn, w_router, w_gate, w_up, w_down, g_final)
    return (y_prompt, y_sample)


_drawn_inputs = setup_inputs


def setup_inputs(seed=0):
    import zlib

    import numpy as np

    out = dict(_drawn_inputs(seed))
    spreads = {}
    factors = {'g_attn_a': 7.171,
     'g_q_a': 8.0,
     'g_kv_a': 8.0,
     'g_attn_b': 8.0,
     'g_qn_b': 8.0,
     'g_kn_b': 8.0,
     'g_ffn': 3.274,
     'g_final': 5.678}
    for name, (base, spread) in spreads.items():
        noise = np.random.default_rng([zlib.crc32(name.encode()), seed]).standard_normal(out[name].shape)
        drawn = base * np.exp(spread * noise) if base else spread * noise
        out[name] = jnp.asarray(drawn.astype(out[name].dtype))
    for name, factor in factors.items():
        out[name] = (out[name] * factor).astype(out[name].dtype)
    return out
```

```python
from contextlib import ExitStack

import numpy as np

import concourse.bass as bass
from concourse import mybir

F32 = mybir.dt.float32
F32R = mybir.dt.float32r
U32 = mybir.dt.uint32
ALU = mybir.AluOpType
ACT = mybir.ActivationFunctionType
AX = mybir.AxisListType

P = 128
D = 1024
KD = D // P
PROMPT, SAMPLE = 256, 512
N = PROMPT + SAMPLE
TILES = N // P
PROMPT_TILES = PROMPT // P
EPS = 1e-6

HEADS = 16
GROUPS = HEADS // 2
Q_LORA, KV_LORA, DN, DR, DV = 384, 256, 64, 32, 64
KQ, KKV = Q_LORA // P, KV_LORA // P
W_IN = Q_LORA + KV_LORA + DR
ARENA_FREE_A = KD * W_IN + KQ * HEADS * (DN + DR) + KKV * HEADS * (DN + DV)
HD = 128
KV_HEADS = 8
THETA = 10000.0
GRID_W = 64

EXPERTS = 16
FF = 1024
CAP_P = 2 * PROMPT // EXPERTS
CAP_S = 2 * SAMPLE // EXPERTS
CAP = CAP_P + CAP_S

UNITS = [(0, 0), (0, 1), (2, 0), (4, 0), (2, 1), (4, 1)]
NU = len(UNITS)

SLOTS = 12
SLOT = 2 * D
SPLITS = 4


def keys_of(unit):
    return (0, PROMPT_TILES) if UNITS[unit][0] < PROMPT_TILES else (PROMPT_TILES, TILES - PROMPT_TILES)


def wait(engine, semaphore, count):
    if isinstance(count, int) and count <= 0:
        return
    engine.wait_ge(semaphore, count)


class Space:

    def __init__(self, nc, stack, prefix):
        self.nc, self.stack, self.prefix, self.sems = nc, stack, prefix, []

    def sb(self, name, shape, dtype=F32):
        return self.stack.enter_context(self.nc.sbuf_tensor(self.prefix + name, shape, dtype))

    def psum(self, name, shape, dtype=F32):
        return self.stack.enter_context(self.nc.psum_tensor(self.prefix + "ps_" + name, shape, dtype))

    def sem(self, name):
        self.sems.append(self.nc.alloc_semaphore(self.prefix + name))
        return self.sems[-1]

    def end(self):
        self.nc.clear_and_free_semaphores(self.sems)
        self.nc.all_engine_barrier()


def token_rows(x_prompt, x_sample, t):
    if t < PROMPT_TILES:
        return x_prompt[0, t * P:(t + 1) * P, :]
    return x_sample[0, (t - PROMPT_TILES) * P:(t - PROMPT_TILES + 1) * P, :]


def row_broadcast(vector):
    return vector.partition_broadcast(P)



class InputNorm:

    def __init__(self, s, x_tile_of, gain_row, xnT, psum, x, xn, junk, gain):
        self.x_tile_of, self.gain_row, self.xnT, self.ps = x_tile_of, gain_row, xnT, psum
        self.x, self.xn, self.junk, self.gain = x, xn, junk, gain
        self.ssq = s.sb("norm_ssq", [P, TILES])
        self.mean = s.sb("norm_mean", [P, TILES])
        self.rstd = s.sb("norm_rstd", [P, TILES])
        self.x_landed = [s.sem("norm_x_landed0"), s.sem("norm_x_landed1")]
        self.gain_landed = s.sem("norm_gain_landed")
        self.ssq_ready = s.sem("norm_ssq_ready")
        self.mean_ready = s.sem("norm_mean_ready")
        self.rstd_ready = s.sem("norm_rstd_ready")
        self.xn_ready = s.sem("norm_xn_ready")
        self.turned = s.sem("norm_turned")
        self.copied_act = s.sem("norm_copied_act")
        self.copied_dve = s.sem("norm_copied_dve")

    def act_tile(self, act, t):
        act.wait_ge(self.x_landed[t % 2], 16 * (t // 2 + 1))
        wait(act, self.ssq_ready, t)
        act.activation(self.junk, self.x[:, t % 2, :], ACT.Square,
                       accum_out=self.ssq[:, t:t + 1]).then_inc(self.ssq_ready, 1)

    def act_copy(self, act, t):
        act.wait_ge(self.turned, t + 1)
        act.activation(self.xnT[:, 0:KD // 2, t * P:(t + 1) * P], self.ps[:, 0, :, :],
                       ACT.Copy).then_inc(self.copied_act, 1)

    def pool_tile(self, pool, t, half):
        pool.wait_ge(self.ssq_ready, t + 1)
        pool.tensor_scalar(self.mean[:, t:t + 1], self.ssq[:, t:t + 1], 1.0 / D, EPS,
                           ALU.mult, ALU.add).then_inc(self.mean_ready, 1)
        pool.wait_ge(self.mean_ready, t + 1)
        pool.tensor_tensor(self.rstd[:, t:t + 1], self.mean[:, t:t + 1], half,
                           ALU.pow).then_inc(self.rstd_ready, 1)

    def dve_tile(self, dve, t):
        if t == 0:
            dve.wait_ge(self.gain_landed, 16)
        dve.wait_ge(self.x_landed[t % 2], 16 * (t // 2 + 1))
        dve.wait_ge(self.rstd_ready, t + 1)
        wait(dve, self.turned, t - 1)
        dve.scalar_tensor_tensor(out=self.xn[:, t % 2, :], in0=self.x[:, t % 2, :],
                                 scalar=self.rstd[:, t:t + 1], in1=self.gain,
                                 op0=ALU.mult, op1=ALU.mult).then_inc(self.xn_ready, 1)

    def dve_copy(self, dve, t):
        dve.wait_ge(self.turned, t + 1)
        dve.tensor_copy(self.xnT[:, KD // 2:KD, t * P:(t + 1) * P],
                        self.ps[:, 1, :, :]).then_inc(self.copied_dve, 1)

    def pe_tile(self, pe, t, ident):
        pe.wait_ge(self.xn_ready, t + 1)
        wait(pe, self.copied_act, t)
        wait(pe, self.copied_dve, t)
        for k in range(KD):
            last = pe.transpose(self.ps[:, k // 4, k % 4, :], self.xn[:, t % 2, k * P:(k + 1) * P], ident)
        last.then_inc(self.turned, 1)



class Core:

    def __init__(self, s, dk, dv, scale, o_dram):
        self.dk, self.dv, self.scale, self.o_dram = dk, dv, scale, o_dram
        self.S = s.psum("scores", [P, 2, 2, SAMPLE])
        self.T = s.psum("probsT", [P, 2, 4, P])
        self.proj = s.psum("projected", [P, 2, SAMPLE])
        self.probs = s.sb("probs", [P, 2, 2, SAMPLE])
        self.probsT = s.sb("probsT_sb", [P, 2, 4, P])
        self.out = s.sb("out", [P, 2, TILES, 2 * dv])
        self.rowmax = s.sb("rowmax", [P, 2, 2])
        self.negmax = s.sb("negmax", [P, 2, 2])
        self.rowsum = s.sb("rowsum", [P, 2, 2])
        self.rinv = s.sb("rinv", [P, 2, 2])
        self.scores_done = s.sem("scores_done")
        self.rowmax_done = s.sem("rowmax_done")
        self.negmax_done = s.sem("negmax_done")
        self.exp_done = s.sem("exp_done")
        self.turned = s.sem("probs_turned")
        self.copied_act = s.sem("probs_copied_act")
        self.copied_dve = s.sem("probs_copied_dve")
        self.rinv_done = s.sem("rinv_done")
        self.pv_done = s.sem("pv_done")
        self.out_done = s.sem("out_done")
        self.stored = [s.sem("stored0"), s.sem("stored1")]


    def pe_scores(self, pe, n, unit, qT, kT, q_index, k_index):
        wait(pe, self.exp_done, 2 * n - 2)
        key, nk = keys_of(unit)
        tile, _ = UNITS[unit]
        for j in range(2):
            last = pe.matmul(self.S[:, unit % 2, j, 0:nk * P],
                             qT[0:self.dk, q_index, (tile + j) * P:(tile + j + 1) * P],
                             kT[0:self.dk, k_index, key * P:(key + nk) * P], start=True, stop=True)
        last.then_inc(self.scores_done, 1)

    def pe_turn(self, pe, n, unit, ident):
        _, nk = keys_of(unit)
        for j in range(2):
            pe.wait_ge(self.exp_done, 2 * n + j + 1)
            wait(pe, self.out_done, 2 * n - 1 + j)
            for k in range(nk):
                last = pe.transpose(self.T[:, j, k, :], self.probs[:, unit % 2, j, k * P:(k + 1) * P], ident)
            last.then_inc(self.turned, 1)

    def pe_pv(self, pe, n, unit, v_of):
        key, nk = keys_of(unit)
        for j in range(2):
            pe.wait_ge(self.copied_act if j == 0 else self.copied_dve, n + 1)
            for k in range(nk):
                last = pe.matmul(self.T[:, j, 0, 0:self.dv], self.probsT[:, j, k, :], v_of(key + k),
                                 start=(k == 0), stop=(k == nk - 1))
            last.then_inc(self.pv_done, 1)


    def act_exp(self, act, n, unit):
        _, nk = keys_of(unit)
        act.wait_ge(self.negmax_done, n + 1)
        wait(act, self.turned, 2 * n - 2)
        wait(act, self.rinv_done, n - 1)
        for j in range(2):
            act.activation(self.probs[:, unit % 2, j, 0:nk * P], self.S[:, unit % 2, j, 0:nk * P], ACT.Exp,
                           bias=self.negmax[:, unit % 2, j:j + 1], scale=self.scale,
                           accum_out=self.rowsum[:, unit % 2, j:j + 1]).then_inc(self.exp_done, 1)

    def act_copy(self, act, n, unit):
        _, nk = keys_of(unit)
        act.wait_ge(self.turned, 2 * n + 1)
        wait(act, self.pv_done, 2 * n - 1)
        act.activation(self.probsT[:, 0, 0:nk, :], self.T[:, 0, 0:nk, :], ACT.Copy).then_inc(self.copied_act, 1)


    def dve_max(self, dve, n, unit):
        _, nk = keys_of(unit)
        dve.wait_ge(self.scores_done, n + 1)
        wait(dve, self.negmax_done, n)
        dve.tensor_reduce(self.rowmax[:, unit % 2, :], self.S[:, unit % 2, :, 0:nk * P], AX.X,
                          ALU.max).then_inc(self.rowmax_done, 1)
        dve.wait_ge(self.rowmax_done, n + 1)
        wait(dve, self.exp_done, 2 * n - 2)
        dve.tensor_scalar(self.negmax[:, unit % 2, :], self.rowmax[:, unit % 2, :], -self.scale, None,
                          ALU.mult).then_inc(self.negmax_done, 1)

    def dve_copy(self, dve, n, unit):
        _, nk = keys_of(unit)
        dve.wait_ge(self.turned, 2 * n + 2)
        wait(dve, self.pv_done, 2 * n)
        dve.tensor_copy(self.probsT[:, 1, 0:nk, :], self.T[:, 1, 0:nk, :]).then_inc(self.copied_dve, 1)

    def dve_rinv(self, dve, n, unit):
        dve.wait_ge(self.exp_done, 2 * n + 2)
        wait(dve, self.out_done, 2 * n)
        dve.reciprocal(self.rinv[:, unit % 2, :], self.rowsum[:, unit % 2, :]).then_inc(self.rinv_done, 1)

    def dve_out(self, dve, g, n, unit, slot, first):
        tile, head = UNITS[unit]
        dve.wait_ge(self.rinv_done, n + 1)
        for j in range(2):
            dve.wait_ge(self.pv_done, 2 * n + j + 1)
            if unit == 0 and j == 0 and not first:
                self.wait_stored(dve, g, slot)
            dve.tensor_scalar(self.out[:, slot, tile + j, head * self.dv:(head + 1) * self.dv],
                              self.T[:, j, 0, 0:self.dv], self.rinv[:, unit % 2, j:j + 1], None,
                              ALU.mult).then_inc(self.out_done, 1)

    def wait_stored(self, dve, g, slot):
        dve.wait_ge(self.stored[slot], 8 * (g - slot))


    def store(self, sp, g, slot):
        sp.wait_ge(self.out_done, 2 * NU * g + 2 * NU)
        sp.dma_start(self.o_dram[:, :, bass.ds(g * 2 * self.dv, 2 * self.dv)],
                     self.out[:, slot, :, :]).then_inc(self.stored[slot], 16)


def loop_groups(engine, step):
    step(0, 0, True, False)
    with engine.Fori(0, (GROUPS - 2) // 2) as i:
        step(i * 2 + 1, 1, False, False)
        step(i * 2 + 2, 0, False, False)
    step(GROUPS - 1, (GROUPS - 1) % 2, False, True)


def mla_block(nc, io, shared):
    with ExitStack() as stack:
        s = Space(nc, stack, "a_")
        arena = shared.raw.rearrange("p s n -> p (s n)")
        w_in = arena[:, 0:KD * W_IN].rearrange("p (k n) -> p k n", k=KD)
        at = KD * W_IN
        w_uq = arena[:, at:at + KQ * HEADS * (DN + DR)].rearrange("p (k n) -> p k n", k=KQ)
        at += KQ * HEADS * (DN + DR)
        w_ukv = arena[:, at:at + KKV * HEADS * (DN + DV)].rearrange("p (k n) -> p k n", k=KKV)
        w_ukv_heads = arena[:, at:at + KKV * HEADS * (DN + DV)].rearrange("p (k h n) -> p k h n", k=KKV, n=DN + DV)

        xnT = s.sb("xnT", [P, KD, N])
        c_norm = s.sb("c_norm", [P, 2, Q_LORA + KV_LORA])
        c_gain = s.sb("c_gain", [P, Q_LORA + KV_LORA])
        cT = s.sb("cT", [P, KQ + KKV, N])
        squares = s.sb("c_squares", [P, Q_LORA])
        c_ssq = s.sb("c_ssq", [P, TILES, 2])
        c_mean = s.sb("c_mean", [P, TILES, 2])
        c_rstd = s.sb("c_rstd", [P, TILES, 2])
        half = s.sb("minus_half", [P, 2])
        rope_tok = s.sb("rope_tok", [P, TILES, 2, DR])
        rope_T = s.sb("rope_T", [P, N])
        kr = s.sb("kr", [P, 2, 3, DR])
        qT = s.sb("qT", [DN + DR, 4, N])
        kT = s.sb("kT", [DN + DR, 4, N])
        V = s.sb("V", [P, 2, TILES, 2 * DV])
        stage_q = s.sb("stage_q", [P, 2, KQ, P])
        stage_k = s.sb("stage_k", [P, KKV, P])
        qr = s.sb("qr", [DN + DR, 2, SAMPLE])
        core = Core(s, DN + DR, DV, (DN + DR) ** -0.5, io.o_a.rearrange("(t p) n -> p t n", p=P))
        norm = InputNorm(s, lambda t: token_rows(io.x_prompt, io.x_sample, t), row_broadcast(io.g_attn_a[0]),
                         xnT, core.S[:, 0, :, :].rearrange("p b (k n) -> p b k n", n=P),
                         x=arena[:, ARENA_FREE_A:ARENA_FREE_A + 2 * D].rearrange("p (b n) -> p b n", b=2),
                         xn=core.probs[:, :, :, :].rearrange("p b j n -> p b (j n)"),
                         junk=core.probsT[:, :, :, :].rearrange("p j k n -> p (j k n)"),
                         gain=V[:, :, :, :].rearrange("p b t n -> p (b t n)")[:, 0:D])
        c_raw = core.out[:, :, :, :].rearrange("p b t n -> p b (t n)")[:, :, 0:W_IN]
        c_ps = core.S[:, 1, :, :]
        cT_ps = core.proj[:, :, :].rearrange("p b (k n) -> p b k n", n=P)

        w_in_landed, w_uq_landed, w_ukv_landed = s.sem("w_in_landed"), s.sem("w_uq_landed"), s.sem("w_ukv_landed")
        tables_landed = s.sem("tables_landed")
        half_ready = s.sem("half_ready")
        c_done, c_copied = s.sem("c_done"), s.sem("c_copied")
        c_squared, c_mean_ready, c_rstd_ready = s.sem("c_squared"), s.sem("c_mean_ready"), s.sem("c_rstd_ready")
        c_normed, kr_parts, kr_ready = s.sem("c_normed"), s.sem("kr_parts"), s.sem("kr_ready")
        cT_done, cT_copied, krT_copied = s.sem("cT_done"), s.sem("cT_copied"), s.sem("krT_copied")
        q_staged, k_staged = s.sem("q_staged"), s.sem("k_staged")
        piece_done, piece_act = s.sem("piece_done"), s.sem("piece_act")
        qr_parts, piece_dve = s.sem("qr_parts"), s.sem("piece_dve")

        ROPES = [1, 2, 2, 3, 4, 4]
        block = stack.enter_context(nc.Block())

        @block.sync
        def _(sp):
            sp.dma_start(shared.ident[:, :], io.ident).then_inc(shared.ident_landed, 16)
            sp.dma_start(norm.gain, norm.gain_row).then_inc(norm.gain_landed, 16)
            for t in range(2):
                sp.dma_start(norm.x[:, t, :], norm.x_tile_of(t)).then_inc(norm.x_landed[t], 16)
            sp.dma_start(w_in, io.w_in_a[0].rearrange("(k p) n -> p k n", p=P)).then_inc(w_in_landed, 16)
            sp.dma_start(c_gain[:, 0:Q_LORA], row_broadcast(io.g_q_a[0])).then_inc(tables_landed, 16)
            sp.dma_start(c_gain[:, Q_LORA:], row_broadcast(io.g_kv_a[0])).then_inc(tables_landed, 16)
            sp.dma_start(rope_tok[:, :, :, :], io.rope_a_tok).then_inc(tables_landed, 16)
            sp.dma_start(rope_T[2 * DR:, :], io.rope_a_T).then_inc(tables_landed, 16)
            for t in range(2, TILES):
                sp.wait_ge(norm.xn_ready, t - 1)
                sp.dma_start(norm.x[:, t % 2, :], norm.x_tile_of(t)).then_inc(norm.x_landed[t % 2], 16)
            sp.dma_start(w_uq, io.w_uq_a[0].rearrange("(k p) n -> p k n", p=P)).then_inc(w_uq_landed, 16)
            sp.dma_start(w_ukv, io.w_ukv_a[0].rearrange("(k p) n -> p k n", p=P)).then_inc(w_ukv_landed, 16)
            sp.dma_start(shared.w_o_a, io.w_o_a[0].rearrange("(k p) n -> p k n", p=P)).then_inc(shared.w_o_landed, 16)
            loop_groups(sp, lambda g, slot, first, last: core.store(sp, g, slot))
            for slot in range(2):
                sp.wait_ge(core.stored[slot], 16 * GROUPS // 2)

        @block.gpsimd
        def _(pool):
            pool.memset(half[:, :], -0.5).then_inc(half_ready, 1)
            pool.wait_ge(half_ready, 1)
            for t in range(TILES):
                norm.pool_tile(pool, t, half[:, 0:1])
            for t in range(TILES):
                pool.wait_ge(c_squared, 2 * t + 2)
                pool.tensor_scalar(c_mean[:, t, 0:1], c_ssq[:, t, 0:1], 1.0 / Q_LORA, EPS,
                                   ALU.mult, ALU.add).then_inc(c_mean_ready, 1)
                pool.tensor_scalar(c_mean[:, t, 1:2], c_ssq[:, t, 1:2], 1.0 / KV_LORA, EPS,
                                   ALU.mult, ALU.add).then_inc(c_mean_ready, 1)
                pool.wait_ge(c_mean_ready, 2 * t + 2)
                pool.tensor_tensor(c_rstd[:, t, :], c_mean[:, t, :], half[:, :], ALU.pow).then_inc(c_rstd_ready, 1)
            pool.wait_ge(w_uq_landed, 16)
            pool.wait_ge(w_ukv_landed, 16)

            def stage(g):
                wait(pool, piece_done, NU * g - 3)
                pool.tensor_copy(stage_k[:, :, :].rearrange("p k (h n) -> p k h n", h=2),
                                 w_ukv_heads[:, :, bass.ds(g * 2, 2), 0:DN]).then_inc(k_staged, 1)
                for h in range(2):
                    wait(pool, piece_done, NU * g - 2 + h)
                    at = (g * 2 + h) * (DN + DR)
                    pool.tensor_copy(stage_q[:, h, :, 0:DN + DR], w_uq[:, :, bass.ds(at, DN + DR)])
                    pool.tensor_copy(stage_q[:, h, :, DN + DR:DN + DR + DR // 2],
                                     w_uq[:, :, bass.ds(at + DN + DR // 2, DR // 2)])
                    pool.tensor_copy(stage_q[:, h, :, DN + DR + DR // 2:],
                                     w_uq[:, :, bass.ds(at + DN, DR // 2)]).then_inc(q_staged, 1)

            stage(0)
            stage(1)
            with pool.Fori(2, GROUPS) as g:
                stage(g)

        @block.scalar
        def _(act):
            for t in range(TILES):
                norm.act_tile(act, t)
                if t:
                    norm.act_copy(act, t - 1)
            norm.act_copy(act, TILES - 1)
            for t in range(TILES):
                act.wait_ge(c_done, t + 1)
                wait(act, c_normed, t - 1)
                wait(act, kr_parts, 3 * (t - 1))
                act.activation(c_raw[:, t % 2, 0:SAMPLE], c_ps[:, 0, :], ACT.Copy)
                act.activation(c_raw[:, t % 2, SAMPLE:], c_ps[:, 1, 0:W_IN - SAMPLE], ACT.Copy).then_inc(c_copied, 1)
                act.wait_ge(c_copied, t + 1)
                wait(act, c_squared, 2 * t)
                act.activation(squares[:, :], c_raw[:, t % 2, 0:Q_LORA], ACT.Square,
                               accum_out=c_ssq[:, t, 0:1]).then_inc(c_squared, 1)
                act.wait_ge(c_squared, 2 * t + 1)
                act.activation(squares[:, 0:KV_LORA], c_raw[:, t % 2, Q_LORA:Q_LORA + KV_LORA], ACT.Square,
                               accum_out=c_ssq[:, t, 1:2]).then_inc(c_squared, 1)
                act.wait_ge(cT_done, t + 1)
                act.activation(cT[:, 0:4, t * P:(t + 1) * P], cT_ps[:, 0, :, :], ACT.Copy)
                act.activation(cT[:, 4:5, t * P:(t + 1) * P], cT_ps[:, 1, 0:1, :], ACT.Copy).then_inc(cT_copied, 1)

            def piece(g, slot, p):
                act.wait_ge(piece_done, NU * g + p + 1)
                if not (isinstance(g, int) and g < 2):
                    act.wait_ge(core.scores_done, NU * g - NU)
                    act.wait_ge(core.pv_done, 2 * NU * g - 2 * NU)
                bank = core.proj[:, p % 2, :]
                if p in (0, 2):
                    cols, src = (slice(0, PROMPT), bank[:, 0:PROMPT]) if p == 0 else (slice(PROMPT, N), bank)
                    act.activation(kT[0:DN, 2 * slot, cols], src[0:DN], ACT.Copy)
                    last = act.activation(kT[0:DN, 2 * slot + 1, cols], src[DN:2 * DN], ACT.Copy)
                if p == 0:
                    last = act.activation(qT[0:DN, 2 * slot, 0:PROMPT], bank[0:DN, PROMPT:], ACT.Copy)
                if p == 1:
                    act.activation(qT[0:DN, 2 * slot + 1, 0:PROMPT], bank[0:DN, 0:PROMPT], ACT.Copy)
                    last = act.activation(V[:, slot, 0:PROMPT_TILES, :].rearrange("p t n -> p (t n)"),
                                          bank[:, PROMPT:], ACT.Copy)
                if p in (3, 4):
                    last = act.activation(qT[0:DN, 2 * slot + p - 3, PROMPT:N], bank[0:DN, :], ACT.Copy)
                if p == 5:
                    last = act.activation(V[:, slot, PROMPT_TILES:, :].rearrange("p t n -> p (t n)"),
                                          bank, ACT.Copy)
                last.then_inc(piece_act, 1)

            for p in range(NU):
                piece(0, 0, p)
            core.act_exp(act, 0, 0)

            def step(g, slot, first, last):
                for unit in range(NU):
                    n = g * NU + unit
                    core.act_copy(act, n, unit)
                    if not (last and unit == NU - 1):
                        core.act_exp(act, n + 1, (unit + 1) % NU)
                    if not last:
                        piece(g + 1, 1 - slot, unit)

            loop_groups(act, step)

        @block.vector
        def _(dve):
            for t in range(TILES):
                norm.dve_tile(dve, t)
                if t:
                    norm.dve_copy(dve, t - 1)
            norm.dve_copy(dve, TILES - 1)
            dve.wait_ge(tables_landed, 64)
            for t in range(TILES):
                raw = c_raw[:, t % 2, :]
                dve.wait_ge(c_rstd_ready, t + 1)
                wait(dve, cT_done, t - 1)
                dve.scalar_tensor_tensor(out=c_norm[:, t % 2, 0:Q_LORA], in0=raw[:, 0:Q_LORA],
                                         scalar=c_rstd[:, t, 0:1], in1=c_gain[:, 0:Q_LORA],
                                         op0=ALU.mult, op1=ALU.mult)
                dve.scalar_tensor_tensor(out=c_norm[:, t % 2, Q_LORA:], in0=raw[:, Q_LORA:Q_LORA + KV_LORA],
                                         scalar=c_rstd[:, t, 1:2], in1=c_gain[:, Q_LORA:],
                                         op0=ALU.mult, op1=ALU.mult).then_inc(c_normed, 1)
                r, h = raw[:, Q_LORA + KV_LORA:], DR // 2
                dve.tensor_tensor(kr[:, t % 2, 0, :], r, rope_tok[:, t, 0, :], ALU.mult).then_inc(kr_parts, 1)
                dve.tensor_tensor(kr[:, t % 2, 1, 0:h], r[:, h:], rope_tok[:, t, 1, 0:h],
                                  ALU.mult).then_inc(kr_parts, 1)
                dve.tensor_tensor(kr[:, t % 2, 1, h:], r[:, 0:h], rope_tok[:, t, 1, h:],
                                  ALU.mult).then_inc(kr_parts, 1)
                dve.wait_ge(kr_parts, 3 * t + 3)
                dve.tensor_tensor(kr[:, t % 2, 2, :], kr[:, t % 2, 0, :], kr[:, t % 2, 1, :],
                                  ALU.add).then_inc(kr_ready, 1)
                dve.wait_ge(cT_copied, t + 1)
                for b in range(4):
                    last = dve.tensor_copy(kT[DN:, b, t * P:(t + 1) * P], cT_ps[0:DR, 1, 1, :])
                last.then_inc(krT_copied, 1)

            def piece(g, slot, p):
                if p in (2, 5):
                    return
                r = g * 4 + ROPES[p] - 1
                head = 0 if p in (0, 3) else 1
                bank = core.proj[:, p % 2, :]
                width = PROMPT if p < 2 else SAMPLE
                src = bank[:, PROMPT:] if p == 0 else bank[:, 0:width]
                cols = slice(0, PROMPT) if p < 2 else slice(PROMPT, N)
                dve.wait_ge(piece_done, NU * g + p + 1)
                if p < 2:
                    dve.wait_ge(piece_act, NU * g + p + 1)
                wait(dve, piece_dve, r)
                dve.tensor_tensor(qr[DN:, 0, 0:width], src[DN:DN + DR], rope_T[DN:DN + DR, cols],
                                  ALU.mult).then_inc(qr_parts, 1)
                dve.tensor_tensor(qr[DN:, 1, 0:width], src[DN + DR:], rope_T[DN + DR:, cols],
                                  ALU.mult).then_inc(qr_parts, 1)
                dve.wait_ge(qr_parts, r * 2 + 2)
                if not (isinstance(g, int) and g < 2):
                    dve.wait_ge(core.scores_done, NU * g - NU)
                dve.tensor_tensor(qT[DN:, 2 * slot + head, cols], qr[DN:, 0, 0:width], qr[DN:, 1, 0:width],
                                  ALU.add).then_inc(piece_dve, 1)

            for p in range(NU):
                piece(0, 0, p)
            core.dve_max(dve, 0, 0)
            core.dve_max(dve, 1, 1)

            def step(g, slot, first, last):
                for unit in range(NU):
                    n = g * NU + unit
                    core.dve_copy(dve, n, unit)
                    core.dve_rinv(dve, n, unit)
                    if not last:
                        piece(g + 1, 1 - slot, unit)
                    core.dve_out(dve, g, n, unit, slot, first or (isinstance(g, int) and g < 2))
                    if not (last and unit >= NU - 2):
                        core.dve_max(dve, n + 2, (unit + 2) % NU)

            loop_groups(dve, step)

        @block.tensor
        def _(pe):
            pe.wait_ge(shared.ident_landed, 16)
            for t in range(TILES):
                norm.pe_tile(pe, t, shared.ident[:, :])
            pe.wait_ge(w_in_landed, 16)

            def turn_c(t):
                pe.wait_ge(c_normed, t + 1)
                pe.wait_ge(kr_ready, t + 1)
                wait(pe, cT_copied, t)
                wait(pe, krT_copied, t)
                for k in range(KQ + KKV):
                    pe.transpose(cT_ps[:, k // 4, k % 4, :], c_norm[:, t % 2, k * P:(k + 1) * P], shared.ident[:, :])
                pe.transpose(cT_ps[0:DR, 1, 1, :], kr[:, t % 2, 2, :], shared.ident[:, :]).then_inc(cT_done, 1)

            for t in range(TILES):
                pe.wait_ge(norm.copied_act, t + 1)
                pe.wait_ge(norm.copied_dve, t + 1)
                wait(pe, c_copied, t)
                for lo, hi in ((0, SAMPLE), (SAMPLE, W_IN)):
                    for k in range(KD):
                        last = pe.matmul(c_ps[:, lo // SAMPLE, 0:hi - lo], xnT[:, k, t * P:(t + 1) * P],
                                         w_in[:, k, lo:hi], start=(k == 0), stop=(k == KD - 1))
                last.then_inc(c_done, 1)
                if t:
                    turn_c(t - 1)
            turn_c(TILES - 1)
            pe.wait_ge(cT_copied, TILES)
            pe.wait_ge(krT_copied, TILES)

            def queries(g, h, out, cols):
                pe.wait_ge(q_staged, g * 2 + h + 1)
                for k in range(KQ):
                    last = pe.matmul(out, stage_q[:, h, k, :], cT[:, k, cols], start=(k == 0), stop=(k == KQ - 1))
                return last

            def keys(g, out, cols):
                pe.wait_ge(k_staged, g + 1)
                for k in range(KKV):
                    last = pe.matmul(out, stage_k[:, k, :], cT[:, KQ + k, cols], start=(k == 0), stop=(k == KKV - 1))
                return last

            def values(g, out, t):
                w = w_ukv_heads[:, :, bass.ds(g * 2, 2), DN:]
                for k in range(KKV):
                    last = pe.matmul(out, cT[:, KQ + k, t * P:(t + 1) * P], w[:, k], start=(k == 0),
                                     stop=(k == KKV - 1))
                return last

            def piece(g, p):
                m = g * NU + p
                wait(pe, piece_act, m - 1)
                wait(pe, piece_dve, g * 4 + [-1, 0, 1, 2, 2, 3][p])
                bank = core.proj[:, p % 2, :]
                if p == 0:
                    keys(g, bank[:, 0:PROMPT], slice(0, PROMPT))
                    last = queries(g, 0, bank[:, PROMPT:], slice(0, PROMPT))
                if p == 1:
                    queries(g, 1, bank[:, 0:PROMPT], slice(0, PROMPT))
                    for t in range(PROMPT_TILES):
                        last = values(g, bank[:, PROMPT + t * P:PROMPT + (t + 1) * P], t)
                if p == 2:
                    last = keys(g, bank, slice(PROMPT, N))
                if p in (3, 4):
                    last = queries(g, p - 3, bank, slice(PROMPT, N))
                if p == 5:
                    for t in range(PROMPT_TILES, TILES):
                        last = values(g, bank[:, (t - PROMPT_TILES) * P:(t - PROMPT_TILES + 1) * P], t)
                last.then_inc(piece_done, 1)

            def scores(g, slot, unit):
                tile, head = UNITS[unit]
                needs = (head + 1) if tile < PROMPT_TILES else 4 + head
                pe.wait_ge(piece_act, g * NU + needs)
                pe.wait_ge(piece_dve, g * 4 + ROPES[needs - 1])
                core.pe_scores(pe, g * NU + unit, unit, qT, kT, 2 * slot + head, 2 * slot + head)

            for p in range(NU):
                piece(0, p)
            scores(0, 0, 0)
            scores(0, 0, 1)

            def step(g, slot, first, last):
                for unit in range(NU):
                    n = g * NU + unit
                    _, head = UNITS[unit]
                    core.pe_turn(pe, n, unit, shared.ident[:, :])
                    if not last:
                        piece(g + 1, unit)
                    pe.wait_ge(piece_act, g * NU + (2 if unit < 2 else NU))
                    core.pe_pv(pe, n, unit, lambda t: V[:, slot, t, head * DV:(head + 1) * DV])
                    if unit < NU - 2:
                        scores(g, slot, unit + 2)
                    elif not last:
                        scores(g + 1, 1 - slot, unit + 2 - NU)

            loop_groups(pe, step)
    s.end()


def gqa_block(nc, io, shared):
    with ExitStack() as stack:
        s = Space(nc, stack, "b_")
        arena = shared.raw.rearrange("p s n -> p (s n)")
        W = 4 * HD
        w_qkv = arena[:, 0:2 * KD * W].rearrange("p (b k n) -> p b k n", b=2, k=KD)
        xnT = s.sb("xnT", [P, KD, N])
        tables = s.sb("tables", [P, TILES, 2, 3, HD])
        gains = s.sb("gains", [P, 2, HD])
        half = s.sb("minus_half", [P, 3])
        raw = s.sb("raw", [P, 2, 3, HD])
        squares = s.sb("squares", [P, 2, 3, HD])
        ssq = s.sb("ssq", [P, 2, 3])
        mean = s.sb("mean", [P, 2, 3])
        rstd = s.sb("rstd", [P, 2, 3])
        normed = s.sb("normed", [P, 2, 3, HD])
        straight = s.sb("straight", [P, 2, 3, HD])
        crossed = s.sb("crossed", [P, 3, HD])
        roped = s.sb("roped", [P, 2, 3, HD])
        qkT = s.sb("qkT", [P, 2, 3, N])
        V = s.sb("V", [P, 2, TILES, HD])
        core = Core(s, HD, HD, HD ** -0.5, io.o_b.rearrange("(t p) n -> p t n", p=P))
        norm = InputNorm(s, lambda t: io.acc[t * P:(t + 1) * P, :], row_broadcast(io.g_attn_b[0]), xnT,
                         core.S[:, 0, :, :].rearrange("p b (k n) -> p b k n", n=P),
                         x=core.out[:, :, :, :].rearrange("p b t n -> p b (t n)")[:, :, 0:D],
                         xn=core.probs[:, :, :, :].rearrange("p b j n -> p b (j n)"),
                         junk=core.probsT[:, :, :, :].rearrange("p j k n -> p (j k n)"),
                         gain=V[:, :, :, :].rearrange("p b t n -> p (b t n)")[:, 0:D])
        rope = qkT[:, 1, 0:2, :].rearrange("p h (t a n) -> p (h t) a n", a=2, n=HD)

        w_landed = [s.sem("w_landed0"), s.sem("w_landed1")]
        tables_landed, tables_parts, tables_ready = s.sem("tables_landed"), s.sem("tables_parts"), s.sem("tables_ready")
        half_ready = s.sem("half_ready")
        proj_done, raw_ready, v_ready, sq_ready = s.sem("proj_done"), s.sem("raw_ready"), s.sem("v_ready"), s.sem("sq_ready")
        ssq_ready, mean_ready, rstd_ready = s.sem("ssq_ready"), s.sem("mean_ready"), s.sem("rstd_ready")
        normed_ready, straight_ready, crossed_ready = s.sem("normed_ready"), s.sem("straight_ready"), s.sem("crossed_ready")
        roped_ready, qkT_done, qkT_copied = s.sem("roped_ready"), s.sem("qkT_done"), s.sem("qkT_copied")
        block = stack.enter_context(nc.Block())

        @block.sync
        def _(sp):
            def weights(g, slot):
                if not (isinstance(g, int) and g < 2):
                    sp.wait_ge(proj_done, g * NU - NU)
                src = io.w_qkv_b[0].rearrange("(k p) n -> p k n", p=P)
                dst = w_qkv[:, slot]
                sp.dma_start(dst[:, :, 0:2 * HD], src[:, :, bass.ds(g * 2 * HD, 2 * HD)]).then_inc(w_landed[slot], 16)
                sp.dma_start(dst[:, :, 2 * HD:3 * HD],
                             src[:, :, bass.ds(g * HD + HEADS * HD, HD)]).then_inc(w_landed[slot], 16)
                sp.dma_start(dst[:, :, 3 * HD:],
                             src[:, :, bass.ds(g * HD + (HEADS + KV_HEADS) * HD, HD)]).then_inc(w_landed[slot], 16)

            sp.dma_start(norm.gain, norm.gain_row).then_inc(norm.gain_landed, 16)
            for t in range(2):
                sp.dma_start(norm.x[:, t % 2, :], norm.x_tile_of(t)).then_inc(norm.x_landed[t], 16)
            weights(0, 0)
            sp.dma_start(rope[:, :, :, :], io.rope_b).then_inc(tables_landed, 16)
            sp.dma_start(gains[:, 0, :], row_broadcast(io.g_qn_b[0])).then_inc(tables_landed, 16)
            sp.dma_start(gains[:, 1, :], row_broadcast(io.g_kn_b[0])).then_inc(tables_landed, 16)
            for t in range(2, TILES):
                sp.wait_ge(norm.xn_ready, t - 1)
                sp.dma_start(norm.x[:, t % 2, :], norm.x_tile_of(t)).then_inc(norm.x_landed[t % 2], 16)
            weights(1, 1)
            sp.dma_start(shared.w_o_b, io.w_o_b[0].rearrange("(k p) n -> p k n", p=P)).then_inc(shared.w_o_landed, 16)

            def step(g, slot):
                weights(g + 2, slot)
                core.store(sp, g, slot)

            step(0, 0)
            step(1, 1)
            with sp.Fori(1, GROUPS // 2 - 1) as i:
                step(i * 2, 0)
                step(i * 2 + 1, 1)
            core.store(sp, GROUPS - 2, 0)
            core.store(sp, GROUPS - 1, 1)
            for slot in range(2):
                sp.wait_ge(core.stored[slot], 16 * GROUPS // 2)

        @block.gpsimd
        def _(pool):
            pool.memset(half[:, :], -0.5).then_inc(half_ready, 1)
            pool.wait_ge(half_ready, 1)
            for t in range(TILES):
                norm.pool_tile(pool, t, half[:, 0:1])
            pool.wait_ge(tables_ready, 5 * 3)

            def tile(m, t):
                pool.wait_ge(mean_ready, m + 1)
                wait(pool, normed_ready, m)
                pool.tensor_tensor(rstd[:, t % 2, :], mean[:, t % 2, :], half[:, :], ALU.pow).then_inc(rstd_ready, 1)
                pool.wait_ge(rstd_ready, m + 1)
                wait(pool, crossed_ready, 2 * m - 2)
                pool.tensor_tensor(normed[:, t % 2, :, :], raw[:, t % 2, :, :],
                                   rstd[:, t % 2, :].unsqueeze(2).to_broadcast([P, 3, HD]),
                                   ALU.mult).then_inc(normed_ready, 1)
                pool.wait_ge(normed_ready, m + 1)
                wait(pool, roped_ready, m - 1)
                pool.tensor_tensor(straight[:, t % 2, :, :], normed[:, t % 2, :, :], tables[:, t, 0, :, :],
                                   ALU.mult).then_inc(straight_ready, 1)

            for t in range(TILES):
                tile(t, t)
            with pool.Fori(1, GROUPS) as g:
                for t in range(TILES):
                    tile(g * NU + t, t)

        @block.scalar
        def _(act):
            for t in range(TILES):
                norm.act_tile(act, t)
                if t:
                    norm.act_copy(act, t - 1)
            norm.act_copy(act, TILES - 1)

            def projected(g, slot, t):
                m = g * NU + t
                bank = core.proj[:, t % 2, :].rearrange("p (h n) -> p h n", h=4)
                act.wait_ge(proj_done, m + 1)
                wait(act, normed_ready, m - 1)
                act.activation(raw[:, t % 2, :, :], bank[:, 0:3, :], ACT.Copy).then_inc(raw_ready, 1)
                wait(act, ssq_ready, m - 1)
                act.activation(squares[:, t % 2, :, :], bank[:, 0:3, :], ACT.Square).then_inc(sq_ready, 1)
                if not (isinstance(g, int) and g < 2):
                    act.wait_ge(core.pv_done, 2 * NU * g - 2 * NU)
                act.activation(V[:, slot, t, :], bank[:, 3, :], ACT.Copy).then_inc(v_ready, 1)

            def turned(g, slot, t):
                m = g * NU + t
                bank = core.proj[:, t % 2, :].rearrange("p (h n) -> p h n", h=4)
                act.wait_ge(qkT_done, m + 1)
                if not (isinstance(g, int) and g < 2):
                    act.wait_ge(core.scores_done, NU * g - NU)
                act.activation(qkT[:, slot, :, t * P:(t + 1) * P], bank[:, 0:3, :],
                               ACT.Copy).then_inc(qkT_copied, 1)

            for t in range(TILES):
                projected(0, 0, t)
                if t:
                    turned(0, 0, t - 1)
            core.act_exp(act, 0, 0)

            def step(g, slot, first, last):
                for unit in range(NU):
                    n = g * NU + unit
                    core.act_copy(act, n, unit)
                    if unit == 0:
                        core.act_exp(act, n + 1, 1)
                        if not last:
                            projected(g + 1, 1 - slot, 0)
                        turned(g, slot, TILES - 1)
                        continue
                    if not (last and unit == NU - 1):
                        core.act_exp(act, n + 1, (unit + 1) % NU)
                    if not last:
                        projected(g + 1, 1 - slot, unit)
                        turned(g + 1, 1 - slot, unit - 1)

            loop_groups(act, step)

        @block.vector
        def _(dve):
            for t in range(TILES):
                norm.dve_tile(dve, t)
                if t:
                    norm.dve_copy(dve, t - 1)
            norm.dve_copy(dve, TILES - 1)
            dve.wait_ge(tables_landed, 48)
            for h in range(3):
                gain = gains[:, h // 2, :]
                dve.tensor_tensor(tables[:, :, 0, h, :], rope[:, :, 0, :],
                                  gain.unsqueeze(1).to_broadcast([P, TILES, HD]), ALU.mult).then_inc(tables_ready, 1)
                for axis in range(2):
                    for side in range(2):
                        at, other = axis * 64 + side * 32, axis * 64 + (1 - side) * 32
                        dve.tensor_tensor(tables[:, :, 1, h, at:at + 32], rope[:, :, 1, at:at + 32],
                                          gain[:, other:other + 32].unsqueeze(1).to_broadcast([P, TILES, 32]),
                                          ALU.mult).then_inc(tables_ready, 1)
            dve.wait_ge(tables_ready, 15)

            def squared(m, t):
                dve.wait_ge(sq_ready, m + 1)
                wait(dve, mean_ready, m - 1)
                dve.tensor_reduce(ssq[:, t % 2, :], squares[:, t % 2, :, :], AX.X, ALU.add).then_inc(ssq_ready, 1)
                dve.wait_ge(ssq_ready, m + 1)
                wait(dve, rstd_ready, m - 1)
                dve.tensor_scalar(mean[:, t % 2, :], ssq[:, t % 2, :], 1.0 / HD, EPS,
                                  ALU.mult, ALU.add).then_inc(mean_ready, 1)

            def rotate(m, t):
                dve.wait_ge(normed_ready, m + 1)
                wait(dve, roped_ready, m)
                a = normed[:, t % 2, :, :].rearrange("p h (x s n) -> p (h x) s n", x=2, s=2)
                c = crossed[:, :, :].rearrange("p h (x s n) -> p (h x) s n", x=2, s=2)
                sin = tables[:, t, 1, :, :].rearrange("p h (x s n) -> p (h x) s n", x=2, s=2)
                for side in range(2):
                    dve.tensor_tensor(c[:, :, side, :], a[:, :, 1 - side, :], sin[:, :, side, :],
                                      ALU.mult).then_inc(crossed_ready, 1)
                dve.wait_ge(crossed_ready, 2 * m + 2)
                dve.wait_ge(straight_ready, m + 1)
                wait(dve, qkT_done, m - 1)
                dve.tensor_tensor(roped[:, t % 2, :, :], straight[:, t % 2, :, :], crossed[:, :, :],
                                  ALU.add).then_inc(roped_ready, 1)

            for t in range(TILES):
                squared(t, t)
                if t:
                    rotate(t - 1, t - 1)
            core.dve_max(dve, 0, 0)
            core.dve_max(dve, 1, 1)

            def step(g, slot, first, last):
                for unit in range(NU):
                    n = g * NU + unit
                    core.dve_copy(dve, n, unit)
                    core.dve_rinv(dve, n, unit)
                    if unit == 0:
                        rotate(g * NU + TILES - 1, TILES - 1)
                    elif not last:
                        rotate(g * NU + NU + unit - 1, unit - 1)
                    if not last:
                        squared(g * NU + NU + unit, unit)
                    core.dve_out(dve, g, n, unit, slot, first or (isinstance(g, int) and g < 2))
                    if not (last and unit >= NU - 2):
                        core.dve_max(dve, n + 2, (unit + 2) % NU)

            loop_groups(dve, step)

        @block.tensor
        def _(pe):
            for t in range(TILES):
                norm.pe_tile(pe, t, shared.ident[:, :])
            pe.wait_ge(norm.copied_act, TILES)
            pe.wait_ge(norm.copied_dve, TILES)

            def project(g, slot, t):
                m = g * NU + t
                if t == 0:
                    pe.wait_ge(w_landed[slot], 24 * (g - slot) + 48)
                wait(pe, qkT_copied, m - 1)
                for k in range(KD):
                    last = pe.matmul(core.proj[:, t % 2, :], xnT[:, k, t * P:(t + 1) * P], w_qkv[:, slot, k, :],
                                     start=(k == 0), stop=(k == KD - 1))
                last.then_inc(proj_done, 1)

            def turn(g, t):
                m = g * NU + t
                pe.wait_ge(roped_ready, m + 1)
                pe.wait_ge(v_ready, m + 1)
                for h in range(3):
                    last = pe.transpose(core.proj[:, t % 2, h * HD:(h + 1) * HD], roped[:, t % 2, h, :],
                                        shared.ident[:, :])
                last.then_inc(qkT_done, 1)

            def scores(g, slot, unit):
                tile, head = UNITS[unit]
                pe.wait_ge(qkT_copied, g * NU + (2 if tile < PROMPT_TILES else TILES))
                both = qkT[:, slot, :, :]
                core.pe_scores(pe, g * NU + unit, unit, both, both, head, 2)

            for t in range(TILES):
                project(0, 0, t)
                if t:
                    turn(0, t - 1)
            scores(0, 0, 0)
            scores(0, 0, 1)

            def step(g, slot, first, last):
                for unit in range(NU):
                    n = g * NU + unit
                    core.pe_turn(pe, n, unit, shared.ident[:, :])
                    if not last:
                        project(g + 1, 1 - slot, unit)
                    core.pe_pv(pe, n, unit, lambda t: V[:, slot, t, :])
                    if unit == 0:
                        turn(g, TILES - 1)
                    elif not last:
                        turn(g + 1, unit - 1)
                    if unit < NU - 2:
                        scores(g, slot, unit + 2)
                    elif not last:
                        scores(g + 1, 1 - slot, unit + 2 - NU)

            loop_groups(pe, step)
    s.end()


def output_block(nc, io, shared, layer):
    with ExitStack() as stack:
        s = Space(nc, stack, f"o{layer}_")
        o_dram, w_o = (io.o_a, shared.w_o_a) if layer == 0 else (io.o_b, shared.w_o_b)
        KO = o_dram.shape[1] // P
        HALVES = KO // KD
        o_in = s.sb("o_in", [P, 2, KO * P])
        oT = s.sb("oT", [P, 2, KO, P])
        x = s.sb("x", [P, 2, D])
        xn = s.sb("xn", [P, 2, D])
        xnT = s.sb("xnT", [P, KD, P])
        junk = s.sb("squares", [P, D])
        gain = s.sb("gain", [P, D])
        w_r = s.sb("w_router", [P, KD, EXPERTS])
        ssq, mean, rstd = s.sb("ssq", [P, TILES]), s.sb("mean", [P, TILES]), s.sb("rstd", [P, TILES])
        half = s.sb("minus_half", [P, 1])
        logits = s.sb("logits", [P, TILES, EXPERTS])
        top = s.sb("top", [P, TILES])
        shifted = s.sb("shifted", [P, TILES, EXPERTS])
        expd = s.sb("expd", [P, TILES, EXPERTS])
        total, inv = s.sb("total", [P, TILES]), s.sb("inv", [P, TILES])
        ROWS = 32 + EXPERTS
        aff = s.sb("aff", [P, TILES - PROMPT_TILES, ROWS])
        work = s.sb("work", [ROWS, SAMPLE])
        best = s.sb("best", [ROWS, CAP_S])
        best_at = s.sb("best_at", [ROWS, CAP_S], U32)
        chosen = s.sb("chosen", [EXPERTS, 2, CAP])
        oT_ps = s.psum("oT", [P, 2, 4, P])
        y_ps = s.psum("y", [P, 2, SAMPLE])
        xT_ps = s.psum("xT", [P, 2, 4, P])
        r_ps = s.psum("router", [P, TILES, EXPERTS])
        aT_ps = s.psum("affT", [ROWS, SAMPLE])

        o_landed = [s.sem("o_landed0"), s.sem("o_landed1")]
        x_landed = [s.sem("x_landed0"), s.sem("x_landed1")]
        small_landed = s.sem("small_landed")
        oT_done, oT_copied, y_done = s.sem("oT_done"), s.sem("oT_copied"), s.sem("y_done")
        x_ready, x_stored = s.sem("x_ready"), [s.sem("x_stored0"), s.sem("x_stored1")]
        ssq_ready, half_ready, mean_ready, rstd_ready = s.sem("ssq"), s.sem("half"), s.sem("mean"), s.sem("rstd")
        xn_ready, xn_stored = s.sem("xn_ready"), [s.sem("xn_stored0"), s.sem("xn_stored1")]
        xT_done, xT_copied, router_done, logits_ready = s.sem("xT_done"), s.sem("xT_copied"), s.sem("router_done"), s.sem("logits")
        chain, exp_ready, pad_ready, aff_ready = s.sem("softmax_steps"), s.sem("exp"), s.sem("pad"), s.sem("aff")
        affT_done, choice, chosen_ready, chosenT_done = s.sem("affT_done"), s.sem("choice"), s.sem("chosen"), s.sem("chosenT_done")
        block = stack.enter_context(nc.Block())

        def rows(dram, t):
            return dram.rearrange("(t p) n -> t p n", p=P)[bass.ds(t, 1)].rearrange("o p n -> (o p) n")

        @block.sync
        def _(sp):
            def load_o(t, slot):
                if t >= 2:
                    sp.wait_ge(oT_done, HALVES * (t - 1))
                sp.dma_start(o_in[:, slot, :], rows(o_dram, t)).then_inc(o_landed[slot], 16)

            def load_x(t, slot):
                if t >= 2:
                    sp.wait_ge(xn_ready, t - 1)
                    sp.wait_ge(ssq_ready, t - 1)
                    sp.wait_ge(x_stored[slot], 8 * (t - slot))
                src = token_rows(io.x_prompt, io.x_sample, t) if layer == 0 else rows(io.acc, t)
                sp.dma_start(x[:, slot, :], src).then_inc(x_landed[slot], 16)

            def store(t, slot):
                sp.wait_ge(x_ready, t + 1)
                sp.dma_start(rows(io.acc, t), x[:, slot, :]).then_inc(x_stored[slot], 16)
                sp.wait_ge(xn_ready, t + 1)
                sp.dma_start(rows(io.xn, t), xn[:, slot, :]).then_inc(xn_stored[slot], 16)

            load_o(0, 0)
            load_x(0, 0)
            load_o(1, 1)
            load_x(1, 1)
            sp.dma_start(gain[:, :], row_broadcast(io.g_ffn[layer])).then_inc(small_landed, 16)
            sp.dma_start(w_r[:, :, :], io.w_router[layer].rearrange("(k p) e -> p k e", p=P)).then_inc(small_landed, 16)
            for t in range(TILES):
                if t + 2 < TILES:
                    load_o(t + 2, t % 2)
                store(t, t % 2)
                if t + 2 < TILES:
                    load_x(t + 2, t % 2)
                    shared.load_first(sp, io.w_up, layer, 0, t)
                    if layer == 0:
                        shared.load_first(sp, io.w_gate, layer, 4, t)
            for j in range(4):
                if layer == 1:
                    shared.load_first(sp, io.w_gate, layer, 4, j)
            for j in range(4):
                shared.load_first(sp, io.w_down, layer, 8, j)
            for slot in range(2):
                sp.wait_ge(x_stored[slot], 16 * TILES // 2)
                sp.wait_ge(xn_stored[slot], 16 * TILES // 2)

        @block.gpsimd
        def _(pool):
            pool.memset(half[:, :], -0.5).then_inc(half_ready, 1)
            pool.memset(aff[:, :, :], -2.0).then_inc(pad_ready, 1)
            pool.wait_ge(half_ready, 1)
            for t in range(TILES):
                pool.wait_ge(ssq_ready, t + 1)
                pool.tensor_scalar(mean[:, t:t + 1], ssq[:, t:t + 1], 1.0 / D, EPS,
                                   ALU.mult, ALU.add).then_inc(mean_ready, 1)
                pool.wait_ge(mean_ready, t + 1)
                pool.tensor_tensor(rstd[:, t:t + 1], mean[:, t:t + 1], half[:, :], ALU.pow).then_inc(rstd_ready, 1)

        @block.scalar
        def _(act):
            def copy_oT(t, slot):
                for h in range(HALVES):
                    act.wait_ge(oT_done, HALVES * t + h + 1)
                    if not (isinstance(t, int) and t < 2):
                        act.wait_ge(y_done, t - 1)
                    act.activation(oT[:, slot, h * KD:(h + 1) * KD, :],
                                   oT_ps[:, :, :, :].rearrange("p b k n -> p (b k) n"), ACT.Copy).then_inc(oT_copied, 1)

            def square(t):
                act.wait_ge(x_ready, t + 1)
                wait(act, ssq_ready, t)
                act.activation(junk[:, :], x[:, t % 2, :], ACT.Square,
                               accum_out=ssq[:, t:t + 1]).then_inc(ssq_ready, 1)

            copy_oT(0, 0)
            for t in range(TILES):
                if t + 1 < TILES:
                    copy_oT(t + 1, (t + 1) % 2)
                square(t)
            act.wait_ge(chain, 2)
            act.activation(expd[:, :, :], shifted[:, :, :], ACT.Exp).then_inc(exp_ready, 1)

        @block.vector
        def _(dve):
            def copy_xT(t):
                dve.wait_ge(xT_done, t + 1)
                wait(dve, router_done, t)
                dve.tensor_copy(xnT[:, :, :], xT_ps[:, :, :, :].rearrange("p b k n -> p (b k) n")).then_inc(xT_copied, 1)

            for t in range(TILES):
                slot = t % 2
                dve.wait_ge(y_done, t + 1)
                dve.wait_ge(x_landed[slot], 16 * (t // 2 + 1))
                dve.tensor_tensor(x[:, slot, :], x[:, slot, :], y_ps[:, :, :].rearrange("p b n -> p (b n)"),
                                  ALU.add).then_inc(x_ready, 1)
                dve.wait_ge(x_ready, t + 1)
                dve.wait_ge(rstd_ready, t + 1)
                if t == 0:
                    dve.wait_ge(small_landed, 32)
                if t >= 2:
                    dve.wait_ge(xT_done, t - 1)
                    dve.wait_ge(xn_stored[slot], 16 * (t // 2))
                dve.scalar_tensor_tensor(out=xn[:, slot, :], in0=x[:, slot, :], scalar=rstd[:, t:t + 1],
                                         in1=gain[:, :], op0=ALU.mult, op1=ALU.mult).then_inc(xn_ready, 1)
                if t:
                    copy_xT(t - 1)
            copy_xT(TILES - 1)
            dve.wait_ge(router_done, TILES)
            dve.tensor_copy(logits[:, :, :], r_ps[:, :, :]).then_inc(logits_ready, 1)
            dve.wait_ge(logits_ready, 1)
            dve.tensor_reduce(top[:, :], logits[:, :, :], AX.X, ALU.max).then_inc(chain, 1)
            dve.wait_ge(chain, 1)
            dve.tensor_tensor(shifted[:, :, :], logits[:, :, :],
                              top[:, :].unsqueeze(2).to_broadcast([P, TILES, EXPERTS]), ALU.subtract).then_inc(chain, 1)
            dve.wait_ge(exp_ready, 1)
            dve.tensor_reduce(total[:, :], expd[:, :, :], AX.X, ALU.add).then_inc(chain, 1)
            dve.wait_ge(chain, 3)
            dve.reciprocal(inv[:, :], total[:, :]).then_inc(chain, 1)
            dve.wait_ge(chain, 4)
            dve.wait_ge(pad_ready, 1)
            dve.tensor_tensor(aff[:, 0:PROMPT_TILES, 0:EXPERTS], expd[:, 0:PROMPT_TILES, :],
                              inv[:, 0:PROMPT_TILES].unsqueeze(2).to_broadcast([P, PROMPT_TILES, EXPERTS]),
                              ALU.mult).then_inc(aff_ready, 1)
            dve.tensor_tensor(aff[:, :, 32:ROWS], expd[:, PROMPT_TILES:, :],
                              inv[:, PROMPT_TILES:].unsqueeze(2).to_broadcast([P, TILES - PROMPT_TILES, EXPERTS]),
                              ALU.mult).then_inc(aff_ready, 1)
            dve.wait_ge(affT_done, 1)
            dve.tensor_copy(work[:, :], aT_ps[:, :]).then_inc(choice, 1)
            for r in range(CAP_S // 8):
                rows_ = slice(0, ROWS) if r < CAP_P // 8 else slice(32, ROWS)
                at = slice(8 * r, 8 * r + 8)
                dve.wait_ge(choice, 3 * r + 1)
                dve.max(best[rows_, at], work[rows_, :]).then_inc(choice, 1)
                dve.wait_ge(choice, 3 * r + 2)
                dve.max_index(best_at[rows_, at], best[rows_, at], work[rows_, :]).then_inc(choice, 1)
                dve.wait_ge(choice, 3 * r + 3)
                dve.match_replace(work[rows_, :], best[rows_, at], work[rows_, :], -1.0).then_inc(choice, 1)
            dve.wait_ge(choice, 3 * (CAP_S // 8) + 1)
            dve.tensor_scalar(chosen[:, 0, 0:CAP_S], best_at[32:ROWS, :], float(PROMPT), None,
                              ALU.add).then_inc(chosen_ready, 1)
            dve.tensor_copy(chosen[:, 0, CAP_S:], best_at[0:EXPERTS, 0:CAP_P]).then_inc(chosen_ready, 1)
            dve.tensor_copy(chosen[:, 1, 0:CAP_S], best[32:ROWS, :]).then_inc(chosen_ready, 1)
            dve.tensor_copy(chosen[:, 1, CAP_S:], best[0:EXPERTS, 0:CAP_P]).then_inc(chosen_ready, 1)
            dve.wait_ge(chosenT_done, 1)
            dve.tensor_copy(shared.row_of[:, :], r_ps[0:CAP, 0, :]).then_inc(shared.lists_ready, 1)
            dve.tensor_copy(shared.gate_of[:, :], r_ps[0:CAP, 1, :]).then_inc(shared.lists_ready, 1)

        @block.tensor
        def _(pe):
            ident = shared.ident[:, :]
            pe.wait_ge(shared.w_o_landed, 16 * (layer + 1))

            def turn_o(t, slot):
                pe.wait_ge(o_landed[slot], 8 * (t - slot) + 16)
                for h in range(HALVES):
                    if not (isinstance(t, int) and t == 0 and h == 0):
                        pe.wait_ge(oT_copied, HALVES * t + h)
                    for k in range(KD):
                        last = pe.transpose(oT_ps[:, k // 4, k % 4, :],
                                            o_in[:, slot, (h * KD + k) * P:(h * KD + k + 1) * P], ident)
                    last.then_inc(oT_done, 1)

            def project(t, slot):
                pe.wait_ge(oT_copied, HALVES * (t + 1))
                if not (isinstance(t, int) and t == 0):
                    pe.wait_ge(x_ready, t)
                for half_ in range(2):
                    for k in range(KO):
                        last = pe.matmul(y_ps[:, half_, :], oT[:, slot, k, :],
                                         w_o[:, k, half_ * SAMPLE:(half_ + 1) * SAMPLE],
                                         start=(k == 0), stop=(k == KO - 1))
                last.then_inc(y_done, 1)

            def turn_x(t):
                pe.wait_ge(xn_ready, t + 1)
                wait(pe, xT_copied, t)
                for k in range(KD):
                    last = pe.transpose(xT_ps[:, k // 4, k % 4, :], xn[:, t % 2, k * P:(k + 1) * P], ident)
                last.then_inc(xT_done, 1)

            def route(t):
                if t == 0:
                    pe.wait_ge(small_landed, 32)
                pe.wait_ge(xT_copied, t + 1)
                for k in range(KD):
                    last = pe.matmul(r_ps[:, t, :], xnT[:, k, :], w_r[:, k, :], start=(k == 0), stop=(k == KD - 1))
                last.then_inc(router_done, 1)

            turn_o(0, 0)
            for t in range(TILES):
                if t + 1 < TILES:
                    turn_o(t + 1, (t + 1) % 2)
                project(t, t % 2)
                if t >= 2:
                    route(t - 2)
                if t >= 1:
                    turn_x(t - 1)
            route(TILES - 2)
            turn_x(TILES - 1)
            route(TILES - 1)
            pe.wait_ge(aff_ready, 2)
            for t in range(TILES - PROMPT_TILES):
                last = pe.transpose(aT_ps[:, t * P:(t + 1) * P], aff[:, t, :], ident)
            last.then_inc(affT_done, 1)
            pe.wait_ge(chosen_ready, 4)
            pe.wait_ge(logits_ready, 1)
            for what in range(2):
                last = pe.transpose(r_ps[0:CAP, what, :], chosen[:, what, :], shared.ident[0:EXPERTS, 0:EXPERTS])
            last.then_inc(chosenT_done, 1)
    s.end()


def moe_block(nc, io, shared, layer):
    with ExitStack() as stack:
        s = Space(nc, stack, f"m{layer}_")
        raw = shared.raw
        hi = s.sb("w_hi", [P, SPLITS, 2, D], F32R)
        lo = s.sb("w_lo", [P, SPLITS, 2, D], F32R)
        xe = s.sb("xe", [CAP, D])
        xeT_hi = s.sb("xeT_hi", [P, 2, KD, CAP], F32R)
        xeT_lo = s.sb("xeT_lo", [P, 2, KD, CAP], F32R)
        silu = s.sb("silu", [CAP, FF])
        hid = s.sb("hid", [CAP, FF])
        hidT_hi = s.sb("hidT_hi", [P, KD, CAP], F32R)
        hidT_lo = s.sb("hidT_lo", [P, KD, CAP], F32R)
        ye = s.sb("ye", [CAP, D])
        row_gather = s.sb("row_gather", [CAP, 1], U32)
        row_scatter = s.sb("row_scatter", [CAP, 1], U32)
        gate_ps = s.psum("gate", [CAP, FF])
        up_ps = s.psum("up", [CAP, FF])
        down_ps = s.psum("down", [CAP, D])
        T_ps = s.psum("turned", [P, KD, P])

        hi_ready, lo_ready, split_used = s.sem("hi_ready"), s.sem("lo_ready"), s.sem("split_used")
        first_rows_ready, rows_ready, gathered = s.sem("first_rows_ready"), s.sem("rows_ready"), s.sem("gathered")
        scatter_rows_ready, scattered = s.sem("scatter_rows_ready"), s.sem("scattered")
        T_done, T_hi, T_lo = s.sem("T_done"), s.sem("T_hi"), s.sem("T_lo")
        silu_ready, hid_ready, ye_ready = s.sem("silu_ready"), s.sem("hid_ready"), s.sem("ye_ready")
        block = stack.enter_context(nc.Block())

        LAST = EXPERTS - 1

        def loop_experts(engine, step):
            step(0, 0)
            with engine.Fori(0, (EXPERTS - 2) // 2) as i:
                step(i * 2 + 1, 1)
                step(i * 2 + 2, 0)
            step(LAST, 1)

        def is_last(e):
            return isinstance(e, int) and e == LAST

        def pieces(e):
            slots = [0, 1, 2, 3, 8, 9, 10, 11] if is_last(e) else list(range(SLOTS))
            return list(enumerate(slots))

        def q_of(e, place):
            return e * SLOTS + 4 + place

        def wait_low(engine, e, place):
            engine.wait_ge(lo_ready, q_of(e, place) + 1)

        @block.sync
        def _(sp):
            def load(e, matrix, j, first_slot):
                src = matrix[layer].rearrange("e (c k p) n -> e c p k n", c=4, p=P)[bass.ds(e, 1), j]
                sp.dma_start(raw[:, first_slot + j, :].rearrange("p (k n) -> p k n", k=2),
                             src.rearrange("e p k n -> (e p) k n")).then_inc(shared.landed[first_slot + j], 16)

            for j in range(4):
                sp.wait_ge(lo_ready, j + 1)
                load(1, io.w_gate, j, 4)

            def step(e):
                for j in range(4):
                    wait_low(sp, e - 1, j)
                    load(e, io.w_up, j, 0)
                if not is_last(e):
                    for j in range(4):
                        wait_low(sp, e - 1, 4 + j)
                        load(e + 1, io.w_gate, j, 4)
                for j in range(4):
                    wait_low(sp, e - 1, 8 + j)
                    load(e, io.w_down, j, 8)

            with sp.Fori(1, LAST) as e:
                step(e)
            step(LAST)

        @block.gpsimd
        def _(pool):
            def gather(e, rows_ready, count):
                wait(pool, gathered, e * 16)
                wait(pool, T_done, e if isinstance(e, int) and e < 2 else e * 2 - 2)
                pool.tensor_copy(row_gather[:, :], shared.row_of[:, bass.ds(e, 1)]).then_inc(rows_ready, 1)
                pool.wait_ge(shared.lists_ready, 2 * layer + 2)
                pool.wait_ge(rows_ready, count)
                pool.indirect_dma_start(out=xe[:, :], out_offset=None, in_=io.xn,
                                        in_offset=bass.IndirectOffsetOnAxis(ap=row_gather[:, :], axis=0)
                                        ).then_inc(gathered, 16)

            def scatter(e):
                wait(pool, scattered, e * 16)
                pool.tensor_copy(row_scatter[:, :], shared.row_of[:, bass.ds(e, 1)]).then_inc(scatter_rows_ready, 1)
                pool.wait_ge(shared.lists_ready, 2 * layer + 2)
                pool.wait_ge(scatter_rows_ready, e + 1)
                pool.wait_ge(ye_ready, e + 1)
                pool.indirect_dma_start(out=io.acc, out_offset=bass.IndirectOffsetOnAxis(ap=row_scatter[:, :], axis=0),
                                        in_=ye[:, :], in_offset=None, compute_op=ALU.add).then_inc(scattered, 16)

            def step(e, ahead):
                if not (isinstance(e, int) and e == 0):
                    scatter(e - 1)
                if ahead:
                    if isinstance(e, int):
                        gather(e + 2, first_rows_ready, e + 3)
                    else:
                        gather(e + 2, rows_ready, e)

            gather(0, first_rows_ready, 1)
            gather(1, first_rows_ready, 2)
            step(0, True)
            with pool.Fori(1, LAST - 1) as e:
                step(e, True)
            step(LAST - 1, False)
            step(LAST, False)
            scatter(LAST)
            pool.wait_ge(scattered, 16 * EXPERTS)

        @block.scalar
        def _(act):
            def high(q, split, slot, landed):
                act.wait_ge(shared.landed[slot], landed)
                wait(act, split_used, q + 1 - SPLITS)
                act.activation(hi[:, split, :, :].rearrange("p k n -> p (k n)"), raw[:, slot, :],
                               ACT.Copy).then_inc(hi_ready, 1)

            def turned(dst, n):
                act.wait_ge(T_done, n)
                act.activation(dst, T_ps[:, :, 0:CAP], ACT.Copy).then_inc(T_hi, 1)

            def gate_out(e, done):
                act.wait_ge(split_used, done)
                wait(act, hid_ready, e)
                act.activation(silu[:, :], gate_ps[:, :], ACT.Silu).then_inc(silu_ready, 1)

            def down_out(e, done):
                act.wait_ge(split_used, done)
                wait(act, scattered, e * 16)
                act.activation(ye[:, :], down_ps[:, :], ACT.Copy,
                               scale=shared.gate_of[:, bass.ds(e, 1)]).then_inc(ye_ready, 1)

            base = 16 * layer * EXPERTS
            turned(xeT_hi[:, 0, :, :], 1)
            for j in range(4):
                high(j, j % SPLITS, 4 + j, base + 16)

            def step(e, parity):
                for place, slot in pieces(e):
                    ahead = 1 if 4 <= slot < 8 else 0
                    high(q_of(e, place), (4 + place) % SPLITS, slot, (e + ahead) * 16 + base + 16)
                    if place == 2:
                        if isinstance(e, int) and e == 0:
                            gate_out(0, 4)
                    if place == 3 and not is_last(e):
                        turned(xeT_hi[:, 1 - parity, :, :], e * 2 + 2)
                    if place == 3 and not (isinstance(e, int) and e == 0):
                        down_out(e - 1, q_of(e, 0))
                    if place == (5 if is_last(e) else 8):
                        turned(hidT_hi[:, :, :], e * 2 + (2 if is_last(e) else 3))
                    if place == 10:
                        gate_out(e + 1, q_of(e, 8))
                if is_last(e):
                    down_out(e, q_of(e, 8))

            loop_experts(act, step)

        @block.vector
        def _(dve):
            def low(q, split, slot):
                dve.wait_ge(hi_ready, q + 1)
                wait(dve, split_used, q + 1 - SPLITS)
                dve.tensor_tensor(lo[:, split, :, :].rearrange("p k n -> p (k n)"), raw[:, slot, :],
                                  hi[:, split, :, :].rearrange("p k n -> p (k n)"),
                                  ALU.subtract).then_inc(lo_ready, 1)

            def turned(dst, high_part, n):
                dve.wait_ge(T_hi, n)
                dve.tensor_tensor(dst, T_ps[:, :, 0:CAP], high_part, ALU.subtract).then_inc(T_lo, 1)

            turned(xeT_lo[:, 0, :, :], xeT_hi[:, 0, :, :], 1)
            for j in range(4):
                low(j, j % SPLITS, 4 + j)

            def step(e, parity):
                for place, slot in pieces(e):
                    low(q_of(e, place), (4 + place) % SPLITS, slot)
                    if place == 3 and not is_last(e):
                        turned(xeT_lo[:, 1 - parity, :, :], xeT_hi[:, 1 - parity, :, :], e * 2 + 2)
                    if place == 5:
                        dve.wait_ge(silu_ready, e + 1)
                        dve.wait_ge(split_used, q_of(e, 4))
                        wait(dve, T_done, 2 * e + 1)
                        dve.tensor_tensor(hid[:, :], silu[:, :], up_ps[:, :], ALU.mult).then_inc(hid_ready, 1)
                    if place == (5 if is_last(e) else 8):
                        turned(hidT_lo[:, :, :], hidT_hi[:, :, :], e * 2 + (2 if is_last(e) else 3))

            loop_experts(dve, step)

        @block.tensor
        def _(pe):
            def turn(src, n):
                wait(pe, T_lo, n)
                for k in range(KD):
                    last = pe.transpose(T_ps[:, k, 0:CAP], src[:, k * P:(k + 1) * P], shared.ident[0:CAP, 0:CAP])
                last.then_inc(T_done, 1)

            def products(out, left_hi, left_lo, j, split, q):
                for half in range(2):
                    cols = slice(half * SAMPLE, (half + 1) * SAMPLE)
                    for kk in range(2):
                        k = 2 * j + kk
                        pe.matmul(out[:, cols], left_hi[:, k, :], hi[:, split, kk, cols], start=(k == 0), stop=False)
                        pe.matmul(out[:, cols], left_hi[:, k, :], lo[:, split, kk, cols], start=False, stop=False)
                        last = pe.matmul(out[:, cols], left_lo[:, k, :], hi[:, split, kk, cols], start=False,
                                         stop=(k == KD - 1))
                last.then_inc(split_used, 1)

            pe.wait_ge(gathered, 16)
            turn(xe, 0)
            pe.wait_ge(T_lo, 1)
            for j in range(4):
                pe.wait_ge(lo_ready, j + 1)
                products(gate_ps, xeT_hi[:, 0], xeT_lo[:, 0], j, j % SPLITS, j)

            def step(e, parity):
                for place, slot in pieces(e):
                    split = (4 + place) % SPLITS
                    if slot == 0:
                        wait(pe, hid_ready, e)
                    if slot == 4:
                        pe.wait_ge(silu_ready, e + 1)
                        pe.wait_ge(T_lo, e * 2 + 2)
                    if slot == 8:
                        if not (isinstance(e, int) and e == 0):
                            pe.wait_ge(ye_ready, e)
                        if is_last(e):
                            pe.wait_ge(hid_ready, e + 1)
                            turn(hid, e * 2 + 1)
                        pe.wait_ge(T_lo, e * 2 + (2 if is_last(e) else 3))
                    if slot == 1 and not is_last(e):
                        pe.wait_ge(gathered, e * 16 + 32)
                        turn(xe, e * 2 + 1)
                    if slot == 6:
                        pe.wait_ge(hid_ready, e + 1)
                        turn(hid, e * 2 + 2)
                    wait_low(pe, e, place)
                    q = q_of(e, place)
                    if slot < 4:
                        products(up_ps, xeT_hi[:, parity], xeT_lo[:, parity], slot, split, q)
                    elif slot < 8:
                        products(gate_ps, xeT_hi[:, 1 - parity], xeT_lo[:, 1 - parity], slot - 4, split, q)
                    else:
                        products(down_ps, hidT_hi, hidT_lo, slot - 8, split, q)

            loop_experts(pe, step)
    s.end()


def final_block(nc, io, shared):
    with ExitStack() as stack:
        s = Space(nc, stack, "f_")
        x = s.sb("x", [P, TILES, D])
        y = s.sb("y", [P, TILES, D])
        gain = s.sb("gain", [P, D])
        ssq, mean, rstd = s.sb("ssq", [P, TILES]), s.sb("mean", [P, TILES]), s.sb("rstd", [P, TILES])
        half = s.sb("minus_half", [P, 1])
        gain_landed, x_landed = s.sem("gain_landed"), [s.sem(f"x_landed{t}") for t in range(TILES)]
        half_ready, ssq_ready, mean_ready = s.sem("half_ready"), s.sem("ssq_ready"), s.sem("mean_ready")
        rstd_ready, y_ready, stored = s.sem("rstd_ready"), s.sem("y_ready"), s.sem("stored")
        block = stack.enter_context(nc.Block())

        @block.sync
        def _(sp):
            sp.dma_start(gain[:, :], row_broadcast(io.g_final)).then_inc(gain_landed, 16)
            for t in range(TILES):
                sp.dma_start(x[:, t, :], io.acc[t * P:(t + 1) * P, :]).then_inc(x_landed[t], 16)
            for t in range(TILES):
                sp.wait_ge(y_ready, t + 1)
                sp.dma_start(token_rows(io.y_prompt, io.y_sample, t), y[:, t, :]).then_inc(stored, 16)
            sp.wait_ge(stored, 16 * TILES)

        @block.scalar
        def _(act):
            for t in range(TILES):
                act.wait_ge(x_landed[t], 16)
                act.activation(y[:, t, :], x[:, t, :], ACT.Square, accum_out=ssq[:, t:t + 1]).then_inc(ssq_ready, 1)

        @block.gpsimd
        def _(pool):
            pool.memset(half[:, :], -0.5).then_inc(half_ready, 1)
            pool.wait_ge(half_ready, 1)
            for t in range(TILES):
                pool.wait_ge(ssq_ready, t + 1)
                pool.tensor_scalar(mean[:, t:t + 1], ssq[:, t:t + 1], 1.0 / D, EPS,
                                   ALU.mult, ALU.add).then_inc(mean_ready, 1)
                pool.wait_ge(mean_ready, t + 1)
                pool.tensor_tensor(rstd[:, t:t + 1], mean[:, t:t + 1], half[:, :], ALU.pow).then_inc(rstd_ready, 1)

        @block.vector
        def _(dve):
            dve.wait_ge(gain_landed, 16)
            for t in range(TILES):
                dve.wait_ge(rstd_ready, t + 1)
                dve.scalar_tensor_tensor(out=y[:, t, :], in0=x[:, t, :], scalar=rstd[:, t:t + 1], in1=gain[:, :],
                                         op0=ALU.mult, op1=ALU.mult).then_inc(y_ready, 1)
    s.end()


class Tensors:

    def __init__(self, t):
        self.x_prompt, self.x_sample, self.g_attn_a = t["x_prompt"], t["x_sample"], t["g_attn_a"]
        self.w_in_a, self.g_q_a, self.w_uq_a = t["w_in_a"], t["g_q_a"], t["w_uq_a"]
        self.g_kv_a, self.w_ukv_a, self.w_o_a = t["g_kv_a"], t["w_ukv_a"], t["w_o_a"]
        self.g_attn_b, self.w_qkv_b, self.g_qn_b = t["g_attn_b"], t["w_qkv_b"], t["g_qn_b"]
        self.g_kn_b, self.w_o_b, self.g_ffn = t["g_kn_b"], t["w_o_b"], t["g_ffn"]
        self.w_router, self.w_gate, self.w_up = t["w_router"], t["w_gate"], t["w_up"]
        self.w_down, self.g_final, self.rope_a_tok = t["w_down"], t["g_final"], t["rope_a_tok"]
        self.rope_a_T, self.rope_b, self.ident = t["rope_a_T"], t["rope_b"], t["ident"]
        self.y_prompt, self.y_sample, self.acc = t["y_prompt"], t["y_sample"], t["acc"]
        self.xn, self.o_a, self.o_b = t["xn"], t["o_a"], t["o_b"]


class Shared:

    def __init__(self, nc, stack, io):
        s = Space(nc, stack, "s_")
        self.io = io
        self.raw = s.sb("raw", [P, SLOTS, SLOT])
        self.ident = s.sb("ident", [P, P])
        self.row_of = s.sb("row_of", [CAP, EXPERTS], U32)
        self.gate_of = s.sb("gate_of", [CAP, EXPERTS])
        self.ident_landed = s.sem("ident_landed")
        self.w_o_landed = s.sem("w_o_landed")
        self.lists_ready = s.sem("lists_ready")
        self.landed = [s.sem(f"landed{j}") for j in range(SLOTS)]
        arena = self.raw.rearrange("p s n -> p (s n)")
        self.w_o_a = arena[:, (SLOTS - 4) * SLOT:].rearrange("p (k n) -> p k n", n=D)
        self.w_o_b = arena[:, (SLOTS - 8) * SLOT:].rearrange("p (k n) -> p k n", n=D)

    def load_first(self, sp, matrix, layer, first_slot, j):
        src = matrix[layer, 0].rearrange("(c k p) n -> c p k n", c=4, p=P)
        sp.dma_start(self.raw[:, first_slot + j, :].rearrange("p (k n) -> p k n", k=2),
                     src[j]).then_inc(self.landed[first_slot + j], 16)


def build(nc, io):
    with ExitStack() as stack:
        shared = Shared(nc, stack, io)
        mla_block(nc, io, shared)
        output_block(nc, io, shared, 0)
        moe_block(nc, io, shared, 0)
        gqa_block(nc, io, shared)
        output_block(nc, io, shared, 1)
        moe_block(nc, io, shared, 1)
        final_block(nc, io, shared)


def rope_constants():
    def angles(positions, d):
        inv = np.float32(THETA) ** -(np.arange(d // 2, dtype=np.float32) * np.float32(2.0) / np.float32(d))
        a = positions.astype(np.float32)[:, None] * inv[None, :].astype(np.float32)
        c, s = np.cos(a).astype(np.float32), np.sin(a).astype(np.float32)
        return np.concatenate([c, c], 1), np.concatenate([-s, s], 1)

    pos = np.concatenate([np.arange(PROMPT), np.arange(SAMPLE)])
    ca, sa = angles(pos, DR)
    tok = np.stack([ca, sa], 1).reshape(TILES, P, 2, DR).transpose(1, 0, 2, 3)
    turned = np.concatenate([ca.T, sa.T], 0)
    cr, sr = angles(pos // GRID_W, HD // 2)
    cc, sc = angles(pos % GRID_W, HD // 2)
    b = np.stack([np.concatenate([cr, cc], 1), np.concatenate([sr, sc], 1)], 1)
    b = b.reshape(TILES, P, 2, HD).transpose(1, 0, 2, 3)
    return {"rope_a_tok": np.ascontiguousarray(tok), "rope_a_T": np.ascontiguousarray(turned),
            "rope_b": np.ascontiguousarray(b), "ident": np.eye(P, dtype=np.float32)}


INPUTS = ["x_prompt", "x_sample", "g_attn_a", "w_in_a", "g_q_a", "w_uq_a", "g_kv_a", "w_ukv_a", "w_o_a",
          "g_attn_b", "w_qkv_b", "g_qn_b", "g_kn_b", "w_o_b", "g_ffn", "w_router", "w_gate", "w_up",
          "w_down", "g_final"]


def kernel(**inputs):
    import concourse.bacc as bacc
    from concourse.bass_utils import run_bass_kernel_spmd

    nc = bacc.Bacc("TRN2", target_bir_lowering=False, num_devices=1)
    arrays, io = {}, {}
    host = {name: np.ascontiguousarray(inputs[name]) for name in INPUTS} | rope_constants()
    for name, a in host.items():
        arrays[f"in_{name}"] = a
        io[name] = nc.dram_tensor(f"in_{name}", a.shape, mybir.dt.from_np(a.dtype), kind="ExternalInput").ap()
    for name, rows in (("y_prompt", PROMPT), ("y_sample", SAMPLE)):
        io[name] = nc.dram_tensor(f"out_{name}", (1, rows, D), F32, kind="ExternalOutput").ap()
    io["acc"] = nc.dram_tensor("acc", (N, D), F32, kind="Internal").ap()
    io["xn"] = nc.dram_tensor("xn", (N, D), F32, kind="Internal").ap()
    io["o_a"] = nc.dram_tensor("o_a", (N, HEADS * DV), F32, kind="Internal").ap()
    io["o_b"] = nc.dram_tensor("o_b", (N, HEADS * HD), F32, kind="Internal").ap()
    build(nc, Tensors(io))
    r = run_bass_kernel_spmd(nc, [arrays], core_ids=[0])
    return r.results[0]["out_y_prompt"], r.results[0]["out_y_sample"]
```

```python
from contextlib import ExitStack

import numpy as np

import concourse.bass as bass
from concourse import mybir

F32 = mybir.dt.float32
F32R = mybir.dt.float32r
U32 = mybir.dt.uint32
ALU = mybir.AluOpType
ACT = mybir.ActivationFunctionType
AX = mybir.AxisListType

P = 128
D = 1024
KD = D // P
PROMPT, SAMPLE = 256, 512
N = PROMPT + SAMPLE
TILES = N // P
PROMPT_TILES = PROMPT // P
EPS = 1e-6

HEADS = 16
GROUPS = HEADS // 2
Q_LORA, KV_LORA, DN, DR, DV = 384, 256, 64, 32, 64
KQ, KKV = Q_LORA // P, KV_LORA // P
W_IN = Q_LORA + KV_LORA + DR
ARENA_FREE_A = KD * W_IN + KQ * HEADS * (DN + DR) + KKV * HEADS * (DN + DV)
HD = 128
KV_HEADS = 8
THETA = 10000.0
GRID_W = 64

EXPERTS = 16
FF = 1024
CAP_P = 2 * PROMPT // EXPERTS
CAP_S = 2 * SAMPLE // EXPERTS
CAP = CAP_P + CAP_S

UNITS = [(0, 0), (0, 1), (2, 0), (4, 0), (2, 1), (4, 1)]
NU = len(UNITS)

SLOTS = 12
SLOT = 2 * D
SPLITS = 4


def keys_of(unit):
    return (0, PROMPT_TILES) if UNITS[unit][0] < PROMPT_TILES else (PROMPT_TILES, TILES - PROMPT_TILES)


def wait(engine, semaphore, count):
    if isinstance(count, int) and count <= 0:
        return
    engine.wait_ge(semaphore, count)


class Space:

    def __init__(self, nc, stack, prefix):
        self.nc, self.stack, self.prefix, self.sems = nc, stack, prefix, []

    def sb(self, name, shape, dtype=F32):
        return self.stack.enter_context(self.nc.sbuf_tensor(self.prefix + name, shape, dtype))

    def psum(self, name, shape, dtype=F32):
        return self.stack.enter_context(self.nc.psum_tensor(self.prefix + "ps_" + name, shape, dtype))

    def sem(self, name):
        self.sems.append(self.nc.alloc_semaphore(self.prefix + name))
        return self.sems[-1]

    def end(self):
        self.nc.clear_and_free_semaphores(self.sems)
        self.nc.all_engine_barrier()


def token_rows(x_prompt, x_sample, t):
    if t < PROMPT_TILES:
        return x_prompt[0, t * P:(t + 1) * P, :]
    return x_sample[0, (t - PROMPT_TILES) * P:(t - PROMPT_TILES + 1) * P, :]


def row_broadcast(vector):
    return vector.partition_broadcast(P)



class InputNorm:

    def __init__(self, s, x_tile_of, gain_row, xnT, psum, x, xn, junk, gain, xnT_lo=None):
        self.x_tile_of, self.gain_row, self.xnT, self.ps = x_tile_of, gain_row, xnT, psum
        self.xnT_lo = xnT_lo
        self.x, self.xn, self.junk, self.gain = x, xn, junk, gain
        self.ssq = s.sb("norm_ssq", [P, TILES])
        self.mean = s.sb("norm_mean", [P, TILES])
        self.rstd = s.sb("norm_rstd", [P, TILES])
        self.x_landed = [s.sem("norm_x_landed0"), s.sem("norm_x_landed1")]
        self.gain_landed = s.sem("norm_gain_landed")
        self.ssq_ready = s.sem("norm_ssq_ready")
        self.mean_ready = s.sem("norm_mean_ready")
        self.rstd_ready = s.sem("norm_rstd_ready")
        self.xn_ready = s.sem("norm_xn_ready")
        self.turned = s.sem("norm_turned")
        self.copied_act = s.sem("norm_copied_act")
        self.copied_dve = s.sem("norm_copied_dve")

    def act_tile(self, act, t):
        act.wait_ge(self.x_landed[t % 2], 16 * (t // 2 + 1))
        wait(act, self.ssq_ready, t)
        act.activation(self.junk, self.x[:, t % 2, :], ACT.Square,
                       accum_out=self.ssq[:, t:t + 1]).then_inc(self.ssq_ready, 1)

    def act_copy(self, act, t):
        act.wait_ge(self.turned, t + 1)
        if self.xnT_lo is None:
            act.activation(self.xnT[:, 0:KD // 2, t * P:(t + 1) * P], self.ps[:, 0, :, :],
                           ACT.Copy).then_inc(self.copied_act, 1)
        else:
            act.activation(self.xnT[:, :, t * P:(t + 1) * P], self.ps[:, :, :, :].rearrange("p b k n -> p (b k) n"),
                           ACT.Copy).then_inc(self.copied_act, 1)

    def pool_tile(self, pool, t, half):
        pool.wait_ge(self.ssq_ready, t + 1)
        pool.tensor_scalar(self.mean[:, t:t + 1], self.ssq[:, t:t + 1], 1.0 / D, EPS,
                           ALU.mult, ALU.add).then_inc(self.mean_ready, 1)
        pool.wait_ge(self.mean_ready, t + 1)
        pool.tensor_tensor(self.rstd[:, t:t + 1], self.mean[:, t:t + 1], half,
                           ALU.pow).then_inc(self.rstd_ready, 1)

    def dve_tile(self, dve, t):
        if t == 0:
            dve.wait_ge(self.gain_landed, 16)
        dve.wait_ge(self.x_landed[t % 2], 16 * (t // 2 + 1))
        dve.wait_ge(self.rstd_ready, t + 1)
        wait(dve, self.turned, t - 1)
        dve.scalar_tensor_tensor(out=self.xn[:, t % 2, :], in0=self.x[:, t % 2, :],
                                 scalar=self.rstd[:, t:t + 1], in1=self.gain,
                                 op0=ALU.mult, op1=ALU.mult).then_inc(self.xn_ready, 1)

    def dve_copy(self, dve, t):
        if self.xnT_lo is None:
            dve.wait_ge(self.turned, t + 1)
            dve.tensor_copy(self.xnT[:, KD // 2:KD, t * P:(t + 1) * P],
                            self.ps[:, 1, :, :]).then_inc(self.copied_dve, 1)
        else:
            dve.wait_ge(self.copied_act, t + 1)
            at = slice(t * P, (t + 1) * P)
            dve.tensor_tensor(self.xnT_lo[:, :, at], self.ps[:, :, :, :].rearrange("p b k n -> p (b k) n"),
                              self.xnT[:, :, at], ALU.subtract).then_inc(self.copied_dve, 1)

    def pe_tile(self, pe, t, ident):
        pe.wait_ge(self.xn_ready, t + 1)
        wait(pe, self.copied_act, t)
        wait(pe, self.copied_dve, t)
        for k in range(KD):
            last = pe.transpose(self.ps[:, k // 4, k % 4, :], self.xn[:, t % 2, k * P:(k + 1) * P], ident)
        last.then_inc(self.turned, 1)



class Core:

    def __init__(self, s, dk, dv, scale, o_dram, probs):
        self.dk, self.dv, self.scale, self.o_dram = dk, dv, scale, o_dram
        self.S = s.psum("scores", [P, 2, 2, SAMPLE])
        self.T = s.psum("probsT", [P, 2, 4, P])
        self.proj = s.psum("projected", [P, 2, SAMPLE])
        self.probs = probs
        self.probsT = s.sb("probsT_sb", [P, 2, 4, P])
        self.out = s.sb("out", [P, 2, TILES, 2 * dv])
        self.rowmax = s.sb("rowmax", [P, 2, 2])
        self.negmax = s.sb("negmax", [P, 2, 2])
        self.rowsum = s.sb("rowsum", [P, 2, 2])
        self.rinv = s.sb("rinv", [P, 2, 2])
        self.scores_done = s.sem("scores_done")
        self.rowmax_done = s.sem("rowmax_done")
        self.negmax_done = s.sem("negmax_done")
        self.exp_done = s.sem("exp_done")
        self.turned = s.sem("probs_turned")
        self.copied_act = s.sem("probs_copied_act")
        self.copied_dve = s.sem("probs_copied_dve")
        self.rinv_done = s.sem("rinv_done")
        self.pv_done = s.sem("pv_done")
        self.out_done = s.sem("out_done")
        self.stored = [s.sem("stored0"), s.sem("stored1")]


    def pe_scores(self, pe, n, unit, qT, kT, q_index, k_index):
        wait(pe, self.exp_done, 2 * n - 2)
        key, nk = keys_of(unit)
        tile, _ = UNITS[unit]
        for j in range(2):
            last = pe.matmul(self.S[:, unit % 2, j, 0:nk * P],
                             qT[0:self.dk, q_index, (tile + j) * P:(tile + j + 1) * P],
                             kT[0:self.dk, k_index, key * P:(key + nk) * P], start=True, stop=True)
        last.then_inc(self.scores_done, 1)

    def pe_turn(self, pe, n, unit, ident):
        _, nk = keys_of(unit)
        for j in range(2):
            pe.wait_ge(self.exp_done, 2 * n + j + 1)
            wait(pe, self.out_done, 2 * n - 1 + j)
            for k in range(nk):
                last = pe.transpose(self.T[:, j, k, :], self.probs[:, unit % 2, j, k * P:(k + 1) * P], ident)
            last.then_inc(self.turned, 1)

    def pe_pv(self, pe, n, unit, v_of):
        key, nk = keys_of(unit)
        for j in range(2):
            pe.wait_ge(self.copied_act if j == 0 else self.copied_dve, n + 1)
            for k in range(nk):
                last = pe.matmul(self.T[:, j, 0, 0:self.dv], self.probsT[:, j, k, :], v_of(key + k),
                                 start=(k == 0), stop=(k == nk - 1))
            last.then_inc(self.pv_done, 1)


    def act_exp(self, act, n, unit):
        _, nk = keys_of(unit)
        act.wait_ge(self.negmax_done, n + 1)
        wait(act, self.turned, 2 * n - 2)
        wait(act, self.rinv_done, n - 1)
        for j in range(2):
            act.activation(self.probs[:, unit % 2, j, 0:nk * P], self.S[:, unit % 2, j, 0:nk * P], ACT.Exp,
                           bias=self.negmax[:, unit % 2, j:j + 1], scale=self.scale,
                           accum_out=self.rowsum[:, unit % 2, j:j + 1]).then_inc(self.exp_done, 1)

    def act_copy(self, act, n, unit):
        _, nk = keys_of(unit)
        act.wait_ge(self.turned, 2 * n + 1)
        wait(act, self.pv_done, 2 * n - 1)
        act.activation(self.probsT[:, 0, 0:nk, :], self.T[:, 0, 0:nk, :], ACT.Copy).then_inc(self.copied_act, 1)


    def dve_max(self, dve, n, unit):
        _, nk = keys_of(unit)
        dve.wait_ge(self.scores_done, n + 1)
        wait(dve, self.negmax_done, n)
        dve.tensor_reduce(self.rowmax[:, unit % 2, :], self.S[:, unit % 2, :, 0:nk * P], AX.X,
                          ALU.max).then_inc(self.rowmax_done, 1)
        dve.wait_ge(self.rowmax_done, n + 1)
        wait(dve, self.exp_done, 2 * n - 2)
        dve.tensor_scalar(self.negmax[:, unit % 2, :], self.rowmax[:, unit % 2, :], -self.scale, None,
                          ALU.mult).then_inc(self.negmax_done, 1)

    def dve_copy(self, dve, n, unit):
        _, nk = keys_of(unit)
        dve.wait_ge(self.turned, 2 * n + 2)
        wait(dve, self.pv_done, 2 * n)
        dve.tensor_copy(self.probsT[:, 1, 0:nk, :], self.T[:, 1, 0:nk, :]).then_inc(self.copied_dve, 1)

    def dve_rinv(self, dve, n, unit):
        dve.wait_ge(self.exp_done, 2 * n + 2)
        wait(dve, self.out_done, 2 * n)
        dve.reciprocal(self.rinv[:, unit % 2, :], self.rowsum[:, unit % 2, :]).then_inc(self.rinv_done, 1)

    def dve_out(self, dve, g, n, unit, slot, first):
        tile, head = UNITS[unit]
        dve.wait_ge(self.rinv_done, n + 1)
        for j in range(2):
            dve.wait_ge(self.pv_done, 2 * n + j + 1)
            if unit == 0 and j == 0 and not first:
                self.wait_stored(dve, g, slot)
            dve.tensor_scalar(self.out[:, slot, tile + j, head * self.dv:(head + 1) * self.dv],
                              self.T[:, j, 0, 0:self.dv], self.rinv[:, unit % 2, j:j + 1], None,
                              ALU.mult).then_inc(self.out_done, 1)

    def wait_stored(self, dve, g, slot):
        dve.wait_ge(self.stored[slot], 8 * (g - slot))


    def store(self, sp, g, slot):
        sp.wait_ge(self.out_done, 2 * NU * g + 2 * NU)
        sp.dma_start(self.o_dram[:, :, bass.ds(g * 2 * self.dv, 2 * self.dv)],
                     self.out[:, slot, :, :]).then_inc(self.stored[slot], 16)


def loop_groups(engine, step):
    step(0, 0, True, False)
    with engine.Fori(0, (GROUPS - 2) // 2) as i:
        step(i * 2 + 1, 1, False, False)
        step(i * 2 + 2, 0, False, False)
    step(GROUPS - 1, (GROUPS - 1) % 2, False, True)


def loop_groups_but_two(engine, step):
    step(0, 0, True, False)
    with engine.Fori(0, (GROUPS - 4) // 2) as i:
        step(i * 2 + 1, 1, False, False)
        step(i * 2 + 2, 0, False, False)
    step(GROUPS - 3, 1, False, False)
    step(GROUPS - 2, 0, False, False)
    step(GROUPS - 1, 1, False, True)


def mla_block(nc, io, shared):
    with ExitStack() as stack:
        s = Space(nc, stack, "a_")
        arena = shared.raw.rearrange("p s n -> p (s n)")
        w_in = arena[:, 0:KD * W_IN].rearrange("p (k n) -> p k n", k=KD)
        at = KD * W_IN
        w_uq = arena[:, at:at + KQ * HEADS * (DN + DR)].rearrange("p (k n) -> p k n", k=KQ)
        at += KQ * HEADS * (DN + DR)
        w_ukv = arena[:, at:at + KKV * HEADS * (DN + DV)].rearrange("p (k n) -> p k n", k=KKV)
        w_ukv_heads = arena[:, at:at + KKV * HEADS * (DN + DV)].rearrange("p (k h n) -> p k h n", k=KKV, n=DN + DV)

        xnT = s.sb("xnT", [P, KD, N])
        c_norm = s.sb("c_norm", [P, 2, Q_LORA + KV_LORA])
        c_gain = s.sb("c_gain", [P, Q_LORA + KV_LORA])
        cT = s.sb("cT", [P, KQ + KKV, N])
        squares = s.sb("c_squares", [P, Q_LORA])
        c_ssq = s.sb("c_ssq", [P, TILES, 2])
        c_mean = s.sb("c_mean", [P, TILES, 2])
        c_rstd = s.sb("c_rstd", [P, TILES, 2])
        half = s.sb("minus_half", [P, 2])
        rope_tok = s.sb("rope_tok", [P, TILES, 2, DR])
        rope_T = s.sb("rope_T", [P, N])
        kr = s.sb("kr", [P, 2, 3, DR])
        qT = s.sb("qT", [DN + DR, 4, N])
        kT = s.sb("kT", [DN + DR, 4, N])
        V = s.sb("V", [P, 2, TILES, 2 * DV])
        stage_q = s.sb("stage_q", [P, 2, KQ, P])
        stage_k = s.sb("stage_k", [P, KKV, P])
        qr = s.sb("qr", [DN + DR, 2, SAMPLE])
        core = Core(s, DN + DR, DV, (DN + DR) ** -0.5, io.o_a.rearrange("(t p) n -> p t n", p=P),
                    s.sb("probs", [P, 2, 2, SAMPLE]))
        norm = InputNorm(s, lambda t: token_rows(io.x_prompt, io.x_sample, t), row_broadcast(io.g_attn_a[0]),
                         xnT, core.S[:, 0, :, :].rearrange("p b (k n) -> p b k n", n=P),
                         x=arena[:, ARENA_FREE_A:ARENA_FREE_A + 2 * D].rearrange("p (b n) -> p b n", b=2),
                         xn=core.probs.rearrange("p b j n -> p b (j n)"),
                         junk=core.probsT[:, :, :, :].rearrange("p j k n -> p (j k n)"),
                         gain=V[:, :, :, :].rearrange("p b t n -> p (b t n)")[:, 0:D])
        c_raw = core.out[:, :, :, :].rearrange("p b t n -> p b (t n)")[:, :, 0:W_IN]
        c_ps = core.S[:, 1, :, :]
        cT_ps = core.T

        w_in_landed, w_uq_landed, w_ukv_landed = s.sem("w_in_landed"), s.sem("w_uq_landed"), s.sem("w_ukv_landed")
        tables_landed = s.sem("tables_landed")
        half_ready = s.sem("half_ready")
        c_done, c_copied = s.sem("c_done"), s.sem("c_copied")
        c_squared, c_mean_ready, c_rstd_ready = s.sem("c_squared"), s.sem("c_mean_ready"), s.sem("c_rstd_ready")
        c_normed, kr_parts, kr_ready = s.sem("c_normed"), s.sem("kr_parts"), s.sem("kr_ready")
        cT_done, cT_copied, krT_copied = s.sem("cT_done"), s.sem("cT_copied"), s.sem("krT_copied")
        q_staged, k_staged = s.sem("q_staged"), s.sem("k_staged")
        piece_done, piece_act = s.sem("piece_done"), s.sem("piece_act")
        qr_parts, piece_dve = s.sem("qr_parts"), s.sem("piece_dve")

        ROPES = [1, 2, 2, 3, 4, 4]
        block = stack.enter_context(nc.Block())

        @block.sync
        def _(sp):
            sp.dma_start(shared.ident[:, :], io.ident).then_inc(shared.ident_landed, 16)
            for t in range(2):
                sp.dma_start(norm.x[:, t, :], norm.x_tile_of(t)).then_inc(norm.x_landed[t], 16)
            sp.dma_start(norm.gain, norm.gain_row).then_inc(norm.gain_landed, 16)
            sp.dma_start(w_in, io.w_in_a[0].rearrange("(k p) n -> p k n", p=P)).then_inc(w_in_landed, 16)
            sp.dma_start(c_gain[:, 0:Q_LORA], row_broadcast(io.g_q_a[0])).then_inc(tables_landed, 16)
            sp.dma_start(c_gain[:, Q_LORA:], row_broadcast(io.g_kv_a[0])).then_inc(tables_landed, 16)
            sp.dma_start(rope_tok[:, :, :, :], io.rope_a_tok).then_inc(tables_landed, 16)
            sp.dma_start(rope_T[2 * DR:, :], io.rope_a_T).then_inc(tables_landed, 16)
            for t in range(2, TILES):
                sp.wait_ge(norm.xn_ready, t - 1)
                sp.dma_start(norm.x[:, t % 2, :], norm.x_tile_of(t)).then_inc(norm.x_landed[t % 2], 16)
            sp.dma_start(w_uq, io.w_uq_a[0].rearrange("(k p) n -> p k n", p=P)).then_inc(w_uq_landed, 16)
            sp.dma_start(w_ukv, io.w_ukv_a[0].rearrange("(k p) n -> p k n", p=P)).then_inc(w_ukv_landed, 16)
            sp.dma_start(shared.w_o_a, io.w_o_a[0].rearrange("(k p) n -> p k n", p=P)).then_inc(shared.w_o_landed, 16)
            loop_groups(sp, lambda g, slot, first, last: core.store(sp, g, slot))
            for slot in range(2):
                sp.wait_ge(core.stored[slot], 16 * GROUPS // 2)

        @block.gpsimd
        def _(pool):
            pool.memset(half[:, :], -0.5).then_inc(half_ready, 1)
            pool.wait_ge(half_ready, 1)

            def c_scale(t):
                pool.wait_ge(c_squared, 2 * t + 2)
                pool.tensor_scalar(c_mean[:, t, 0:1], c_ssq[:, t, 0:1], 1.0 / Q_LORA, EPS,
                                   ALU.mult, ALU.add).then_inc(c_mean_ready, 1)
                pool.tensor_scalar(c_mean[:, t, 1:2], c_ssq[:, t, 1:2], 1.0 / KV_LORA, EPS,
                                   ALU.mult, ALU.add).then_inc(c_mean_ready, 1)
                pool.wait_ge(c_mean_ready, 2 * t + 2)
                pool.tensor_tensor(c_rstd[:, t, :], c_mean[:, t, :], half[:, :], ALU.pow).then_inc(c_rstd_ready, 1)

            def stage(g):
                wait(pool, piece_done, NU * g - 3)
                pool.tensor_copy(stage_k[:, :, :].rearrange("p k (h n) -> p k h n", h=2),
                                 w_ukv_heads[:, :, bass.ds(g * 2, 2), 0:DN]).then_inc(k_staged, 1)
                for h in range(2):
                    wait(pool, piece_done, NU * g - 2 + h)
                    at = (g * 2 + h) * (DN + DR)
                    pool.tensor_copy(stage_q[:, h, :, 0:DN + DR], w_uq[:, :, bass.ds(at, DN + DR)])
                    pool.tensor_copy(stage_q[:, h, :, DN + DR:DN + DR + DR // 2],
                                     w_uq[:, :, bass.ds(at + DN + DR // 2, DR // 2)])
                    pool.tensor_copy(stage_q[:, h, :, DN + DR + DR // 2:],
                                     w_uq[:, :, bass.ds(at + DN, DR // 2)]).then_inc(q_staged, 1)

            norm.pool_tile(pool, 0, half[:, 0:1])
            norm.pool_tile(pool, 1, half[:, 0:1])
            for t in range(TILES):
                if t + 2 < TILES:
                    norm.pool_tile(pool, t + 2, half[:, 0:1])
                if t == TILES - 2:
                    pool.wait_ge(w_uq_landed, 16)
                    pool.wait_ge(w_ukv_landed, 16)
                    stage(0)
                c_scale(t)
            stage(1)
            with pool.Fori(2, GROUPS) as g:
                stage(g)

        @block.scalar
        def _(act):
            def compressed(t):
                act.wait_ge(c_done, t + 1)
                wait(act, c_normed, t - 1)
                wait(act, kr_parts, 3 * (t - 1))
                act.activation(c_raw[:, t % 2, 0:SAMPLE], c_ps[:, 0, :], ACT.Copy)
                act.activation(c_raw[:, t % 2, SAMPLE:], c_ps[:, 1, 0:W_IN - SAMPLE], ACT.Copy).then_inc(c_copied, 1)
                act.wait_ge(c_copied, t + 1)
                wait(act, c_squared, 2 * t)
                act.activation(squares[:, :], c_raw[:, t % 2, 0:Q_LORA], ACT.Square,
                               accum_out=c_ssq[:, t, 0:1]).then_inc(c_squared, 1)
                act.wait_ge(c_squared, 2 * t + 1)
                act.activation(squares[:, 0:KV_LORA], c_raw[:, t % 2, Q_LORA:Q_LORA + KV_LORA], ACT.Square,
                               accum_out=c_ssq[:, t, 1:2]).then_inc(c_squared, 1)

            def turned_c(t):
                act.wait_ge(cT_done, t + 1)
                act.activation(cT[:, 0:4, t * P:(t + 1) * P], cT_ps[:, 0, :, :], ACT.Copy)
                act.activation(cT[:, 4:5, t * P:(t + 1) * P], cT_ps[:, 1, 0:1, :], ACT.Copy).then_inc(cT_copied, 1)

            def piece(g, slot, p):
                act.wait_ge(piece_done, NU * g + p + 1)
                if not (isinstance(g, int) and g < 2):
                    act.wait_ge(core.scores_done, NU * g - NU)
                    act.wait_ge(core.pv_done, 2 * NU * g - 2 * NU)
                bank = core.proj[:, p % 2, :]
                if p in (0, 2):
                    cols, src = (slice(0, PROMPT), bank[:, 0:PROMPT]) if p == 0 else (slice(PROMPT, N), bank)
                    act.activation(kT[0:DN, 2 * slot, cols], src[0:DN], ACT.Copy)
                    last = act.activation(kT[0:DN, 2 * slot + 1, cols], src[DN:2 * DN], ACT.Copy)
                if p == 0:
                    last = act.activation(qT[0:DN, 2 * slot, 0:PROMPT], bank[0:DN, PROMPT:], ACT.Copy)
                if p == 1:
                    act.activation(qT[0:DN, 2 * slot + 1, 0:PROMPT], bank[0:DN, 0:PROMPT], ACT.Copy)
                    last = act.activation(V[:, slot, 0:PROMPT_TILES, :].rearrange("p t n -> p (t n)"),
                                          bank[:, PROMPT:], ACT.Copy)
                if p in (3, 4):
                    last = act.activation(qT[0:DN, 2 * slot + p - 3, PROMPT:N], bank[0:DN, :], ACT.Copy)
                if p == 5:
                    last = act.activation(V[:, slot, PROMPT_TILES:, :].rearrange("p t n -> p (t n)"),
                                          bank, ACT.Copy)
                last.then_inc(piece_act, 1)

            norm.act_tile(act, 0)
            norm.act_tile(act, 1)
            for i in range(TILES + 1):
                if i < TILES:
                    norm.act_copy(act, i)
                if i + 2 < TILES:
                    norm.act_tile(act, i + 2)
                if i >= 1:
                    compressed(i - 1)
                if i >= 2:
                    turned_c(i - 2)
            for p in range(NU):
                if p == 2:
                    turned_c(TILES - 1)
                piece(0, 0, p)
            core.act_exp(act, 0, 0)

            def step(g, slot, first, last):
                for unit in range(NU):
                    n = g * NU + unit
                    core.act_copy(act, n, unit)
                    if not (last and unit == NU - 1):
                        core.act_exp(act, n + 1, (unit + 1) % NU)
                    if not last:
                        piece(g + 1, 1 - slot, unit)

            loop_groups(act, step)

        @block.vector
        def _(dve):
            def compressed(t):
                raw = c_raw[:, t % 2, :]
                if t == 0:
                    dve.wait_ge(tables_landed, 64)
                dve.wait_ge(c_rstd_ready, t + 1)
                wait(dve, cT_done, t - 1)
                dve.scalar_tensor_tensor(out=c_norm[:, t % 2, 0:Q_LORA], in0=raw[:, 0:Q_LORA],
                                         scalar=c_rstd[:, t, 0:1], in1=c_gain[:, 0:Q_LORA],
                                         op0=ALU.mult, op1=ALU.mult)
                dve.scalar_tensor_tensor(out=c_norm[:, t % 2, Q_LORA:], in0=raw[:, Q_LORA:Q_LORA + KV_LORA],
                                         scalar=c_rstd[:, t, 1:2], in1=c_gain[:, Q_LORA:],
                                         op0=ALU.mult, op1=ALU.mult).then_inc(c_normed, 1)
                r, h = raw[:, Q_LORA + KV_LORA:], DR // 2
                dve.tensor_tensor(kr[:, t % 2, 0, :], r, rope_tok[:, t, 0, :], ALU.mult).then_inc(kr_parts, 1)
                dve.tensor_tensor(kr[:, t % 2, 1, 0:h], r[:, h:], rope_tok[:, t, 1, 0:h],
                                  ALU.mult).then_inc(kr_parts, 1)
                dve.tensor_tensor(kr[:, t % 2, 1, h:], r[:, 0:h], rope_tok[:, t, 1, h:],
                                  ALU.mult).then_inc(kr_parts, 1)
                dve.wait_ge(kr_parts, 3 * t + 3)
                dve.tensor_tensor(kr[:, t % 2, 2, :], kr[:, t % 2, 0, :], kr[:, t % 2, 1, :],
                                  ALU.add).then_inc(kr_ready, 1)

            def turned_c(t):
                dve.wait_ge(cT_copied, t + 1)
                for b in range(4):
                    last = dve.tensor_copy(kT[DN:, b, t * P:(t + 1) * P], cT_ps[0:DR, 1, 1, :])
                last.then_inc(krT_copied, 1)

            def piece(g, slot, p):
                if p in (2, 5):
                    return
                r = g * 4 + ROPES[p] - 1
                head = 0 if p in (0, 3) else 1
                bank = core.proj[:, p % 2, :]
                width = PROMPT if p < 2 else SAMPLE
                src = bank[:, PROMPT:] if p == 0 else bank[:, 0:width]
                cols = slice(0, PROMPT) if p < 2 else slice(PROMPT, N)
                dve.wait_ge(piece_done, NU * g + p + 1)
                if p < 2:
                    dve.wait_ge(piece_act, NU * g + p + 1)
                wait(dve, piece_dve, r)
                dve.tensor_tensor(qr[DN:, 0, 0:width], src[DN:DN + DR], rope_T[DN:DN + DR, cols],
                                  ALU.mult).then_inc(qr_parts, 1)
                dve.tensor_tensor(qr[DN:, 1, 0:width], src[DN + DR:], rope_T[DN + DR:, cols],
                                  ALU.mult).then_inc(qr_parts, 1)
                dve.wait_ge(qr_parts, r * 2 + 2)
                if not (isinstance(g, int) and g < 2):
                    dve.wait_ge(core.scores_done, NU * g - NU)
                dve.tensor_tensor(qT[DN:, 2 * slot + head, cols], qr[DN:, 0, 0:width], qr[DN:, 1, 0:width],
                                  ALU.add).then_inc(piece_dve, 1)

            norm.dve_tile(dve, 0)
            for i in range(TILES + 1):
                if i + 1 < TILES:
                    norm.dve_tile(dve, i + 1)
                if i < TILES:
                    norm.dve_copy(dve, i)
                if i >= 1:
                    compressed(i - 1)
                if i >= 2:
                    turned_c(i - 2)
            for p in range(NU):
                if p == 2:
                    turned_c(TILES - 1)
                piece(0, 0, p)
            core.dve_max(dve, 0, 0)
            core.dve_max(dve, 1, 1)

            def step(g, slot, first, last):
                for unit in range(NU):
                    n = g * NU + unit
                    core.dve_copy(dve, n, unit)
                    core.dve_rinv(dve, n, unit)
                    if not last:
                        piece(g + 1, 1 - slot, unit)
                    core.dve_out(dve, g, n, unit, slot, first or (isinstance(g, int) and g < 2))
                    if not (last and unit >= NU - 2):
                        core.dve_max(dve, n + 2, (unit + 2) % NU)

            loop_groups(dve, step)

        @block.tensor
        def _(pe):
            pe.wait_ge(shared.ident_landed, 16)
            def turn_c(t):
                pe.wait_ge(c_normed, t + 1)
                pe.wait_ge(kr_ready, t + 1)
                wait(pe, cT_copied, t)
                wait(pe, krT_copied, t)
                for k in range(KQ + KKV):
                    pe.transpose(cT_ps[:, k // 4, k % 4, :], c_norm[:, t % 2, k * P:(k + 1) * P], shared.ident[:, :])
                pe.transpose(cT_ps[0:DR, 1, 1, :], kr[:, t % 2, 2, :], shared.ident[:, :]).then_inc(cT_done, 1)

            def compress(t):
                if t == 0:
                    pe.wait_ge(w_in_landed, 16)
                pe.wait_ge(norm.copied_act, t + 1)
                pe.wait_ge(norm.copied_dve, t + 1)
                wait(pe, c_copied, t)
                for lo, hi in ((0, SAMPLE), (SAMPLE, W_IN)):
                    for k in range(KD):
                        last = pe.matmul(c_ps[:, lo // SAMPLE, 0:hi - lo], xnT[:, k, t * P:(t + 1) * P],
                                         w_in[:, k, lo:hi], start=(k == 0), stop=(k == KD - 1))
                last.then_inc(c_done, 1)

            def queries(g, h, out, cols):
                pe.wait_ge(q_staged, g * 2 + h + 1)
                for k in range(KQ):
                    last = pe.matmul(out, stage_q[:, h, k, :], cT[:, k, cols], start=(k == 0), stop=(k == KQ - 1))
                return last

            def keys(g, out, cols):
                pe.wait_ge(k_staged, g + 1)
                for k in range(KKV):
                    last = pe.matmul(out, stage_k[:, k, :], cT[:, KQ + k, cols], start=(k == 0), stop=(k == KKV - 1))
                return last

            def values(g, out, t):
                w = w_ukv_heads[:, :, bass.ds(g * 2, 2), DN:]
                for k in range(KKV):
                    last = pe.matmul(out, cT[:, KQ + k, t * P:(t + 1) * P], w[:, k], start=(k == 0),
                                     stop=(k == KKV - 1))
                return last

            def piece(g, p):
                m = g * NU + p
                wait(pe, piece_act, m - 1)
                wait(pe, piece_dve, g * 4 + [-1, 0, 1, 2, 2, 3][p])
                bank = core.proj[:, p % 2, :]
                if p == 0:
                    keys(g, bank[:, 0:PROMPT], slice(0, PROMPT))
                    last = queries(g, 0, bank[:, PROMPT:], slice(0, PROMPT))
                if p == 1:
                    queries(g, 1, bank[:, 0:PROMPT], slice(0, PROMPT))
                    for t in range(PROMPT_TILES):
                        last = values(g, bank[:, PROMPT + t * P:PROMPT + (t + 1) * P], t)
                if p == 2:
                    last = keys(g, bank, slice(PROMPT, N))
                if p in (3, 4):
                    last = queries(g, p - 3, bank, slice(PROMPT, N))
                if p == 5:
                    for t in range(PROMPT_TILES, TILES):
                        last = values(g, bank[:, (t - PROMPT_TILES) * P:(t - PROMPT_TILES + 1) * P], t)
                last.then_inc(piece_done, 1)

            def scores(g, slot, unit):
                tile, head = UNITS[unit]
                needs = (head + 1) if tile < PROMPT_TILES else 4 + head
                pe.wait_ge(piece_act, g * NU + needs)
                pe.wait_ge(piece_dve, g * 4 + ROPES[needs - 1])
                core.pe_scores(pe, g * NU + unit, unit, qT, kT, 2 * slot + head, 2 * slot + head)

            for i in range(TILES + 1):
                if i < TILES:
                    norm.pe_tile(pe, i, shared.ident[:, :])
                if i >= 1:
                    compress(i - 1)
                if i >= 2:
                    turn_c(i - 2)
            pe.wait_ge(cT_copied, PROMPT_TILES)
            for p in range(NU):
                if p == 2:
                    turn_c(TILES - 1)
                    pe.wait_ge(cT_copied, TILES)
                    pe.wait_ge(krT_copied, TILES)
                piece(0, p)
            scores(0, 0, 0)
            scores(0, 0, 1)

            def step(g, slot, first, last):
                for unit in range(NU):
                    n = g * NU + unit
                    _, head = UNITS[unit]
                    core.pe_turn(pe, n, unit, shared.ident[:, :])
                    if not last:
                        piece(g + 1, unit)
                    pe.wait_ge(piece_act, g * NU + (2 if unit < 2 else NU))
                    core.pe_pv(pe, n, unit, lambda t: V[:, slot, t, head * DV:(head + 1) * DV])
                    if unit < NU - 2:
                        scores(g, slot, unit + 2)
                    elif not last:
                        scores(g + 1, 1 - slot, unit + 2 - NU)

            loop_groups(pe, step)
    s.end()


def gqa_block(nc, io, shared):
    with ExitStack() as stack:
        s = Space(nc, stack, "b_")
        arena = shared.raw.rearrange("p s n -> p (s n)")
        W = 4 * HD
        HALF_K = KD // 2
        w_raw = arena[:, 0:KD * W].rearrange("p (b k n) -> p b k n", b=2, k=HALF_K)
        w_hi = shared.over_raw(nc, "b_w_hi", [P, 2, KD, W], 4)
        w_lo = shared.over_raw(nc, "b_w_lo", [P, 2, KD, W], 8)
        squares = arena[:, KD * W:KD * W + 3 * HD].rearrange("p (h n) -> p h n", h=3)
        straight = arena[:, KD * W + 3 * HD:KD * W + 6 * HD].rearrange("p (h n) -> p h n", h=3)
        crossed = arena[:, KD * W + 6 * HD:KD * W + 9 * HD].rearrange("p (h n) -> p h n", h=3)
        raw = arena[:, KD * W + 9 * HD:KD * W + 15 * HD].rearrange("p (b h n) -> p b h n", b=2, h=3)
        probs = arena[:, KD * W + 15 * HD:KD * W + 15 * HD + 4 * SAMPLE].rearrange("p (b j n) -> p b j n", b=2, j=2)
        xnT = s.sb("xnT", [P, KD, N], F32R)
        xnT_lo = s.sb("xnT_lo", [P, KD, N], F32R)
        tables = s.sb("tables", [P, TILES, 2, 3, HD])
        half = s.sb("minus_half", [P, 3])
        ssq = s.sb("ssq", [P, 2, 3])
        mean = s.sb("mean", [P, 2, 3])
        rstd = s.sb("rstd", [P, 2, 3])
        normed = s.sb("normed", [P, 2, 3, HD])
        qkT = s.sb("qkT", [P, 2, 3, N])
        V = s.sb("V", [P, 2, TILES, HD])
        core = Core(s, HD, HD, HD ** -0.5, io.o_b.rearrange("(t p) n -> p t n", p=P), probs)
        out_flat = core.out[:, :, :, :].rearrange("p b t n -> p (b t n)")
        norm = InputNorm(s, lambda t: io.acc[t * P:(t + 1) * P, :], row_broadcast(io.g_attn_b[0]), xnT,
                         core.S[:, 0, :, :].rearrange("p b (k n) -> p b k n", n=P),
                         x=out_flat[:, 0:2 * D].rearrange("p (b n) -> p b n", b=2),
                         xn=core.probs.rearrange("p b j n -> p b (j n)"),
                         junk=core.probsT[:, :, :, :].rearrange("p j k n -> p (j k n)"),
                         gain=out_flat[:, 2 * D:3 * D], xnT_lo=xnT_lo)
        first_turns = core.T[:, :, :, :].rearrange("p b k n -> p b (k n)")
        rope = qkT[:, 1, 0:2, :].rearrange("p h (t a n) -> p (h t) a n", a=2, n=HD)
        gains = qkT[:, 1, 2, 0:2 * HD].rearrange("p (g n) -> p g n", g=2)

        w_landed = [s.sem("w_landed0"), s.sem("w_landed1")]
        tables_landed, tables_parts, tables_ready = s.sem("tables_landed"), s.sem("tables_parts"), s.sem("tables_ready")
        half_ready, w_high, w_split = s.sem("half_ready"), s.sem("w_high"), s.sem("w_split")
        proj_done, raw_ready, v_ready, sq_ready = s.sem("proj_done"), s.sem("raw_ready"), s.sem("v_ready"), s.sem("sq_ready")
        ssq_ready, mean_ready, rstd_ready = s.sem("ssq_ready"), s.sem("mean_ready"), s.sem("rstd_ready")
        normed_ready, straight_ready, crossed_ready = s.sem("normed_ready"), s.sem("straight_ready"), s.sem("crossed_ready")
        roped_ready, qkT_done, qkT_copied = s.sem("roped_ready"), s.sem("qkT_done"), s.sem("qkT_copied")
        block = stack.enter_context(nc.Block())

        @block.sync
        def _(sp):
            def weights(g, h):
                if not (isinstance(g, int) and g == 0):
                    sp.wait_ge(w_split, g * 2 - 1 + h)
                src = io.w_qkv_b[0].rearrange("(h k p) n -> h p k n", h=2, p=P)[h]
                dst = w_raw[:, h]
                sp.dma_start(dst[:, :, 0:2 * HD], src[:, :, bass.ds(g * 2 * HD, 2 * HD)]).then_inc(w_landed[h], 16)
                sp.dma_start(dst[:, :, 2 * HD:3 * HD],
                             src[:, :, bass.ds(g * HD + HEADS * HD, HD)]).then_inc(w_landed[h], 16)
                sp.dma_start(dst[:, :, 3 * HD:],
                             src[:, :, bass.ds(g * HD + (HEADS + KV_HEADS) * HD, HD)]).then_inc(w_landed[h], 16)

            for t in range(2):
                sp.dma_start(norm.x[:, t % 2, :], norm.x_tile_of(t)).then_inc(norm.x_landed[t], 16)
            sp.dma_start(norm.gain, norm.gain_row).then_inc(norm.gain_landed, 16)
            weights(0, 0)
            weights(0, 1)
            sp.dma_start(rope[:, :, :, :], io.rope_b).then_inc(tables_landed, 16)
            sp.dma_start(gains[:, 0, :], row_broadcast(io.g_qn_b[0])).then_inc(tables_landed, 16)
            sp.dma_start(gains[:, 1, :], row_broadcast(io.g_kn_b[0])).then_inc(tables_landed, 16)
            for t in range(2, TILES):
                sp.wait_ge(norm.xn_ready, t - 1)
                sp.dma_start(norm.x[:, t % 2, :], norm.x_tile_of(t)).then_inc(norm.x_landed[t % 2], 16)
            weights(1, 0)
            weights(1, 1)

            def step(g, slot):
                weights(g + 2, 0)
                weights(g + 2, 1)
                core.store(sp, g, slot)

            step(0, 0)
            step(1, 1)
            with sp.Fori(1, GROUPS // 2 - 1) as i:
                step(i * 2, 0)
                step(i * 2 + 1, 1)
            sp.wait_ge(proj_done, NU * GROUPS)
            sp.dma_start(shared.w_o_b, io.w_o_b[0].rearrange("(k p) n -> p k n", p=P)).then_inc(shared.w_o_landed, 16)
            core.store(sp, GROUPS - 2, 0)
            core.store(sp, GROUPS - 1, 1)
            for slot in range(2):
                sp.wait_ge(core.stored[slot], 16 * GROUPS // 2)

        @block.gpsimd
        def _(pool):
            pool.memset(half[:, :], -0.5).then_inc(half_ready, 1)
            pool.wait_ge(half_ready, 1)

            def table(h):
                gain = gains[:, h // 2, :]
                pool.tensor_tensor(tables[:, :, 0, h, :], rope[:, :, 0, :],
                                   gain.unsqueeze(1).to_broadcast([P, TILES, HD]), ALU.mult).then_inc(tables_ready, 1)
                for axis in range(2):
                    for side in range(2):
                        at, other = axis * 64 + side * 32, axis * 64 + (1 - side) * 32
                        pool.tensor_tensor(tables[:, :, 1, h, at:at + 32], rope[:, :, 1, at:at + 32],
                                           gain[:, other:other + 32].unsqueeze(1).to_broadcast([P, TILES, 32]),
                                           ALU.mult).then_inc(tables_ready, 1)

            def tile(m, t):
                pool.wait_ge(mean_ready, m + 1)
                wait(pool, normed_ready, m)
                pool.tensor_tensor(rstd[:, t % 2, :], mean[:, t % 2, :], half[:, :], ALU.pow).then_inc(rstd_ready, 1)
                pool.wait_ge(rstd_ready, m + 1)
                wait(pool, qkT_done, m - 1)
                pool.tensor_tensor(normed[:, t % 2, :, :], raw[:, t % 2, :, :],
                                   rstd[:, t % 2, :].unsqueeze(2).to_broadcast([P, 3, HD]),
                                   ALU.mult).then_inc(normed_ready, 1)
                pool.wait_ge(normed_ready, m + 1)
                wait(pool, roped_ready, m)
                pool.tensor_tensor(straight[:, :, :], normed[:, t % 2, :, :], tables[:, t, 0, :, :],
                                   ALU.mult).then_inc(straight_ready, 1)

            norm.pool_tile(pool, 0, half[:, 0:1])
            norm.pool_tile(pool, 1, half[:, 0:1])
            pool.wait_ge(tables_landed, 48)
            for h in range(3):
                table(h)
                norm.pool_tile(pool, 2 + h, half[:, 0:1])
            norm.pool_tile(pool, TILES - 1, half[:, 0:1])
            pool.wait_ge(tables_ready, 5 * 3)
            for t in range(TILES):
                tile(t, t)
            with pool.Fori(1, GROUPS) as g:
                for t in range(TILES):
                    tile(g * NU + t, t)

        @block.scalar
        def _(act):
            def split_high(g, slot, h):
                act.wait_ge(w_landed[h], g * 48 + 48)
                if not (isinstance(g, int) and g < 2):
                    act.wait_ge(proj_done, g * NU - NU)
                act.activation(w_hi[:, slot, h * HALF_K:(h + 1) * HALF_K, :], w_raw[:, h],
                               ACT.Copy).then_inc(w_high, 1)

            def projected(g, slot, t):
                m = g * NU + t
                bank = core.proj[:, t % 2, :].rearrange("p (h n) -> p h n", h=4)
                act.wait_ge(proj_done, m + 1)
                wait(act, normed_ready, m - 1)
                act.activation(raw[:, t % 2, :, :], bank[:, 0:3, :], ACT.Copy).then_inc(raw_ready, 1)
                wait(act, ssq_ready, m)
                act.activation(squares, bank[:, 0:3, :], ACT.Square).then_inc(sq_ready, 1)
                if not (isinstance(g, int) and g < 2):
                    act.wait_ge(core.pv_done, 2 * NU * g - 2 * NU)
                act.activation(V[:, slot, t, :], bank[:, 3, :], ACT.Copy).then_inc(v_ready, 1)

            def turned(g, slot, t, banks):
                m = g * NU + t
                bank = banks[:, t % 2, :].rearrange("p (h n) -> p h n", h=4)
                act.wait_ge(qkT_done, m + 1)
                if not (isinstance(g, int) and g < 2):
                    act.wait_ge(core.scores_done, NU * g - NU)
                act.activation(qkT[:, slot, :, t * P:(t + 1) * P], bank[:, 0:3, :],
                               ACT.Copy).then_inc(qkT_copied, 1)

            norm.act_tile(act, 0)
            norm.act_tile(act, 1)
            for i in range(TILES + 2):
                if i < TILES:
                    norm.act_copy(act, i)
                if i == 0:
                    split_high(0, 0, 0)
                    split_high(0, 0, 1)
                if i + 2 < TILES:
                    norm.act_tile(act, i + 2)
                if 1 <= i <= TILES:
                    projected(0, 0, i - 1)
                if i >= 3:
                    turned(0, 0, i - 3, first_turns)
                if i >= TILES:
                    split_high(1, 1, i - TILES)
            core.act_exp(act, 0, 0)

            def step(g, slot, first, last):
                for unit in range(NU):
                    n = g * NU + unit
                    core.act_copy(act, n, unit)
                    if unit == 0:
                        core.act_exp(act, n + 1, 1)
                        if not last:
                            projected(g + 1, 1 - slot, 0)
                        turned(g, slot, TILES - 1, core.proj)
                        continue
                    if not (last and unit == NU - 1):
                        core.act_exp(act, n + 1, (unit + 1) % NU)
                    if not last:
                        projected(g + 1, 1 - slot, unit)
                        turned(g + 1, 1 - slot, unit - 1, core.proj)
                    if unit in (1, 4) and not (isinstance(g, int) and g >= GROUPS - 2):
                        split_high(g + 2, slot, unit // 4)

            loop_groups_but_two(act, step)

        @block.vector
        def _(dve):
            def split_low(g, slot, h):
                dve.wait_ge(w_high, g * 2 + h + 1)
                dve.tensor_tensor(w_lo[:, slot, h * HALF_K:(h + 1) * HALF_K, :], w_raw[:, h],
                                  w_hi[:, slot, h * HALF_K:(h + 1) * HALF_K, :], ALU.subtract).then_inc(w_split, 1)

            def squared(m, t):
                dve.wait_ge(sq_ready, m + 1)
                wait(dve, mean_ready, m - 1)
                dve.tensor_reduce(ssq[:, t % 2, :], squares, AX.X, ALU.add).then_inc(ssq_ready, 1)
                dve.wait_ge(ssq_ready, m + 1)
                wait(dve, rstd_ready, m - 1)
                dve.tensor_scalar(mean[:, t % 2, :], ssq[:, t % 2, :], 1.0 / HD, EPS,
                                  ALU.mult, ALU.add).then_inc(mean_ready, 1)

            def rotate(m, t):
                dve.wait_ge(normed_ready, m + 1)
                wait(dve, roped_ready, m)
                a = normed[:, t % 2, :, :].rearrange("p h (x s n) -> p (h x) s n", x=2, s=2)
                c = crossed[:, :, :].rearrange("p h (x s n) -> p (h x) s n", x=2, s=2)
                sin = tables[:, t, 1, :, :].rearrange("p h (x s n) -> p (h x) s n", x=2, s=2)
                for side in range(2):
                    dve.tensor_tensor(c[:, :, side, :], a[:, :, 1 - side, :], sin[:, :, side, :],
                                      ALU.mult).then_inc(crossed_ready, 1)
                dve.wait_ge(crossed_ready, 2 * m + 2)
                dve.wait_ge(straight_ready, m + 1)
                dve.tensor_tensor(normed[:, t % 2, :, :], straight[:, :, :], crossed[:, :, :],
                                  ALU.add).then_inc(roped_ready, 1)

            norm.dve_tile(dve, 0)
            for i in range(TILES + 2):
                if i + 1 < TILES:
                    norm.dve_tile(dve, i + 1)
                if i < TILES:
                    norm.dve_copy(dve, i)
                if i == 0:
                    split_low(0, 0, 0)
                    split_low(0, 0, 1)
                if 1 <= i <= TILES:
                    squared(i - 1, i - 1)
                if 2 <= i < TILES + 1:
                    rotate(i - 2, i - 2)
                if i >= TILES:
                    split_low(1, 1, i - TILES)
            core.dve_max(dve, 0, 0)
            core.dve_max(dve, 1, 1)

            def step(g, slot, first, last):
                for unit in range(NU):
                    n = g * NU + unit
                    core.dve_copy(dve, n, unit)
                    core.dve_rinv(dve, n, unit)
                    if unit == 0:
                        rotate(g * NU + TILES - 1, TILES - 1)
                    elif not last:
                        rotate(g * NU + NU + unit - 1, unit - 1)
                    if not last:
                        squared(g * NU + NU + unit, unit)
                    core.dve_out(dve, g, n, unit, slot, first or (isinstance(g, int) and g < 2))
                    if not (last and unit >= NU - 2):
                        core.dve_max(dve, n + 2, (unit + 2) % NU)
                    if unit in (1, 4) and not (isinstance(g, int) and g >= GROUPS - 2):
                        split_low(g + 2, slot, unit // 4)

            loop_groups_but_two(dve, step)

        @block.tensor
        def _(pe):
            def project(g, slot, t):
                m = g * NU + t
                if isinstance(g, int) and g == 0:
                    pe.wait_ge(norm.copied_act, t + 1)
                    pe.wait_ge(norm.copied_dve, t + 1)
                    wait(pe, v_ready, m - 1)
                else:
                    pe.wait_ge(qkT_copied, m - 1)
                at, out = slice(t * P, (t + 1) * P), core.proj[:, t % 2, :]
                for k in range(KD):
                    if t == 0 and k % HALF_K == 0:
                        pe.wait_ge(w_split, g * 2 + k // HALF_K + 1)
                    pe.matmul(out, xnT[:, k, at], w_hi[:, slot, k, :], start=(k == 0), stop=False)
                    pe.matmul(out, xnT[:, k, at], w_lo[:, slot, k, :], start=False, stop=False)
                    last = pe.matmul(out, xnT_lo[:, k, at], w_hi[:, slot, k, :], start=False, stop=(k == KD - 1))
                last.then_inc(proj_done, 1)

            def turn(g, t, banks):
                m = g * NU + t
                pe.wait_ge(roped_ready, m + 1)
                if banks is first_turns:
                    wait(pe, qkT_copied, m - 1)
                else:
                    pe.wait_ge(v_ready, m + 1)
                for h in range(3):
                    last = pe.transpose(banks[:, t % 2, h * HD:(h + 1) * HD], normed[:, t % 2, h, :],
                                        shared.ident[:, :])
                last.then_inc(qkT_done, 1)

            def scores(g, slot, unit):
                tile, head = UNITS[unit]
                pe.wait_ge(qkT_copied, g * NU + (2 if tile < PROMPT_TILES else TILES))
                both = qkT[:, slot, :, :]
                core.pe_scores(pe, g * NU + unit, unit, both, both, head, 2)

            for i in range(TILES + 2):
                if i < TILES:
                    norm.pe_tile(pe, i, shared.ident[:, :])
                if 1 <= i <= TILES:
                    project(0, 0, i - 1)
                if i >= 3:
                    turn(0, i - 3, first_turns)
            pe.wait_ge(qkT_copied, TILES - 1)
            scores(0, 0, 0)
            scores(0, 0, 1)

            def step(g, slot, first, last):
                for unit in range(NU):
                    n = g * NU + unit
                    core.pe_turn(pe, n, unit, shared.ident[:, :])
                    if not last:
                        project(g + 1, 1 - slot, unit)
                    core.pe_pv(pe, n, unit, lambda t: V[:, slot, t, :])
                    if unit == 0:
                        turn(g, TILES - 1, core.proj)
                    elif not last:
                        turn(g + 1, unit - 1, core.proj)
                    if unit < NU - 2:
                        scores(g, slot, unit + 2)
                    elif not last:
                        scores(g + 1, 1 - slot, unit + 2 - NU)

            loop_groups(pe, step)
    s.end()


def output_block(nc, io, shared, layer):
    with ExitStack() as stack:
        s = Space(nc, stack, f"o{layer}_")
        o_dram, w_o = (io.o_a, shared.w_o_a) if layer == 0 else (io.o_b, shared.w_o_b)
        KO = o_dram.shape[1] // P
        HALVES = KO // KD
        o_in = s.sb("o_in", [P, 2, KO * P])
        oT = s.sb("oT", [P, 2, KO, P])
        x = s.sb("x", [P, 2, D])
        xn = s.sb("xn", [P, 2, D])
        xnT = s.sb("xnT", [P, KD, P])
        junk = s.sb("squares", [P, D])
        gain = s.sb("gain", [P, D])
        w_r = s.sb("w_router", [P, KD, EXPERTS])
        ssq, mean, rstd = s.sb("ssq", [P, TILES]), s.sb("mean", [P, TILES]), s.sb("rstd", [P, TILES])
        half = s.sb("minus_half", [P, 1])
        logits = s.sb("logits", [P, TILES, EXPERTS])
        top = s.sb("top", [P, TILES])
        shifted = s.sb("shifted", [P, TILES, EXPERTS])
        expd = s.sb("expd", [P, TILES, EXPERTS])
        total, inv = s.sb("total", [P, TILES]), s.sb("inv", [P, TILES])
        ROWS = 32 + EXPERTS
        aff = s.sb("aff", [P, TILES - PROMPT_TILES, ROWS])
        work = s.sb("work", [ROWS, SAMPLE])
        best = s.sb("best", [ROWS, CAP_S])
        best_at = s.sb("best_at", [ROWS, CAP_S], U32)
        chosen = s.sb("chosen", [EXPERTS, 2, CAP])
        oT_ps = s.psum("oT", [P, 2, 4, P])
        y_ps = s.psum("y", [P, 2, SAMPLE])
        xT_ps = s.psum("xT", [P, 2, 4, P])
        r_ps = s.psum("router", [P, TILES, EXPERTS])
        aT_ps = s.psum("affT", [ROWS, SAMPLE])

        o_landed = [s.sem("o_landed0"), s.sem("o_landed1")]
        x_landed = [s.sem("x_landed0"), s.sem("x_landed1")]
        small_landed = s.sem("small_landed")
        oT_done, oT_copied, y_done = s.sem("oT_done"), s.sem("oT_copied"), s.sem("y_done")
        x_ready, x_stored = s.sem("x_ready"), [s.sem("x_stored0"), s.sem("x_stored1")]
        ssq_ready, half_ready, mean_ready, rstd_ready = s.sem("ssq"), s.sem("half"), s.sem("mean"), s.sem("rstd")
        xn_ready, xn_stored = s.sem("xn_ready"), [s.sem("xn_stored0"), s.sem("xn_stored1")]
        xT_done, xT_copied, router_done, logits_ready = s.sem("xT_done"), s.sem("xT_copied"), s.sem("router_done"), s.sem("logits")
        chain, exp_ready, pad_ready, aff_ready = s.sem("softmax_steps"), s.sem("exp"), s.sem("pad"), s.sem("aff")
        affT_done, choice, chosen_ready, chosenT_done = s.sem("affT_done"), s.sem("choice"), s.sem("chosen"), s.sem("chosenT_done")
        block = stack.enter_context(nc.Block())

        def rows(dram, t):
            return dram.rearrange("(t p) n -> t p n", p=P)[bass.ds(t, 1)].rearrange("o p n -> (o p) n")

        @block.sync
        def _(sp):
            def load_o(t, slot):
                if t >= 2:
                    sp.wait_ge(oT_done, HALVES * (t - 1))
                sp.dma_start(o_in[:, slot, :], rows(o_dram, t)).then_inc(o_landed[slot], 16)

            def load_x(t, slot):
                if t >= 2:
                    sp.wait_ge(xn_ready, t - 1)
                    sp.wait_ge(ssq_ready, t - 1)
                    sp.wait_ge(x_stored[slot], 8 * (t - slot))
                src = token_rows(io.x_prompt, io.x_sample, t) if layer == 0 else rows(io.acc, t)
                sp.dma_start(x[:, slot, :], src).then_inc(x_landed[slot], 16)

            def store(t, slot):
                sp.wait_ge(x_ready, t + 1)
                sp.dma_start(rows(io.acc, t), x[:, slot, :]).then_inc(x_stored[slot], 16)
                sp.wait_ge(xn_ready, t + 1)
                sp.dma_start(rows(io.xn, t), xn[:, slot, :]).then_inc(xn_stored[slot], 16)

            load_o(0, 0)
            load_x(0, 0)
            load_o(1, 1)
            load_x(1, 1)
            sp.dma_start(gain[:, :], row_broadcast(io.g_ffn[layer])).then_inc(small_landed, 16)
            sp.dma_start(w_r[:, :, :], io.w_router[layer].rearrange("(k p) e -> p k e", p=P)).then_inc(small_landed, 16)
            for t in range(TILES):
                if t + 2 < TILES:
                    load_o(t + 2, t % 2)
                store(t, t % 2)
                if t + 2 < TILES:
                    load_x(t + 2, t % 2)
                    shared.load_first(sp, io.w_up, layer, 0, t)
                    if layer == 0:
                        shared.load_first(sp, io.w_gate, layer, 4, t)
            for j in range(4):
                if layer == 1:
                    shared.load_first(sp, io.w_gate, layer, 4, j)
            for j in range(4):
                shared.load_first(sp, io.w_down, layer, 8, j)
            for slot in range(2):
                sp.wait_ge(x_stored[slot], 16 * TILES // 2)
                sp.wait_ge(xn_stored[slot], 16 * TILES // 2)

        @block.gpsimd
        def _(pool):
            pool.memset(half[:, :], -0.5).then_inc(half_ready, 1)
            pool.memset(aff[:, :, :], -2.0).then_inc(pad_ready, 1)
            pool.wait_ge(half_ready, 1)
            for t in range(TILES):
                pool.wait_ge(ssq_ready, t + 1)
                pool.tensor_scalar(mean[:, t:t + 1], ssq[:, t:t + 1], 1.0 / D, EPS,
                                   ALU.mult, ALU.add).then_inc(mean_ready, 1)
                pool.wait_ge(mean_ready, t + 1)
                pool.tensor_tensor(rstd[:, t:t + 1], mean[:, t:t + 1], half[:, :], ALU.pow).then_inc(rstd_ready, 1)

        @block.scalar
        def _(act):
            def copy_oT(t, slot):
                for h in range(HALVES):
                    act.wait_ge(oT_done, HALVES * t + h + 1)
                    if not (isinstance(t, int) and t < 2):
                        act.wait_ge(y_done, t - 1)
                    act.activation(oT[:, slot, h * KD:(h + 1) * KD, :],
                                   oT_ps[:, :, :, :].rearrange("p b k n -> p (b k) n"), ACT.Copy).then_inc(oT_copied, 1)

            def square(t):
                act.wait_ge(x_ready, t + 1)
                wait(act, ssq_ready, t)
                act.activation(junk[:, :], x[:, t % 2, :], ACT.Square,
                               accum_out=ssq[:, t:t + 1]).then_inc(ssq_ready, 1)

            copy_oT(0, 0)
            for t in range(TILES):
                if t + 1 < TILES:
                    copy_oT(t + 1, (t + 1) % 2)
                square(t)
            act.wait_ge(chain, 2)
            act.activation(expd[:, :, :], shifted[:, :, :], ACT.Exp).then_inc(exp_ready, 1)

        @block.vector
        def _(dve):
            def copy_xT(t):
                dve.wait_ge(xT_done, t + 1)
                wait(dve, router_done, t)
                dve.tensor_copy(xnT[:, :, :], xT_ps[:, :, :, :].rearrange("p b k n -> p (b k) n")).then_inc(xT_copied, 1)

            for t in range(TILES):
                slot = t % 2
                dve.wait_ge(y_done, t + 1)
                dve.wait_ge(x_landed[slot], 16 * (t // 2 + 1))
                dve.tensor_tensor(x[:, slot, :], x[:, slot, :], y_ps[:, :, :].rearrange("p b n -> p (b n)"),
                                  ALU.add).then_inc(x_ready, 1)
                dve.wait_ge(x_ready, t + 1)
                dve.wait_ge(rstd_ready, t + 1)
                if t == 0:
                    dve.wait_ge(small_landed, 32)
                if t >= 2:
                    dve.wait_ge(xT_done, t - 1)
                    dve.wait_ge(xn_stored[slot], 16 * (t // 2))
                dve.scalar_tensor_tensor(out=xn[:, slot, :], in0=x[:, slot, :], scalar=rstd[:, t:t + 1],
                                         in1=gain[:, :], op0=ALU.mult, op1=ALU.mult).then_inc(xn_ready, 1)
                if t:
                    copy_xT(t - 1)
            copy_xT(TILES - 1)
            dve.wait_ge(router_done, TILES)
            dve.tensor_copy(logits[:, :, :], r_ps[:, :, :]).then_inc(logits_ready, 1)
            dve.wait_ge(logits_ready, 1)
            dve.tensor_reduce(top[:, :], logits[:, :, :], AX.X, ALU.max).then_inc(chain, 1)
            dve.wait_ge(chain, 1)
            dve.tensor_tensor(shifted[:, :, :], logits[:, :, :],
                              top[:, :].unsqueeze(2).to_broadcast([P, TILES, EXPERTS]), ALU.subtract).then_inc(chain, 1)
            dve.wait_ge(exp_ready, 1)
            dve.tensor_reduce(total[:, :], expd[:, :, :], AX.X, ALU.add).then_inc(chain, 1)
            dve.wait_ge(chain, 3)
            dve.reciprocal(inv[:, :], total[:, :]).then_inc(chain, 1)
            dve.wait_ge(chain, 4)
            dve.wait_ge(pad_ready, 1)
            dve.tensor_tensor(aff[:, 0:PROMPT_TILES, 0:EXPERTS], expd[:, 0:PROMPT_TILES, :],
                              inv[:, 0:PROMPT_TILES].unsqueeze(2).to_broadcast([P, PROMPT_TILES, EXPERTS]),
                              ALU.mult).then_inc(aff_ready, 1)
            dve.tensor_tensor(aff[:, :, 32:ROWS], expd[:, PROMPT_TILES:, :],
                              inv[:, PROMPT_TILES:].unsqueeze(2).to_broadcast([P, TILES - PROMPT_TILES, EXPERTS]),
                              ALU.mult).then_inc(aff_ready, 1)
            dve.wait_ge(affT_done, 1)
            dve.tensor_copy(work[:, :], aT_ps[:, :]).then_inc(choice, 1)
            for r in range(CAP_S // 8):
                rows_ = slice(0, ROWS) if r < CAP_P // 8 else slice(32, ROWS)
                at = slice(8 * r, 8 * r + 8)
                dve.wait_ge(choice, 3 * r + 1)
                dve.max(best[rows_, at], work[rows_, :]).then_inc(choice, 1)
                dve.wait_ge(choice, 3 * r + 2)
                dve.max_index(best_at[rows_, at], best[rows_, at], work[rows_, :]).then_inc(choice, 1)
                dve.wait_ge(choice, 3 * r + 3)
                dve.match_replace(work[rows_, :], best[rows_, at], work[rows_, :], -1.0).then_inc(choice, 1)
            dve.wait_ge(choice, 3 * (CAP_S // 8) + 1)
            dve.tensor_scalar(chosen[:, 0, 0:CAP_S], best_at[32:ROWS, :], float(PROMPT), None,
                              ALU.add).then_inc(chosen_ready, 1)
            dve.tensor_copy(chosen[:, 0, CAP_S:], best_at[0:EXPERTS, 0:CAP_P]).then_inc(chosen_ready, 1)
            dve.tensor_copy(chosen[:, 1, 0:CAP_S], best[32:ROWS, :]).then_inc(chosen_ready, 1)
            dve.tensor_copy(chosen[:, 1, CAP_S:], best[0:EXPERTS, 0:CAP_P]).then_inc(chosen_ready, 1)
            dve.wait_ge(chosenT_done, 1)
            dve.tensor_copy(shared.row_of[:, :], r_ps[0:CAP, 0, :]).then_inc(shared.lists_ready, 1)
            dve.tensor_copy(shared.gate_of[:, :], r_ps[0:CAP, 1, :]).then_inc(shared.lists_ready, 1)

        @block.tensor
        def _(pe):
            ident = shared.ident[:, :]
            pe.wait_ge(shared.w_o_landed, 16 * (layer + 1))

            def turn_o(t, slot):
                pe.wait_ge(o_landed[slot], 8 * (t - slot) + 16)
                for h in range(HALVES):
                    if not (isinstance(t, int) and t == 0 and h == 0):
                        pe.wait_ge(oT_copied, HALVES * t + h)
                    for k in range(KD):
                        last = pe.transpose(oT_ps[:, k // 4, k % 4, :],
                                            o_in[:, slot, (h * KD + k) * P:(h * KD + k + 1) * P], ident)
                    last.then_inc(oT_done, 1)

            def project(t, slot):
                pe.wait_ge(oT_copied, HALVES * (t + 1))
                if not (isinstance(t, int) and t == 0):
                    pe.wait_ge(x_ready, t)
                for half_ in range(2):
                    for k in range(KO):
                        last = pe.matmul(y_ps[:, half_, :], oT[:, slot, k, :],
                                         w_o[:, k, half_ * SAMPLE:(half_ + 1) * SAMPLE],
                                         start=(k == 0), stop=(k == KO - 1))
                last.then_inc(y_done, 1)

            def turn_x(t):
                pe.wait_ge(xn_ready, t + 1)
                wait(pe, xT_copied, t)
                for k in range(KD):
                    last = pe.transpose(xT_ps[:, k // 4, k % 4, :], xn[:, t % 2, k * P:(k + 1) * P], ident)
                last.then_inc(xT_done, 1)

            def route(t):
                if t == 0:
                    pe.wait_ge(small_landed, 32)
                pe.wait_ge(xT_copied, t + 1)
                for k in range(KD):
                    last = pe.matmul(r_ps[:, t, :], xnT[:, k, :], w_r[:, k, :], start=(k == 0), stop=(k == KD - 1))
                last.then_inc(router_done, 1)

            turn_o(0, 0)
            for t in range(TILES):
                if t + 1 < TILES:
                    turn_o(t + 1, (t + 1) % 2)
                project(t, t % 2)
                if t >= 2:
                    route(t - 2)
                if t >= 1:
                    turn_x(t - 1)
            route(TILES - 2)
            turn_x(TILES - 1)
            route(TILES - 1)
            pe.wait_ge(aff_ready, 2)
            for t in range(TILES - PROMPT_TILES):
                last = pe.transpose(aT_ps[:, t * P:(t + 1) * P], aff[:, t, :], ident)
            last.then_inc(affT_done, 1)
            pe.wait_ge(chosen_ready, 4)
            pe.wait_ge(logits_ready, 1)
            for what in range(2):
                last = pe.transpose(r_ps[0:CAP, what, :], chosen[:, what, :], shared.ident[0:EXPERTS, 0:EXPERTS])
            last.then_inc(chosenT_done, 1)
    s.end()


def moe_block(nc, io, shared, layer):
    with ExitStack() as stack:
        s = Space(nc, stack, f"m{layer}_")
        raw = shared.raw
        hi = s.sb("w_hi", [P, SPLITS, 2, D], F32R)
        lo = s.sb("w_lo", [P, SPLITS, 2, D], F32R)
        xe = s.sb("xe", [CAP, D])
        xeT_hi = s.sb("xeT_hi", [P, 2, KD, CAP], F32R)
        xeT_lo = s.sb("xeT_lo", [P, 2, KD, CAP], F32R)
        silu = s.sb("silu", [CAP, FF])
        hid = s.sb("hid", [CAP, FF])
        hidT_hi = s.sb("hidT_hi", [P, KD, CAP], F32R)
        hidT_lo = s.sb("hidT_lo", [P, KD, CAP], F32R)
        ye = s.sb("ye", [CAP, D])
        row_gather = s.sb("row_gather", [CAP, 1], U32)
        row_scatter = s.sb("row_scatter", [CAP, 1], U32)
        gate_ps = s.psum("gate", [CAP, FF])
        up_ps = s.psum("up", [CAP, FF])
        down_ps = s.psum("down", [CAP, D])
        T_ps = s.psum("turned", [P, KD, P])

        hi_ready, lo_ready, split_used = s.sem("hi_ready"), s.sem("lo_ready"), s.sem("split_used")
        first_rows_ready, rows_ready, gathered = s.sem("first_rows_ready"), s.sem("rows_ready"), s.sem("gathered")
        scatter_rows_ready, scattered = s.sem("scatter_rows_ready"), s.sem("scattered")
        T_done, T_hi, T_lo = s.sem("T_done"), s.sem("T_hi"), s.sem("T_lo")
        silu_ready, hid_ready, ye_ready = s.sem("silu_ready"), s.sem("hid_ready"), s.sem("ye_ready")
        block = stack.enter_context(nc.Block())

        LAST = EXPERTS - 1

        def loop_experts(engine, step):
            step(0, 0)
            with engine.Fori(0, (EXPERTS - 2) // 2) as i:
                step(i * 2 + 1, 1)
                step(i * 2 + 2, 0)
            step(LAST, 1)

        def is_last(e):
            return isinstance(e, int) and e == LAST

        def pieces(e):
            slots = [0, 1, 2, 3, 8, 9, 10, 11] if is_last(e) else list(range(SLOTS))
            return list(enumerate(slots))

        def q_of(e, place):
            return e * SLOTS + 4 + place

        def wait_low(engine, e, place):
            engine.wait_ge(lo_ready, q_of(e, place) + 1)

        @block.sync
        def _(sp):
            def load(e, matrix, j, first_slot):
                src = matrix[layer].rearrange("e (c k p) n -> e c p k n", c=4, p=P)[bass.ds(e, 1), j]
                sp.dma_start(raw[:, first_slot + j, :].rearrange("p (k n) -> p k n", k=2),
                             src.rearrange("e p k n -> (e p) k n")).then_inc(shared.landed[first_slot + j], 16)

            for j in range(4):
                sp.wait_ge(lo_ready, j + 1)
                load(1, io.w_gate, j, 4)

            def step(e):
                for j in range(4):
                    wait_low(sp, e - 1, j)
                    load(e, io.w_up, j, 0)
                if not is_last(e):
                    for j in range(4):
                        wait_low(sp, e - 1, 4 + j)
                        load(e + 1, io.w_gate, j, 4)
                for j in range(4):
                    wait_low(sp, e - 1, 8 + j)
                    load(e, io.w_down, j, 8)

            with sp.Fori(1, LAST) as e:
                step(e)
            step(LAST)

        @block.gpsimd
        def _(pool):
            def gather(e, rows_ready, count):
                wait(pool, gathered, e * 16)
                wait(pool, T_done, e if isinstance(e, int) and e < 2 else e * 2 - 2)
                pool.tensor_copy(row_gather[:, :], shared.row_of[:, bass.ds(e, 1)]).then_inc(rows_ready, 1)
                pool.wait_ge(shared.lists_ready, 2 * layer + 2)
                pool.wait_ge(rows_ready, count)
                pool.indirect_dma_start(out=xe[:, :], out_offset=None, in_=io.xn,
                                        in_offset=bass.IndirectOffsetOnAxis(ap=row_gather[:, :], axis=0)
                                        ).then_inc(gathered, 16)

            def scatter(e):
                wait(pool, scattered, e * 16)
                pool.tensor_copy(row_scatter[:, :], shared.row_of[:, bass.ds(e, 1)]).then_inc(scatter_rows_ready, 1)
                pool.wait_ge(shared.lists_ready, 2 * layer + 2)
                pool.wait_ge(scatter_rows_ready, e + 1)
                pool.wait_ge(ye_ready, e + 1)
                pool.indirect_dma_start(out=io.acc, out_offset=bass.IndirectOffsetOnAxis(ap=row_scatter[:, :], axis=0),
                                        in_=ye[:, :], in_offset=None, compute_op=ALU.add).then_inc(scattered, 16)

            def step(e, ahead):
                if not (isinstance(e, int) and e == 0):
                    scatter(e - 1)
                if ahead:
                    if isinstance(e, int):
                        gather(e + 2, first_rows_ready, e + 3)
                    else:
                        gather(e + 2, rows_ready, e)

            gather(0, first_rows_ready, 1)
            gather(1, first_rows_ready, 2)
            step(0, True)
            with pool.Fori(1, LAST - 1) as e:
                step(e, True)
            step(LAST - 1, False)
            step(LAST, False)
            scatter(LAST)
            pool.wait_ge(scattered, 16 * EXPERTS)

        @block.scalar
        def _(act):
            def high(q, split, slot, landed):
                act.wait_ge(shared.landed[slot], landed)
                wait(act, split_used, q + 1 - SPLITS)
                act.activation(hi[:, split, :, :].rearrange("p k n -> p (k n)"), raw[:, slot, :],
                               ACT.Copy).then_inc(hi_ready, 1)

            def turned(dst, n):
                act.wait_ge(T_done, n)
                act.activation(dst, T_ps[:, :, 0:CAP], ACT.Copy).then_inc(T_hi, 1)

            def gate_out(e, done):
                act.wait_ge(split_used, done)
                wait(act, hid_ready, e)
                act.activation(silu[:, :], gate_ps[:, :], ACT.Silu).then_inc(silu_ready, 1)

            def down_out(e, done):
                act.wait_ge(split_used, done)
                wait(act, scattered, e * 16)
                act.activation(ye[:, :], down_ps[:, :], ACT.Copy,
                               scale=shared.gate_of[:, bass.ds(e, 1)]).then_inc(ye_ready, 1)

            base = 16 * layer * EXPERTS
            turned(xeT_hi[:, 0, :, :], 1)
            for j in range(4):
                high(j, j % SPLITS, 4 + j, base + 16)

            def step(e, parity):
                for place, slot in pieces(e):
                    ahead = 1 if 4 <= slot < 8 else 0
                    high(q_of(e, place), (4 + place) % SPLITS, slot, (e + ahead) * 16 + base + 16)
                    if place == 2:
                        if isinstance(e, int) and e == 0:
                            gate_out(0, 4)
                    if place == 3 and not is_last(e):
                        turned(xeT_hi[:, 1 - parity, :, :], e * 2 + 2)
                    if place == 3 and not (isinstance(e, int) and e == 0):
                        down_out(e - 1, q_of(e, 0))
                    if place == (5 if is_last(e) else 8):
                        turned(hidT_hi[:, :, :], e * 2 + (2 if is_last(e) else 3))
                    if place == 10:
                        gate_out(e + 1, q_of(e, 8))
                if is_last(e):
                    down_out(e, q_of(e, 8))

            loop_experts(act, step)

        @block.vector
        def _(dve):
            def low(q, split, slot):
                dve.wait_ge(hi_ready, q + 1)
                wait(dve, split_used, q + 1 - SPLITS)
                dve.tensor_tensor(lo[:, split, :, :].rearrange("p k n -> p (k n)"), raw[:, slot, :],
                                  hi[:, split, :, :].rearrange("p k n -> p (k n)"),
                                  ALU.subtract).then_inc(lo_ready, 1)

            def turned(dst, high_part, n):
                dve.wait_ge(T_hi, n)
                dve.tensor_tensor(dst, T_ps[:, :, 0:CAP], high_part, ALU.subtract).then_inc(T_lo, 1)

            turned(xeT_lo[:, 0, :, :], xeT_hi[:, 0, :, :], 1)
            for j in range(4):
                low(j, j % SPLITS, 4 + j)

            def step(e, parity):
                for place, slot in pieces(e):
                    low(q_of(e, place), (4 + place) % SPLITS, slot)
                    if place == 3 and not is_last(e):
                        turned(xeT_lo[:, 1 - parity, :, :], xeT_hi[:, 1 - parity, :, :], e * 2 + 2)
                    if place == 5:
                        dve.wait_ge(silu_ready, e + 1)
                        dve.wait_ge(split_used, q_of(e, 4))
                        wait(dve, T_done, 2 * e + 1)
                        dve.tensor_tensor(hid[:, :], silu[:, :], up_ps[:, :], ALU.mult).then_inc(hid_ready, 1)
                    if place == (5 if is_last(e) else 8):
                        turned(hidT_lo[:, :, :], hidT_hi[:, :, :], e * 2 + (2 if is_last(e) else 3))

            loop_experts(dve, step)

        @block.tensor
        def _(pe):
            def turn(src, n):
                wait(pe, T_lo, n)
                for k in range(KD):
                    last = pe.transpose(T_ps[:, k, 0:CAP], src[:, k * P:(k + 1) * P], shared.ident[0:CAP, 0:CAP])
                last.then_inc(T_done, 1)

            def products(out, left_hi, left_lo, j, split, q):
                for half in range(2):
                    cols = slice(half * SAMPLE, (half + 1) * SAMPLE)
                    for kk in range(2):
                        k = 2 * j + kk
                        pe.matmul(out[:, cols], left_hi[:, k, :], hi[:, split, kk, cols], start=(k == 0), stop=False)
                        pe.matmul(out[:, cols], left_hi[:, k, :], lo[:, split, kk, cols], start=False, stop=False)
                        last = pe.matmul(out[:, cols], left_lo[:, k, :], hi[:, split, kk, cols], start=False,
                                         stop=(k == KD - 1))
                last.then_inc(split_used, 1)

            pe.wait_ge(gathered, 16)
            turn(xe, 0)
            pe.wait_ge(T_lo, 1)
            for j in range(4):
                pe.wait_ge(lo_ready, j + 1)
                products(gate_ps, xeT_hi[:, 0], xeT_lo[:, 0], j, j % SPLITS, j)

            def step(e, parity):
                for place, slot in pieces(e):
                    split = (4 + place) % SPLITS
                    if slot == 0:
                        wait(pe, hid_ready, e)
                    if slot == 4:
                        pe.wait_ge(silu_ready, e + 1)
                        pe.wait_ge(T_lo, e * 2 + 2)
                    if slot == 8:
                        if not (isinstance(e, int) and e == 0):
                            pe.wait_ge(ye_ready, e)
                        if is_last(e):
                            pe.wait_ge(hid_ready, e + 1)
                            turn(hid, e * 2 + 1)
                        pe.wait_ge(T_lo, e * 2 + (2 if is_last(e) else 3))
                    if slot == 1 and not is_last(e):
                        pe.wait_ge(gathered, e * 16 + 32)
                        turn(xe, e * 2 + 1)
                    if slot == 6:
                        pe.wait_ge(hid_ready, e + 1)
                        turn(hid, e * 2 + 2)
                    wait_low(pe, e, place)
                    q = q_of(e, place)
                    if slot < 4:
                        products(up_ps, xeT_hi[:, parity], xeT_lo[:, parity], slot, split, q)
                    elif slot < 8:
                        products(gate_ps, xeT_hi[:, 1 - parity], xeT_lo[:, 1 - parity], slot - 4, split, q)
                    else:
                        products(down_ps, hidT_hi, hidT_lo, slot - 8, split, q)

            loop_experts(pe, step)
    s.end()


def final_block(nc, io, shared):
    with ExitStack() as stack:
        s = Space(nc, stack, "f_")
        x = s.sb("x", [P, TILES, D])
        y = s.sb("y", [P, TILES, D])
        gain = s.sb("gain", [P, D])
        ssq, mean, rstd = s.sb("ssq", [P, TILES]), s.sb("mean", [P, TILES]), s.sb("rstd", [P, TILES])
        half = s.sb("minus_half", [P, 1])
        gain_landed, x_landed = s.sem("gain_landed"), [s.sem(f"x_landed{t}") for t in range(TILES)]
        half_ready, ssq_ready, mean_ready = s.sem("half_ready"), s.sem("ssq_ready"), s.sem("mean_ready")
        rstd_ready, y_ready, stored = s.sem("rstd_ready"), s.sem("y_ready"), s.sem("stored")
        block = stack.enter_context(nc.Block())

        @block.sync
        def _(sp):
            sp.dma_start(gain[:, :], row_broadcast(io.g_final)).then_inc(gain_landed, 16)
            for t in range(TILES):
                sp.dma_start(x[:, t, :], io.acc[t * P:(t + 1) * P, :]).then_inc(x_landed[t], 16)
            for t in range(TILES):
                sp.wait_ge(y_ready, t + 1)
                sp.dma_start(token_rows(io.y_prompt, io.y_sample, t), y[:, t, :]).then_inc(stored, 16)
            sp.wait_ge(stored, 16 * TILES)

        @block.scalar
        def _(act):
            for t in range(TILES):
                act.wait_ge(x_landed[t], 16)
                act.activation(y[:, t, :], x[:, t, :], ACT.Square, accum_out=ssq[:, t:t + 1]).then_inc(ssq_ready, 1)

        @block.gpsimd
        def _(pool):
            pool.memset(half[:, :], -0.5).then_inc(half_ready, 1)
            pool.wait_ge(half_ready, 1)
            for t in range(TILES):
                pool.wait_ge(ssq_ready, t + 1)
                pool.tensor_scalar(mean[:, t:t + 1], ssq[:, t:t + 1], 1.0 / D, EPS,
                                   ALU.mult, ALU.add).then_inc(mean_ready, 1)
                pool.wait_ge(mean_ready, t + 1)
                pool.tensor_tensor(rstd[:, t:t + 1], mean[:, t:t + 1], half[:, :], ALU.pow).then_inc(rstd_ready, 1)

        @block.vector
        def _(dve):
            dve.wait_ge(gain_landed, 16)
            for t in range(TILES):
                dve.wait_ge(rstd_ready, t + 1)
                dve.scalar_tensor_tensor(out=y[:, t, :], in0=x[:, t, :], scalar=rstd[:, t:t + 1], in1=gain[:, :],
                                         op0=ALU.mult, op1=ALU.mult).then_inc(y_ready, 1)
    s.end()


class Tensors:

    def __init__(self, t):
        self.x_prompt, self.x_sample, self.g_attn_a = t["x_prompt"], t["x_sample"], t["g_attn_a"]
        self.w_in_a, self.g_q_a, self.w_uq_a = t["w_in_a"], t["g_q_a"], t["w_uq_a"]
        self.g_kv_a, self.w_ukv_a, self.w_o_a = t["g_kv_a"], t["w_ukv_a"], t["w_o_a"]
        self.g_attn_b, self.w_qkv_b, self.g_qn_b = t["g_attn_b"], t["w_qkv_b"], t["g_qn_b"]
        self.g_kn_b, self.w_o_b, self.g_ffn = t["g_kn_b"], t["w_o_b"], t["g_ffn"]
        self.w_router, self.w_gate, self.w_up = t["w_router"], t["w_gate"], t["w_up"]
        self.w_down, self.g_final, self.rope_a_tok = t["w_down"], t["g_final"], t["rope_a_tok"]
        self.rope_a_T, self.rope_b, self.ident = t["rope_a_T"], t["rope_b"], t["ident"]
        self.y_prompt, self.y_sample, self.acc = t["y_prompt"], t["y_sample"], t["acc"]
        self.xn, self.o_a, self.o_b = t["xn"], t["o_a"], t["o_b"]


class Shared:

    def __init__(self, nc, stack, io):
        s = Space(nc, stack, "s_")
        self.io = io
        self.raw = s.sb("raw", [P, SLOTS, SLOT])
        self.raw_at = nc.sbuf_base - SLOTS * SLOT * 4
        self.ident = s.sb("ident", [P, P])
        self.row_of = s.sb("row_of", [CAP, EXPERTS], U32)
        self.gate_of = s.sb("gate_of", [CAP, EXPERTS])
        self.ident_landed = s.sem("ident_landed")
        self.w_o_landed = s.sem("w_o_landed")
        self.lists_ready = s.sem("lists_ready")
        self.landed = [s.sem(f"landed{j}") for j in range(SLOTS)]
        arena = self.raw.rearrange("p s n -> p (s n)")
        self.w_o_a = arena[:, (SLOTS - 4) * SLOT:].rearrange("p (k n) -> p k n", n=D)
        self.w_o_b = arena[:, (SLOTS - 8) * SLOT:].rearrange("p (k n) -> p k n", n=D)

    def over_raw(self, nc, name, shape, first_slot):
        return nc.alloc_sbuf_tensor_at(name, shape, F32R, offset=self.raw_at + first_slot * SLOT * 4)

    def load_first(self, sp, matrix, layer, first_slot, j):
        src = matrix[layer, 0].rearrange("(c k p) n -> c p k n", c=4, p=P)
        sp.dma_start(self.raw[:, first_slot + j, :].rearrange("p (k n) -> p k n", k=2),
                     src[j]).then_inc(self.landed[first_slot + j], 16)


def build(nc, io):
    with ExitStack() as stack:
        shared = Shared(nc, stack, io)
        mla_block(nc, io, shared)
        output_block(nc, io, shared, 0)
        moe_block(nc, io, shared, 0)
        gqa_block(nc, io, shared)
        output_block(nc, io, shared, 1)
        moe_block(nc, io, shared, 1)
        final_block(nc, io, shared)


def rope_constants():
    def angles(positions, d):
        inv = np.float32(THETA) ** -(np.arange(d // 2, dtype=np.float32) * np.float32(2.0) / np.float32(d))
        a = positions.astype(np.float32)[:, None] * inv[None, :].astype(np.float32)
        c, s = np.cos(a).astype(np.float32), np.sin(a).astype(np.float32)
        return np.concatenate([c, c], 1), np.concatenate([-s, s], 1)

    pos = np.concatenate([np.arange(PROMPT), np.arange(SAMPLE)])
    ca, sa = angles(pos, DR)
    tok = np.stack([ca, sa], 1).reshape(TILES, P, 2, DR).transpose(1, 0, 2, 3)
    turned = np.concatenate([ca.T, sa.T], 0)
    cr, sr = angles(pos // GRID_W, HD // 2)
    cc, sc = angles(pos % GRID_W, HD // 2)
    b = np.stack([np.concatenate([cr, cc], 1), np.concatenate([sr, sc], 1)], 1)
    b = b.reshape(TILES, P, 2, HD).transpose(1, 0, 2, 3)
    return {"rope_a_tok": np.ascontiguousarray(tok), "rope_a_T": np.ascontiguousarray(turned),
            "rope_b": np.ascontiguousarray(b), "ident": np.eye(P, dtype=np.float32)}


INPUTS = ["x_prompt", "x_sample", "g_attn_a", "w_in_a", "g_q_a", "w_uq_a", "g_kv_a", "w_ukv_a", "w_o_a",
          "g_attn_b", "w_qkv_b", "g_qn_b", "g_kn_b", "w_o_b", "g_ffn", "w_router", "w_gate", "w_up",
          "w_down", "g_final"]


def kernel(**inputs):
    import concourse.bacc as bacc
    from concourse.bass_utils import run_bass_kernel_spmd

    nc = bacc.Bacc("TRN2", target_bir_lowering=False, num_devices=1)
    arrays, io = {}, {}
    host = {name: np.ascontiguousarray(inputs[name]) for name in INPUTS} | rope_constants()
    for name, a in host.items():
        arrays[f"in_{name}"] = a
        io[name] = nc.dram_tensor(f"in_{name}", a.shape, mybir.dt.from_np(a.dtype), kind="ExternalInput").ap()
    for name, rows in (("y_prompt", PROMPT), ("y_sample", SAMPLE)):
        io[name] = nc.dram_tensor(f"out_{name}", (1, rows, D), F32, kind="ExternalOutput").ap()
    io["acc"] = nc.dram_tensor("acc", (N, D), F32, kind="Internal").ap()
    io["xn"] = nc.dram_tensor("xn", (N, D), F32, kind="Internal").ap()
    io["o_a"] = nc.dram_tensor("o_a", (N, HEADS * DV), F32, kind="Internal").ap()
    io["o_b"] = nc.dram_tensor("o_b", (N, HEADS * HD), F32, kind="Internal").ap()
    build(nc, Tensors(io))
    r = run_bass_kernel_spmd(nc, [arrays], core_ids=[0])
    return r.results[0]["out_y_prompt"], r.results[0]["out_y_sample"]
```

```python
from contextlib import ExitStack

import numpy as np

import concourse.bass as bass
from concourse import mybir

F32 = mybir.dt.float32
F32R = mybir.dt.float32r
U32 = mybir.dt.uint32
ALU = mybir.AluOpType
ACT = mybir.ActivationFunctionType
AX = mybir.AxisListType

P = 128
D = 1024
KD = D // P
PROMPT, SAMPLE = 256, 512
N = PROMPT + SAMPLE
TILES = N // P
PROMPT_TILES = PROMPT // P
EPS = 1e-6

HEADS = 16
GROUPS = HEADS // 2
Q_LORA, KV_LORA, DN, DR, DV = 384, 256, 64, 32, 64
KQ, KKV = Q_LORA // P, KV_LORA // P
W_IN = Q_LORA + KV_LORA + DR
ARENA_FREE_A = KD * W_IN + KQ * HEADS * (DN + DR) + KKV * HEADS * (DN + DV)
HD = 128
KV_HEADS = 8
THETA = 10000.0
GRID_W = 64

EXPERTS = 16
FF = 1024
CAP_P = 2 * PROMPT // EXPERTS
CAP_S = 2 * SAMPLE // EXPERTS
CAP = CAP_P + CAP_S

UNITS = [(0, 0), (0, 1), (2, 0), (4, 0), (2, 1), (4, 1)]
NU = len(UNITS)

SLOTS = 12
SLOT = 2 * D
SPLITS = 4


def keys_of(unit):
    return (0, PROMPT_TILES) if UNITS[unit][0] < PROMPT_TILES else (PROMPT_TILES, TILES - PROMPT_TILES)


def wait(engine, semaphore, count):
    if isinstance(count, int) and count <= 0:
        return
    engine.wait_ge(semaphore, count)


class Space:

    def __init__(self, nc, stack, prefix):
        self.nc, self.stack, self.prefix, self.sems = nc, stack, prefix, []

    def sb(self, name, shape, dtype=F32):
        return self.stack.enter_context(self.nc.sbuf_tensor(self.prefix + name, shape, dtype))

    def psum(self, name, shape, dtype=F32):
        return self.stack.enter_context(self.nc.psum_tensor(self.prefix + "ps_" + name, shape, dtype))

    def sem(self, name):
        self.sems.append(self.nc.alloc_semaphore(self.prefix + name))
        return self.sems[-1]

    def end(self):
        self.nc.clear_and_free_semaphores(self.sems)
        self.nc.all_engine_barrier()


def token_rows(x_prompt, x_sample, t):
    if t < PROMPT_TILES:
        return x_prompt[0, t * P:(t + 1) * P, :]
    return x_sample[0, (t - PROMPT_TILES) * P:(t - PROMPT_TILES + 1) * P, :]


def row_broadcast(vector):
    return vector.partition_broadcast(P)



class InputNorm:

    def __init__(self, s, x_tile_of, gain_row, xnT, psum, x, xn, junk, gain, xnT_lo=None):
        self.x_tile_of, self.gain_row, self.xnT, self.ps = x_tile_of, gain_row, xnT, psum
        self.xnT_lo = xnT_lo
        self.x, self.xn, self.junk, self.gain = x, xn, junk, gain
        self.ssq = s.sb("norm_ssq", [P, TILES])
        self.mean = self.ssq
        self.rstd = s.sb("norm_rstd", [P, TILES])
        self.x_landed = [s.sem("norm_x_landed0"), s.sem("norm_x_landed1")]
        self.gain_landed = s.sem("norm_gain_landed")
        self.ssq_ready = s.sem("norm_ssq_ready")
        self.mean_ready = s.sem("norm_mean_ready")
        self.rstd_ready = s.sem("norm_rstd_ready")
        self.xn_ready = s.sem("norm_xn_ready")
        self.turned = s.sem("norm_turned")
        self.copied_act = s.sem("norm_copied_act")
        self.copied_dve = s.sem("norm_copied_dve")

    def act_tile(self, act, t):
        act.wait_ge(self.x_landed[t % 2], 16 * (t // 2 + 1))
        wait(act, self.ssq_ready, t)
        act.activation(self.junk, self.x[:, t % 2, :], ACT.Square,
                       accum_out=self.ssq[:, t:t + 1]).then_inc(self.ssq_ready, 1)

    def act_copy(self, act, t):
        act.wait_ge(self.turned, t + 1)
        if self.xnT_lo is None:
            act.activation(self.xnT[:, 0:KD // 2, t * P:(t + 1) * P], self.ps[:, 0, :, :],
                           ACT.Copy).then_inc(self.copied_act, 1)
        else:
            act.activation(self.xnT[:, :, t * P:(t + 1) * P], self.ps[:, :, :, :].rearrange("p b k n -> p (b k) n"),
                           ACT.Copy).then_inc(self.copied_act, 1)

    def pool_tile(self, pool, t, half):
        pool.wait_ge(self.ssq_ready, t + 1)
        pool.tensor_scalar(self.mean[:, t:t + 1], self.ssq[:, t:t + 1], 1.0 / D, EPS,
                           ALU.mult, ALU.add).then_inc(self.mean_ready, 1)
        pool.wait_ge(self.mean_ready, t + 1)
        pool.tensor_tensor(self.rstd[:, t:t + 1], self.mean[:, t:t + 1], half,
                           ALU.pow).then_inc(self.rstd_ready, 1)

    def dve_tile(self, dve, t):
        if t == 0:
            dve.wait_ge(self.gain_landed, 16)
        dve.wait_ge(self.x_landed[t % 2], 16 * (t // 2 + 1))
        dve.wait_ge(self.rstd_ready, t + 1)
        wait(dve, self.turned, t - 1)
        dve.scalar_tensor_tensor(out=self.xn[:, t % 2, :], in0=self.x[:, t % 2, :],
                                 scalar=self.rstd[:, t:t + 1], in1=self.gain,
                                 op0=ALU.mult, op1=ALU.mult).then_inc(self.xn_ready, 1)

    def dve_copy(self, dve, t):
        if self.xnT_lo is None:
            dve.wait_ge(self.turned, t + 1)
            dve.tensor_copy(self.xnT[:, KD // 2:KD, t * P:(t + 1) * P],
                            self.ps[:, 1, :, :]).then_inc(self.copied_dve, 1)
        else:
            dve.wait_ge(self.copied_act, t + 1)
            at = slice(t * P, (t + 1) * P)
            dve.tensor_tensor(self.xnT_lo[:, :, at], self.ps[:, :, :, :].rearrange("p b k n -> p (b k) n"),
                              self.xnT[:, :, at], ALU.subtract).then_inc(self.copied_dve, 1)

    def pe_tile(self, pe, t, ident):
        pe.wait_ge(self.xn_ready, t + 1)
        wait(pe, self.copied_act, t)
        wait(pe, self.copied_dve, t)
        for k in range(KD):
            last = pe.transpose(self.ps[:, k // 4, k % 4, :], self.xn[:, t % 2, k * P:(k + 1) * P], ident)
        last.then_inc(self.turned, 1)



class Core:

    def __init__(self, s, dk, dv, scale, o_dram, probs, probsT, out):
        self.dk, self.dv, self.scale, self.o_dram = dk, dv, scale, o_dram
        self.S = s.psum("scores", [P, 2, 2, SAMPLE])
        self.T = s.psum("probsT", [P, 2, 4, P])
        self.proj = s.psum("projected", [P, 2, SAMPLE])
        self.probs = probs
        self.probsT = probsT
        self.out = out
        self.rowmax = s.sb("rowmax", [P, 2, 2])
        self.negmax = s.sb("negmax", [P, 2, 2])
        self.rowsum = s.sb("rowsum", [P, 2, 2])
        self.rinv = s.sb("rinv", [P, 2, 2])
        self.scores_done = s.sem("scores_done")
        self.rowmax_done = s.sem("rowmax_done")
        self.negmax_done = s.sem("negmax_done")
        self.exp_done = s.sem("exp_done")
        self.turned = s.sem("probs_turned")
        self.copied_act = s.sem("probs_copied_act")
        self.copied_dve = s.sem("probs_copied_dve")
        self.rinv_done = s.sem("rinv_done")
        self.pv_done = s.sem("pv_done")
        self.out_done = s.sem("out_done")
        self.stored = [s.sem("stored0"), s.sem("stored1")]


    def pe_scores(self, pe, n, unit, qT, kT, q_index, k_index):
        wait(pe, self.exp_done, 2 * n - 2)
        key, nk = keys_of(unit)
        tile, _ = UNITS[unit]
        for j in range(2):
            last = pe.matmul(self.S[:, unit % 2, j, 0:nk * P],
                             qT[0:self.dk, q_index, (tile + j) * P:(tile + j + 1) * P],
                             kT[0:self.dk, k_index, key * P:(key + nk) * P], start=True, stop=True)
        last.then_inc(self.scores_done, 1)

    def pe_scores_of_parts(self, pe, n, unit, high, low, q_index, k_index):
        wait(pe, self.exp_done, 2 * n - 2)
        key, nk = keys_of(unit)
        tile, _ = UNITS[unit]
        keys = slice(key * P, (key + nk) * P)
        for j in range(2):
            queries, out = slice((tile + j) * P, (tile + j + 1) * P), self.S[:, unit % 2, j, 0:nk * P]
            pe.matmul(out, high[0:self.dk, q_index, queries], high[0:self.dk, k_index, keys], start=True, stop=False)
            pe.matmul(out, high[0:self.dk, q_index, queries], low[0:self.dk, k_index, keys], start=False, stop=False)
            last = pe.matmul(out, low[0:self.dk, q_index, queries], high[0:self.dk, k_index, keys],
                             start=False, stop=True)
        last.then_inc(self.scores_done, 1)

    def pe_turn(self, pe, n, unit, ident):
        _, nk = keys_of(unit)
        for j in range(2):
            pe.wait_ge(self.exp_done, 2 * n + j + 1)
            wait(pe, self.out_done, 2 * n - 1 + j)
            for k in range(nk):
                last = pe.transpose(self.T[:, j, k, :], self.probs[:, unit % 2, j, k * P:(k + 1) * P], ident)
            last.then_inc(self.turned, 1)

    def pe_pv(self, pe, n, unit, v_of):
        key, nk = keys_of(unit)
        for j in range(2):
            pe.wait_ge(self.copied_act if j == 0 else self.copied_dve, n + 1)
            for k in range(nk):
                last = pe.matmul(self.T[:, j, 0, 0:self.dv], self.probsT[:, j, k, :], v_of(key + k),
                                 start=(k == 0), stop=(k == nk - 1))
            last.then_inc(self.pv_done, 1)


    def act_exp(self, act, n, unit):
        _, nk = keys_of(unit)
        act.wait_ge(self.negmax_done, n + 1)
        wait(act, self.turned, 2 * n - 2)
        wait(act, self.rinv_done, n - 1)
        for j in range(2):
            act.activation(self.probs[:, unit % 2, j, 0:nk * P], self.S[:, unit % 2, j, 0:nk * P], ACT.Exp,
                           bias=self.negmax[:, unit % 2, j:j + 1], scale=self.scale,
                           accum_out=self.rowsum[:, unit % 2, j:j + 1]).then_inc(self.exp_done, 1)

    def act_copy(self, act, n, unit):
        _, nk = keys_of(unit)
        act.wait_ge(self.turned, 2 * n + 1)
        wait(act, self.pv_done, 2 * n - 1)
        act.activation(self.probsT[:, 0, 0:nk, :], self.T[:, 0, 0:nk, :], ACT.Copy).then_inc(self.copied_act, 1)


    def dve_max(self, dve, n, unit):
        _, nk = keys_of(unit)
        dve.wait_ge(self.scores_done, n + 1)
        wait(dve, self.negmax_done, n)
        dve.tensor_reduce(self.rowmax[:, unit % 2, :], self.S[:, unit % 2, :, 0:nk * P], AX.X,
                          ALU.max).then_inc(self.rowmax_done, 1)
        dve.wait_ge(self.rowmax_done, n + 1)
        wait(dve, self.exp_done, 2 * n - 2)
        dve.tensor_scalar(self.negmax[:, unit % 2, :], self.rowmax[:, unit % 2, :], -self.scale, None,
                          ALU.mult).then_inc(self.negmax_done, 1)

    def dve_copy(self, dve, n, unit):
        _, nk = keys_of(unit)
        dve.wait_ge(self.turned, 2 * n + 2)
        wait(dve, self.pv_done, 2 * n)
        dve.tensor_copy(self.probsT[:, 1, 0:nk, :], self.T[:, 1, 0:nk, :]).then_inc(self.copied_dve, 1)

    def dve_rinv(self, dve, n, unit):
        dve.wait_ge(self.exp_done, 2 * n + 2)
        wait(dve, self.out_done, 2 * n)
        dve.reciprocal(self.rinv[:, unit % 2, :], self.rowsum[:, unit % 2, :]).then_inc(self.rinv_done, 1)

    def dve_out(self, dve, g, n, unit, slot, first):
        tile, head = UNITS[unit]
        dve.wait_ge(self.rinv_done, n + 1)
        for j in range(2):
            dve.wait_ge(self.pv_done, 2 * n + j + 1)
            if unit == 0 and j == 0 and not first:
                self.wait_stored(dve, g, slot)
            dve.tensor_scalar(self.out[:, slot, tile + j, head * self.dv:(head + 1) * self.dv],
                              self.T[:, j, 0, 0:self.dv], self.rinv[:, unit % 2, j:j + 1], None,
                              ALU.mult).then_inc(self.out_done, 1)

    def wait_stored(self, dve, g, slot):
        dve.wait_ge(self.stored[slot], 8 * (g - slot))


    def store(self, sp, g, slot):
        sp.wait_ge(self.out_done, 2 * NU * g + 2 * NU)
        sp.dma_start(self.o_dram[:, :, bass.ds(g * 2 * self.dv, 2 * self.dv)],
                     self.out[:, slot, :, :]).then_inc(self.stored[slot], 16)


def loop_groups(engine, step):
    step(0, 0, True, False)
    step(1, 1, False, False)
    with engine.Fori(1, GROUPS // 2 - 1) as i:
        step(i * 2, 0, False, False)
        step(i * 2 + 1, 1, False, False)
    step(GROUPS - 2, 0, False, False)
    step(GROUPS - 1, 1, False, True)


def mla_block(nc, io, shared):
    with ExitStack() as stack:
        s = Space(nc, stack, "a_")
        arena = shared.raw.rearrange("p s n -> p (s n)")
        w_in = arena[:, 0:KD * W_IN].rearrange("p (k n) -> p k n", k=KD)
        at = KD * W_IN
        w_uq = arena[:, at:at + KQ * HEADS * (DN + DR)].rearrange("p (k n) -> p k n", k=KQ)
        at += KQ * HEADS * (DN + DR)
        w_ukv = arena[:, at:at + KKV * HEADS * (DN + DV)].rearrange("p (k n) -> p k n", k=KKV)
        w_ukv_heads = arena[:, at:at + KKV * HEADS * (DN + DV)].rearrange("p (k h n) -> p k h n", k=KKV, n=DN + DV)

        xnT = s.sb("xnT", [P, KD, N])
        cT_lo = nc.alloc_sbuf_tensor_at("a_cT_lo", [P, KQ + KKV, N], F32R, offset=nc.sbuf_base - KD * N * 4)
        c_kvT = xnT[:, KQ + KKV:KQ + 2 * KKV, :]
        c_norm = s.sb("c_norm", [P, 2, Q_LORA + KV_LORA])
        c_gain = s.sb("c_gain", [P, Q_LORA + KV_LORA])
        cT_hi = s.sb("cT_hi", [P, KQ + KKV, N], F32R)
        squares = s.sb("c_squares", [P, Q_LORA])
        c_ssq = s.sb("c_ssq", [P, TILES, 2])
        c_mean = s.sb("c_mean", [P, TILES, 2])
        c_rstd = s.sb("c_rstd", [P, TILES, 2])
        half = s.sb("minus_half", [P, 2])
        rope_tok = s.sb("rope_tok", [P, TILES, 2, DR])
        rope_T = s.sb("rope_T", [P, N])
        kr = s.sb("kr", [P, 2, 3, DR])
        qT = s.sb("qT", [DN + DR, 4, N])
        kT = s.sb("kT", [DN + DR, 4, N])
        V = s.sb("V", [P, 2, TILES, 2 * DV])
        stage_q = s.sb("stage_q", [P, 2, KQ, P])
        q_lo = nc.alloc_sbuf_tensor_at("a_q_lo", [P, 2, KQ, P], F32R, offset=nc.sbuf_base - 2 * KQ * P * 4)
        stage_k = s.sb("stage_k", [P, KKV, P])
        k_lo = nc.alloc_sbuf_tensor_at("a_k_lo", [P, KKV, P], F32R, offset=nc.sbuf_base - KKV * P * 4)
        at = shared.raw_at + ARENA_FREE_A * 4
        q_hi = nc.alloc_sbuf_tensor_at("a_q_hi", [P, 2, KQ, P], F32R, offset=at)
        at += 2 * KQ * P * 4
        k_hi = nc.alloc_sbuf_tensor_at("a_k_hi", [P, KKV, P], F32R, offset=at)
        qr = s.sb("qr", [DN + DR, 2, SAMPLE])
        core = Core(s, DN + DR, DV, (DN + DR) ** -0.5, io.o_a.rearrange("(t p) n -> p t n", p=P),
                    s.sb("probs", [P, 2, 2, SAMPLE]), s.sb("probsT_sb", [P, 2, 4, P]),
                    s.sb("out", [P, 2, TILES, 2 * DV]))
        norm = InputNorm(s, lambda t: token_rows(io.x_prompt, io.x_sample, t), row_broadcast(io.g_attn_a[0]),
                         xnT, core.S[:, 0, :, :].rearrange("p b (k n) -> p b k n", n=P),
                         x=arena[:, ARENA_FREE_A:ARENA_FREE_A + 2 * D].rearrange("p (b n) -> p b n", b=2),
                         xn=core.probs.rearrange("p b j n -> p b (j n)"),
                         junk=core.probsT[:, :, :, :].rearrange("p j k n -> p (j k n)"),
                         gain=V[:, :, :, :].rearrange("p b t n -> p (b t n)")[:, 0:D])
        c_raw = core.out[:, :, :, :].rearrange("p b t n -> p b (t n)")[:, :, 0:W_IN]
        c_ps = core.S[:, 1, :, :]
        cT_ps = core.T

        w_in_landed, w_uq_landed, w_ukv_landed = s.sem("w_in_landed"), s.sem("w_uq_landed"), s.sem("w_ukv_landed")
        tables_landed = s.sem("tables_landed")
        half_ready = s.sem("half_ready")
        c_done, c_copied = s.sem("c_done"), s.sem("c_copied")
        c_squared, c_mean_ready, c_rstd_ready = s.sem("c_squared"), s.sem("c_mean_ready"), s.sem("c_rstd_ready")
        c_normed, kr_parts, kr_ready = s.sem("c_normed"), s.sem("kr_parts"), s.sem("kr_ready")
        cT_done, cT_copied, krT_copied = s.sem("cT_done"), s.sem("cT_copied"), s.sem("krT_copied")
        q_staged, k_staged = s.sem("q_staged"), s.sem("k_staged")
        q_high, k_high = s.sem("q_high"), s.sem("k_high")
        q_split, k_split = s.sem("q_split"), s.sem("k_split")
        piece_done, piece_act = s.sem("piece_done"), s.sem("piece_act")
        qr_parts, piece_dve = s.sem("qr_parts"), s.sem("piece_dve")

        def split_by_unit(split, g, unit):
            if isinstance(g, int) and g >= GROUPS - 2:
                return
            if unit == 3:
                split("k", g + 2)
            if unit >= 4:
                split("q", g + 2, unit - 4)

        ROPES = [1, 2, 2, 3, 4, 4]
        block = stack.enter_context(nc.Block())

        @block.sync
        def _(sp):
            sp.dma_start(shared.ident[:, :], io.ident).then_inc(shared.ident_landed, 16)
            for t in range(2):
                sp.dma_start(norm.x[:, t, :], norm.x_tile_of(t)).then_inc(norm.x_landed[t], 16)
            sp.dma_start(norm.gain, norm.gain_row).then_inc(norm.gain_landed, 16)
            sp.dma_start(w_in, io.w_in_a[0].rearrange("(k p) n -> p k n", p=P)).then_inc(w_in_landed, 16)
            sp.dma_start(c_gain[:, 0:Q_LORA], row_broadcast(io.g_q_a[0])).then_inc(tables_landed, 16)
            sp.dma_start(c_gain[:, Q_LORA:], row_broadcast(io.g_kv_a[0])).then_inc(tables_landed, 16)
            sp.dma_start(rope_tok[:, :, :, :], io.rope_a_tok).then_inc(tables_landed, 16)
            sp.dma_start(rope_T[2 * DR:, :], io.rope_a_T).then_inc(tables_landed, 16)
            for t in range(2, TILES):
                sp.wait_ge(norm.xn_ready, t - 1)
                sp.dma_start(norm.x[:, t % 2, :], norm.x_tile_of(t)).then_inc(norm.x_landed[t % 2], 16)
            sp.dma_start(w_uq, io.w_uq_a[0].rearrange("(k p) n -> p k n", p=P)).then_inc(w_uq_landed, 16)
            sp.dma_start(w_ukv, io.w_ukv_a[0].rearrange("(k p) n -> p k n", p=P)).then_inc(w_ukv_landed, 16)
            sp.dma_start(shared.w_o_a, io.w_o_a[0].rearrange("(k p) n -> p k n", p=P)).then_inc(shared.w_o_landed, 16)
            loop_groups(sp, lambda g, slot, first, last: core.store(sp, g, slot))
            for slot in range(2):
                sp.wait_ge(core.stored[slot], 16 * GROUPS // 2)

        @block.gpsimd
        def _(pool):
            pool.memset(half[:, :], -0.5).then_inc(half_ready, 1)
            pool.wait_ge(half_ready, 1)

            def c_scale(t):
                pool.wait_ge(c_squared, 2 * t + 2)
                pool.tensor_scalar(c_mean[:, t, 0:1], c_ssq[:, t, 0:1], 1.0 / Q_LORA, EPS,
                                   ALU.mult, ALU.add).then_inc(c_mean_ready, 1)
                pool.tensor_scalar(c_mean[:, t, 1:2], c_ssq[:, t, 1:2], 1.0 / KV_LORA, EPS,
                                   ALU.mult, ALU.add).then_inc(c_mean_ready, 1)
                pool.wait_ge(c_mean_ready, 2 * t + 2)
                pool.tensor_tensor(c_rstd[:, t, :], c_mean[:, t, :], half[:, :], ALU.pow).then_inc(c_rstd_ready, 1)

            def stage(g):
                wait(pool, piece_done, NU * g - 3)
                pool.tensor_copy(stage_k[:, :, :].rearrange("p k (h n) -> p k h n", h=2),
                                 w_ukv_heads[:, :, bass.ds(g * 2, 2), 0:DN]).then_inc(k_staged, 1)
                for h in range(2):
                    wait(pool, piece_done, NU * g - 2 + h)
                    at = (g * 2 + h) * (DN + DR)
                    pool.tensor_copy(stage_q[:, h, :, 0:DN + DR], w_uq[:, :, bass.ds(at, DN + DR)])
                    pool.tensor_copy(stage_q[:, h, :, DN + DR:DN + DR + DR // 2],
                                     w_uq[:, :, bass.ds(at + DN + DR // 2, DR // 2)])
                    pool.tensor_copy(stage_q[:, h, :, DN + DR + DR // 2:],
                                     w_uq[:, :, bass.ds(at + DN, DR // 2)]).then_inc(q_staged, 1)

            norm.pool_tile(pool, 0, half[:, 0:1])
            norm.pool_tile(pool, 1, half[:, 0:1])
            for t in range(TILES):
                if t + 2 < TILES:
                    norm.pool_tile(pool, t + 2, half[:, 0:1])
                if t == TILES - 2:
                    pool.wait_ge(w_uq_landed, 16)
                    pool.wait_ge(w_ukv_landed, 16)
                    stage(0)
                c_scale(t)
            stage(1)
            with pool.Fori(2, GROUPS) as g:
                stage(g)

        @block.scalar
        def _(act):
            def compressed(t):
                act.wait_ge(c_done, t + 1)
                wait(act, c_normed, t - 1)
                wait(act, kr_parts, 3 * (t - 1))
                act.activation(c_raw[:, t % 2, 0:SAMPLE], c_ps[:, 0, :], ACT.Copy)
                act.activation(c_raw[:, t % 2, SAMPLE:], c_ps[:, 1, 0:W_IN - SAMPLE], ACT.Copy).then_inc(c_copied, 1)
                act.wait_ge(c_copied, t + 1)
                wait(act, c_squared, 2 * t)
                act.activation(squares[:, :], c_raw[:, t % 2, 0:Q_LORA], ACT.Square,
                               accum_out=c_ssq[:, t, 0:1]).then_inc(c_squared, 1)
                act.wait_ge(c_squared, 2 * t + 1)
                act.activation(squares[:, 0:KV_LORA], c_raw[:, t % 2, Q_LORA:Q_LORA + KV_LORA], ACT.Square,
                               accum_out=c_ssq[:, t, 1:2]).then_inc(c_squared, 1)

            def turned_c(t):
                act.wait_ge(cT_done, t + 1)
                act.activation(cT_hi[:, 0:4, t * P:(t + 1) * P], cT_ps[:, 0, :, :], ACT.Copy)
                act.activation(c_kvT[:, 0, t * P:(t + 1) * P], cT_ps[:, 0, KQ, :], ACT.Copy)
                act.activation(c_kvT[:, 1, t * P:(t + 1) * P], cT_ps[:, 1, 0, :], ACT.Copy)
                act.activation(cT_hi[:, 4:5, t * P:(t + 1) * P], cT_ps[:, 1, 0:1, :], ACT.Copy).then_inc(cT_copied, 1)

            def piece(g, slot, p):
                act.wait_ge(piece_done, NU * g + p + 1)
                if not (isinstance(g, int) and g < 2):
                    act.wait_ge(core.scores_done, NU * g - NU)
                    act.wait_ge(core.pv_done, 2 * NU * g - 2 * NU)
                bank = core.proj[:, p % 2, :]
                if p in (0, 2):
                    cols, src = (slice(0, PROMPT), bank[:, 0:PROMPT]) if p == 0 else (slice(PROMPT, N), bank)
                    act.activation(kT[0:DN, 2 * slot, cols], src[0:DN], ACT.Copy)
                    last = act.activation(kT[0:DN, 2 * slot + 1, cols], src[DN:2 * DN], ACT.Copy)
                if p == 0:
                    last = act.activation(qT[0:DN, 2 * slot, 0:PROMPT], bank[0:DN, PROMPT:], ACT.Copy)
                if p == 1:
                    act.activation(qT[0:DN, 2 * slot + 1, 0:PROMPT], bank[0:DN, 0:PROMPT], ACT.Copy)
                    last = act.activation(V[:, slot, 0:PROMPT_TILES, :].rearrange("p t n -> p (t n)"),
                                          bank[:, PROMPT:], ACT.Copy)
                if p in (3, 4):
                    last = act.activation(qT[0:DN, 2 * slot + p - 3, PROMPT:N], bank[0:DN, :], ACT.Copy)
                if p == 5:
                    last = act.activation(V[:, slot, PROMPT_TILES:, :].rearrange("p t n -> p (t n)"),
                                          bank, ACT.Copy)
                last.then_inc(piece_act, 1)

            def split(what, g, h=None):
                if what == "q":
                    act.wait_ge(q_staged, g * 2 + h + 1)
                    act.activation(q_hi[:, h, :, :], stage_q[:, h, :, :], ACT.Copy).then_inc(q_high, 1)
                if what == "k":
                    if isinstance(g, int) and g == 0:
                        act.wait_ge(norm.xn_ready, TILES)
                    act.wait_ge(k_staged, g + 1)
                    act.activation(k_hi[:, :, :], stage_k[:, :, :], ACT.Copy).then_inc(k_high, 1)

            norm.act_tile(act, 0)
            norm.act_tile(act, 1)
            for i in range(TILES + 1):
                if i < TILES:
                    norm.act_copy(act, i)
                if i + 2 < TILES:
                    norm.act_tile(act, i + 2)
                if i == TILES:
                    split("k", 0)
                    split("q", 0, 0)
                    split("q", 0, 1)
                if i >= 1:
                    compressed(i - 1)
                if i >= 2:
                    turned_c(i - 2)
            for p in range(NU):
                if p == 2:
                    turned_c(TILES - 1)
                piece(0, 0, p)
                if p >= 3:
                    split_by_unit(split, -1, p)
            core.act_exp(act, 0, 0)

            def step(g, slot, first, last):
                for unit in range(NU):
                    n = g * NU + unit
                    core.act_copy(act, n, unit)
                    if not (last and unit == NU - 1):
                        core.act_exp(act, n + 1, (unit + 1) % NU)
                    if not last:
                        piece(g + 1, 1 - slot, unit)
                    split_by_unit(split, g, unit)

            loop_groups(act, step)

        @block.vector
        def _(dve):
            def compressed(t):
                raw = c_raw[:, t % 2, :]
                if t == 0:
                    dve.wait_ge(tables_landed, 64)
                dve.wait_ge(c_rstd_ready, t + 1)
                wait(dve, cT_done, t - 1)
                dve.scalar_tensor_tensor(out=c_norm[:, t % 2, 0:Q_LORA], in0=raw[:, 0:Q_LORA],
                                         scalar=c_rstd[:, t, 0:1], in1=c_gain[:, 0:Q_LORA],
                                         op0=ALU.mult, op1=ALU.mult)
                dve.scalar_tensor_tensor(out=c_norm[:, t % 2, Q_LORA:], in0=raw[:, Q_LORA:Q_LORA + KV_LORA],
                                         scalar=c_rstd[:, t, 1:2], in1=c_gain[:, Q_LORA:],
                                         op0=ALU.mult, op1=ALU.mult).then_inc(c_normed, 1)
                r, h = raw[:, Q_LORA + KV_LORA:], DR // 2
                dve.tensor_tensor(kr[:, t % 2, 0, :], r, rope_tok[:, t, 0, :], ALU.mult).then_inc(kr_parts, 1)
                dve.tensor_tensor(kr[:, t % 2, 1, 0:h], r[:, h:], rope_tok[:, t, 1, 0:h],
                                  ALU.mult).then_inc(kr_parts, 1)
                dve.tensor_tensor(kr[:, t % 2, 1, h:], r[:, 0:h], rope_tok[:, t, 1, h:],
                                  ALU.mult).then_inc(kr_parts, 1)
                dve.wait_ge(kr_parts, 3 * t + 3)
                dve.tensor_tensor(kr[:, t % 2, 2, :], kr[:, t % 2, 0, :], kr[:, t % 2, 1, :],
                                  ALU.add).then_inc(kr_ready, 1)

            def turned_c(t):
                dve.wait_ge(cT_copied, t + 1)
                at = slice(t * P, (t + 1) * P)
                dve.tensor_tensor(cT_lo[:, 0:4, at], cT_ps[:, 0, :, :], cT_hi[:, 0:4, at], ALU.subtract)
                dve.tensor_tensor(cT_lo[:, 4:5, at], cT_ps[:, 1, 0:1, :], cT_hi[:, 4:5, at], ALU.subtract)
                for b in range(4):
                    last = dve.tensor_copy(kT[DN:, b, t * P:(t + 1) * P], cT_ps[0:DR, 1, 1, :])
                last.then_inc(krT_copied, 1)

            def piece(g, slot, p):
                if p in (2, 5):
                    return
                r = g * 4 + ROPES[p] - 1
                head = 0 if p in (0, 3) else 1
                bank = core.proj[:, p % 2, :]
                width = PROMPT if p < 2 else SAMPLE
                src = bank[:, PROMPT:] if p == 0 else bank[:, 0:width]
                cols = slice(0, PROMPT) if p < 2 else slice(PROMPT, N)
                dve.wait_ge(piece_done, NU * g + p + 1)
                if p < 2:
                    dve.wait_ge(piece_act, NU * g + p + 1)
                wait(dve, piece_dve, r)
                dve.tensor_tensor(qr[DN:, 0, 0:width], src[DN:DN + DR], rope_T[DN:DN + DR, cols],
                                  ALU.mult).then_inc(qr_parts, 1)
                dve.tensor_tensor(qr[DN:, 1, 0:width], src[DN + DR:], rope_T[DN + DR:, cols],
                                  ALU.mult).then_inc(qr_parts, 1)
                dve.wait_ge(qr_parts, r * 2 + 2)
                if not (isinstance(g, int) and g < 2):
                    dve.wait_ge(core.scores_done, NU * g - NU)
                dve.tensor_tensor(qT[DN:, 2 * slot + head, cols], qr[DN:, 0, 0:width], qr[DN:, 1, 0:width],
                                  ALU.add).then_inc(piece_dve, 1)

            def split(what, g, h=None):
                if what == "q":
                    dve.wait_ge(q_high, g * 2 + h + 1)
                    dve.tensor_tensor(q_lo[:, h, :, :], stage_q[:, h, :, :], q_hi[:, h, :, :],
                                      ALU.subtract).then_inc(q_split, 1)
                if what == "k":
                    dve.wait_ge(k_high, g + 1)
                    dve.tensor_tensor(k_lo[:, :, :], stage_k[:, :, :], k_hi[:, :, :],
                                      ALU.subtract).then_inc(k_split, 1)

            norm.dve_tile(dve, 0)
            for i in range(TILES + 1):
                if i + 1 < TILES:
                    norm.dve_tile(dve, i + 1)
                if i < TILES:
                    norm.dve_copy(dve, i)
                if i == TILES:
                    split("k", 0)
                    split("q", 0, 0)
                    split("q", 0, 1)
                if i >= 1:
                    compressed(i - 1)
                if i >= 2:
                    turned_c(i - 2)
            for p in range(NU):
                if p == 2:
                    turned_c(TILES - 1)
                piece(0, 0, p)
                if p >= 3:
                    split_by_unit(split, -1, p)
            core.dve_max(dve, 0, 0)
            core.dve_max(dve, 1, 1)

            def step(g, slot, first, last):
                for unit in range(NU):
                    n = g * NU + unit
                    core.dve_copy(dve, n, unit)
                    core.dve_rinv(dve, n, unit)
                    if not last:
                        piece(g + 1, 1 - slot, unit)
                    core.dve_out(dve, g, n, unit, slot, first or (isinstance(g, int) and g < 2))
                    if not (last and unit >= NU - 2):
                        core.dve_max(dve, n + 2, (unit + 2) % NU)
                    split_by_unit(split, g, unit)

            loop_groups(dve, step)

        @block.tensor
        def _(pe):
            pe.wait_ge(shared.ident_landed, 16)
            def turn_c(t):
                pe.wait_ge(c_normed, t + 1)
                pe.wait_ge(kr_ready, t + 1)
                wait(pe, cT_copied, t)
                wait(pe, krT_copied, t)
                for k in range(KQ + KKV):
                    pe.transpose(cT_ps[:, k // 4, k % 4, :], c_norm[:, t % 2, k * P:(k + 1) * P], shared.ident[:, :])
                pe.transpose(cT_ps[0:DR, 1, 1, :], kr[:, t % 2, 2, :], shared.ident[:, :]).then_inc(cT_done, 1)

            def compress(t):
                if t == 0:
                    pe.wait_ge(w_in_landed, 16)
                pe.wait_ge(norm.copied_act, t + 1)
                pe.wait_ge(norm.copied_dve, t + 1)
                wait(pe, c_copied, t)
                for lo, hi in ((0, SAMPLE), (SAMPLE, W_IN)):
                    for k in range(KD):
                        last = pe.matmul(c_ps[:, lo // SAMPLE, 0:hi - lo], xnT[:, k, t * P:(t + 1) * P],
                                         w_in[:, k, lo:hi], start=(k == 0), stop=(k == KD - 1))
                last.then_inc(c_done, 1)

            def products(out, pairs):
                for k, (left_hi, left_lo, right_hi, right_lo) in enumerate(pairs):
                    pe.matmul(out, left_hi, right_hi, start=(k == 0), stop=False)
                    pe.matmul(out, left_hi, right_lo, start=False, stop=False)
                    last = pe.matmul(out, left_lo, right_hi, start=False, stop=(k == len(pairs) - 1))
                return last

            def queries(g, h, out, cols):
                pe.wait_ge(q_split, g * 2 + h + 1)
                return products(out, [(q_hi[:, h, k, :], q_lo[:, h, k, :], cT_hi[:, k, cols], cT_lo[:, k, cols])
                                      for k in range(KQ)])

            def keys(g, out, cols):
                pe.wait_ge(k_split, g + 1)
                return products(out, [(k_hi[:, k, :], k_lo[:, k, :], cT_hi[:, KQ + k, cols], cT_lo[:, KQ + k, cols])
                                      for k in range(KKV)])

            def values(g, out, t):
                w = w_ukv_heads[:, :, bass.ds(g * 2, 2), DN:]
                for k in range(KKV):
                    last = pe.matmul(out, c_kvT[:, k, t * P:(t + 1) * P], w[:, k], start=(k == 0),
                                     stop=(k == KKV - 1))
                return last

            def piece(g, p):
                m = g * NU + p
                wait(pe, piece_act, m - 1)
                wait(pe, piece_dve, g * 4 + [-1, 0, 1, 2, 2, 3][p])
                bank = core.proj[:, p % 2, :]
                if p == 0:
                    keys(g, bank[:, 0:PROMPT], slice(0, PROMPT))
                    last = queries(g, 0, bank[:, PROMPT:], slice(0, PROMPT))
                if p == 1:
                    queries(g, 1, bank[:, 0:PROMPT], slice(0, PROMPT))
                    for t in range(PROMPT_TILES):
                        last = values(g, bank[:, PROMPT + t * P:PROMPT + (t + 1) * P], t)
                if p == 2:
                    last = keys(g, bank, slice(PROMPT, N))
                if p in (3, 4):
                    last = queries(g, p - 3, bank, slice(PROMPT, N))
                if p == 5:
                    for t in range(PROMPT_TILES, TILES):
                        last = values(g, bank[:, (t - PROMPT_TILES) * P:(t - PROMPT_TILES + 1) * P], t)
                last.then_inc(piece_done, 1)

            def scores(g, slot, unit):
                tile, head = UNITS[unit]
                needs = (head + 1) if tile < PROMPT_TILES else 4 + head
                pe.wait_ge(piece_act, g * NU + needs)
                pe.wait_ge(piece_dve, g * 4 + ROPES[needs - 1])
                core.pe_scores(pe, g * NU + unit, unit, qT, kT, 2 * slot + head, 2 * slot + head)

            for i in range(TILES + 1):
                if i < TILES:
                    norm.pe_tile(pe, i, shared.ident[:, :])
                if i >= 1:
                    compress(i - 1)
                if i >= 2:
                    turn_c(i - 2)
            pe.wait_ge(krT_copied, PROMPT_TILES)
            for p in range(NU):
                if p == 2:
                    turn_c(TILES - 1)
                    pe.wait_ge(cT_copied, TILES)
                    pe.wait_ge(krT_copied, TILES)
                piece(0, p)
            scores(0, 0, 0)
            scores(0, 0, 1)

            def step(g, slot, first, last):
                for unit in range(NU):
                    n = g * NU + unit
                    _, head = UNITS[unit]
                    core.pe_turn(pe, n, unit, shared.ident[:, :])
                    if not last:
                        piece(g + 1, unit)
                    pe.wait_ge(piece_act, g * NU + (2 if unit < 2 else NU))
                    core.pe_pv(pe, n, unit, lambda t: V[:, slot, t, head * DV:(head + 1) * DV])
                    if unit < NU - 2:
                        scores(g, slot, unit + 2)
                    elif not last:
                        scores(g + 1, 1 - slot, unit + 2 - NU)

            loop_groups(pe, step)
    s.end()


def gqa_block(nc, io, shared):
    with ExitStack() as stack:
        s = Space(nc, stack, "b_")
        arena = shared.raw.rearrange("p s n -> p (s n)")
        W = 4 * HD
        HALF_K = KD // 2
        w_raw = arena[:, 4 * SLOT:8 * SLOT].rearrange("p (b k n) -> p b k n", b=2, k=KD)
        w_lo = shared.over_raw(nc, "b_w_lo", [P, 2, KD, W], 4)
        w_hi = shared.over_raw(nc, "b_w_hi", [P, 2, KD, W], 8)
        rope = arena[:, 6 * SLOT:6 * SLOT + TILES * 2 * HD].rearrange("p (t a n) -> p t a n", a=2, n=HD)
        gains = arena[:, 7 * SLOT:7 * SLOT + 2 * HD].rearrange("p (g n) -> p g n", g=2)
        squares = arena[:, 0:3 * HD].rearrange("p (h n) -> p h n", h=3)
        straight = arena[:, 3 * HD:6 * HD].rearrange("p (h n) -> p h n", h=3)
        crossed = arena[:, 6 * HD:9 * HD].rearrange("p (h n) -> p h n", h=3)
        raw = arena[:, 9 * HD:15 * HD].rearrange("p (b h n) -> p b h n", b=2, h=3)
        at = 15 * HD
        probs = arena[:, at:at + 4 * SAMPLE].rearrange("p (b j n) -> p b j n", b=2, j=2)
        at += 4 * SAMPLE
        probsT = arena[:, at:at + 2 * SAMPLE].rearrange("p (j k n) -> p j k n", j=2, n=P)
        at += 2 * SAMPLE
        out_flat = arena[:, at:at + 4 * TILES * HD]
        at += 4 * TILES * HD
        ssq, mean, rstd = (arena[:, at + 6 * i:at + 6 * i + 6].rearrange("p (b h) -> p b h", b=2) for i in range(3))
        xnT = s.sb("xnT", [P, KD, N], F32R)
        xnT_lo = s.sb("xnT_lo", [P, KD, N], F32R)
        tables = s.sb("tables", [P, TILES, 2, 3, HD])
        half = s.sb("minus_half", [P, 3])
        normed = s.sb("normed", [P, 2, 3, HD])
        qkT_hi = s.sb("qkT_hi", [P, 2, 3, N], F32R)
        qkT_lo = s.sb("qkT_lo", [P, 2, 3, N], F32R)
        V = s.sb("V", [P, 2, TILES, HD])
        core = Core(s, HD, HD, HD ** -0.5, io.o_b.rearrange("(t p) n -> p t n", p=P), probs, probsT,
                    out_flat.rearrange("p (b t n) -> p b t n", b=2, t=TILES))
        norm = InputNorm(s, lambda t: io.acc[t * P:(t + 1) * P, :], row_broadcast(io.g_attn_b[0]), xnT,
                         core.S[:, 0, :, :].rearrange("p b (k n) -> p b k n", n=P),
                         x=out_flat[:, 0:2 * D].rearrange("p (b n) -> p b n", b=2),
                         xn=core.probs.rearrange("p b j n -> p b (j n)"),
                         junk=core.probsT[:, :, :, :].rearrange("p j k n -> p (j k n)"),
                         gain=out_flat[:, 2 * D:3 * D], xnT_lo=xnT_lo)
        first_turns = core.T[:, :, :, :].rearrange("p b k n -> p b (k n)")

        w_landed = [s.sem("w_landed0"), s.sem("w_landed1")]
        tables_landed, tables_ready = s.sem("tables_landed"), s.sem("tables_ready")
        half_ready, w_high, w_split = s.sem("half_ready"), s.sem("w_high"), s.sem("w_split")
        proj_done, raw_ready, v_ready, sq_ready = s.sem("proj_done"), s.sem("raw_ready"), s.sem("v_ready"), s.sem("sq_ready")
        ssq_ready, mean_ready, rstd_ready = s.sem("ssq_ready"), s.sem("mean_ready"), s.sem("rstd_ready")
        normed_ready, straight_ready, crossed_ready = s.sem("normed_ready"), s.sem("straight_ready"), s.sem("crossed_ready")
        roped_ready, qkT_done = s.sem("roped_ready"), s.sem("qkT_done")
        qkT_high, qkT_split = s.sem("qkT_high"), s.sem("qkT_split")
        block = stack.enter_context(nc.Block())

        @block.sync
        def _(sp):
            def weights(g, slot, h):
                if not (isinstance(g, int) and g < 2):
                    sp.wait_ge(proj_done, g * NU - NU)
                if not (isinstance(g, int) and g == 0):
                    sp.wait_ge(w_split, g * 2 - 1 + h)
                src = io.w_qkv_b[0].rearrange("(h k p) n -> h p k n", h=2, p=P)[h]
                dst = w_raw[:, slot, h * HALF_K:(h + 1) * HALF_K, :]
                sp.dma_start(dst[:, :, 0:2 * HD], src[:, :, bass.ds(g * 2 * HD, 2 * HD)]).then_inc(w_landed[h], 16)
                sp.dma_start(dst[:, :, 2 * HD:3 * HD],
                             src[:, :, bass.ds(g * HD + HEADS * HD, HD)]).then_inc(w_landed[h], 16)
                sp.dma_start(dst[:, :, 3 * HD:],
                             src[:, :, bass.ds(g * HD + (HEADS + KV_HEADS) * HD, HD)]).then_inc(w_landed[h], 16)

            for t in range(2):
                sp.dma_start(norm.x[:, t % 2, :], norm.x_tile_of(t)).then_inc(norm.x_landed[t], 16)
            sp.dma_start(norm.gain, norm.gain_row).then_inc(norm.gain_landed, 16)
            weights(0, 0, 0)
            weights(0, 0, 1)
            sp.dma_start(rope, io.rope_b).then_inc(tables_landed, 16)
            sp.dma_start(gains[:, 0, :], row_broadcast(io.g_qn_b[0])).then_inc(tables_landed, 16)
            sp.dma_start(gains[:, 1, :], row_broadcast(io.g_kn_b[0])).then_inc(tables_landed, 16)
            for t in range(2, TILES):
                sp.wait_ge(norm.xn_ready, t - 1)
                sp.dma_start(norm.x[:, t % 2, :], norm.x_tile_of(t)).then_inc(norm.x_landed[t % 2], 16)
            sp.wait_ge(tables_ready, 15)
            weights(1, 1, 0)
            weights(1, 1, 1)

            def step(g, slot):
                weights(g + 2, slot, 0)
                weights(g + 2, slot, 1)
                core.store(sp, g, slot)

            step(0, 0)
            step(1, 1)
            with sp.Fori(1, GROUPS // 2 - 1) as i:
                step(i * 2, 0)
                step(i * 2 + 1, 1)
            sp.wait_ge(proj_done, NU * GROUPS)
            sp.dma_start(shared.w_o_b, io.w_o_b[0].rearrange("(k p) n -> p k n", p=P)).then_inc(shared.w_o_landed, 16)
            core.store(sp, GROUPS - 2, 0)
            core.store(sp, GROUPS - 1, 1)
            for slot in range(2):
                sp.wait_ge(core.stored[slot], 16 * GROUPS // 2)

        @block.gpsimd
        def _(pool):
            pool.memset(half[:, :], -0.5).then_inc(half_ready, 1)
            pool.wait_ge(half_ready, 1)

            def table(h):
                gain = gains[:, h // 2, :]
                pool.tensor_tensor(tables[:, :, 0, h, :], rope[:, :, 0, :],
                                   gain.unsqueeze(1).to_broadcast([P, TILES, HD]), ALU.mult).then_inc(tables_ready, 1)
                for axis in range(2):
                    for side in range(2):
                        at, other = axis * 64 + side * 32, axis * 64 + (1 - side) * 32
                        pool.tensor_tensor(tables[:, :, 1, h, at:at + 32], rope[:, :, 1, at:at + 32],
                                           gain[:, other:other + 32].unsqueeze(1).to_broadcast([P, TILES, 32]),
                                           ALU.mult).then_inc(tables_ready, 1)

            def tile(m, t):
                pool.wait_ge(mean_ready, m + 1)
                wait(pool, normed_ready, m)
                pool.tensor_tensor(rstd[:, t % 2, :], mean[:, t % 2, :], half[:, :], ALU.pow).then_inc(rstd_ready, 1)
                pool.wait_ge(rstd_ready, m + 1)
                wait(pool, qkT_done, m - 1)
                pool.tensor_tensor(normed[:, t % 2, :, :], raw[:, t % 2, :, :],
                                   rstd[:, t % 2, :].unsqueeze(2).to_broadcast([P, 3, HD]),
                                   ALU.mult).then_inc(normed_ready, 1)
                pool.wait_ge(normed_ready, m + 1)
                wait(pool, roped_ready, m)
                pool.tensor_tensor(straight[:, :, :], normed[:, t % 2, :, :], tables[:, t, 0, :, :],
                                   ALU.mult).then_inc(straight_ready, 1)

            norm.pool_tile(pool, 0, half[:, 0:1])
            norm.pool_tile(pool, 1, half[:, 0:1])
            pool.wait_ge(tables_landed, 48)
            for h in range(3):
                table(h)
                norm.pool_tile(pool, 2 + h, half[:, 0:1])
            norm.pool_tile(pool, TILES - 1, half[:, 0:1])
            pool.wait_ge(tables_ready, 5 * 3)
            for t in range(TILES):
                tile(t, t)
            with pool.Fori(1, GROUPS) as g:
                for t in range(TILES):
                    tile(g * NU + t, t)

        @block.scalar
        def _(act):
            def split_high(g, slot, h):
                act.wait_ge(w_landed[h], g * 48 + 48)
                if not (isinstance(g, int) and g < 2):
                    act.wait_ge(proj_done, g * NU - NU)
                act.activation(w_hi[:, slot, h * HALF_K:(h + 1) * HALF_K, :], w_raw[:, slot, h * HALF_K:(h + 1) * HALF_K, :],
                               ACT.Copy).then_inc(w_high, 1)

            def projected(g, slot, t):
                m = g * NU + t
                bank = core.proj[:, t % 2, :].rearrange("p (h n) -> p h n", h=4)
                act.wait_ge(proj_done, m + 1)
                wait(act, normed_ready, m - 1)
                act.activation(raw[:, t % 2, :, :], bank[:, 0:3, :], ACT.Copy).then_inc(raw_ready, 1)
                wait(act, ssq_ready, m)
                act.activation(squares, bank[:, 0:3, :], ACT.Square).then_inc(sq_ready, 1)
                if not (isinstance(g, int) and g < 2):
                    act.wait_ge(core.pv_done, 2 * NU * g - 2 * NU)
                act.activation(V[:, slot, t, :], bank[:, 3, :], ACT.Copy).then_inc(v_ready, 1)

            def turned(g, slot, t, banks):
                m = g * NU + t
                bank = banks[:, t % 2, :].rearrange("p (h n) -> p h n", h=4)
                act.wait_ge(qkT_done, m + 1)
                if not (isinstance(g, int) and g < 2):
                    act.wait_ge(core.scores_done, NU * g - NU)
                act.activation(qkT_hi[:, slot, :, t * P:(t + 1) * P], bank[:, 0:3, :],
                               ACT.Copy).then_inc(qkT_high, 1)

            norm.act_tile(act, 0)
            norm.act_tile(act, 1)
            for i in range(TILES + 2):
                if i < TILES:
                    norm.act_copy(act, i)
                if i == 0:
                    split_high(0, 0, 0)
                    split_high(0, 0, 1)
                if i + 2 < TILES:
                    norm.act_tile(act, i + 2)
                if 1 <= i <= TILES:
                    projected(0, 0, i - 1)
                if i >= 3:
                    turned(0, 0, i - 3, first_turns)
                if i == TILES + 1:
                    core.act_exp(act, 0, 0)
                if i >= TILES:
                    split_high(1, 1, i - TILES)

            def step(g, slot, first, last):
                for unit in range(NU):
                    n = g * NU + unit
                    core.act_copy(act, n, unit)
                    if unit == 0:
                        core.act_exp(act, n + 1, 1)
                        if not last:
                            projected(g + 1, 1 - slot, 0)
                        turned(g, slot, TILES - 1, core.proj)
                        continue
                    if not (last and unit == NU - 1):
                        core.act_exp(act, n + 1, (unit + 1) % NU)
                    if not last:
                        projected(g + 1, 1 - slot, unit)
                        turned(g + 1, 1 - slot, unit - 1, core.proj)
                    if unit in (2, 4) and not (isinstance(g, int) and g >= GROUPS - 2):
                        split_high(g + 2, slot, unit // 4)

            loop_groups(act, step)

        @block.vector
        def _(dve):
            def split_low(g, slot, h):
                dve.wait_ge(w_high, g * 2 + h + 1)
                dve.tensor_tensor(w_lo[:, slot, h * HALF_K:(h + 1) * HALF_K, :],
                                  w_raw[:, slot, h * HALF_K:(h + 1) * HALF_K, :],
                                  w_hi[:, slot, h * HALF_K:(h + 1) * HALF_K, :], ALU.subtract).then_inc(w_split, 1)

            def squared(m, t):
                dve.wait_ge(sq_ready, m + 1)
                wait(dve, mean_ready, m - 1)
                dve.tensor_reduce(ssq[:, t % 2, :], squares, AX.X, ALU.add).then_inc(ssq_ready, 1)
                dve.wait_ge(ssq_ready, m + 1)
                wait(dve, rstd_ready, m - 1)
                dve.tensor_scalar(mean[:, t % 2, :], ssq[:, t % 2, :], 1.0 / HD, EPS,
                                  ALU.mult, ALU.add).then_inc(mean_ready, 1)

            def rotate(m, t):
                dve.wait_ge(normed_ready, m + 1)
                wait(dve, roped_ready, m)
                a = normed[:, t % 2, :, :].rearrange("p h (x s n) -> p (h x) s n", x=2, s=2)
                c = crossed[:, :, :].rearrange("p h (x s n) -> p (h x) s n", x=2, s=2)
                sin = tables[:, t, 1, :, :].rearrange("p h (x s n) -> p (h x) s n", x=2, s=2)
                for side in range(2):
                    dve.tensor_tensor(c[:, :, side, :], a[:, :, 1 - side, :], sin[:, :, side, :],
                                      ALU.mult).then_inc(crossed_ready, 1)
                dve.wait_ge(crossed_ready, 2 * m + 2)
                dve.wait_ge(straight_ready, m + 1)
                dve.tensor_tensor(normed[:, t % 2, :, :], straight[:, :, :], crossed[:, :, :],
                                  ALU.add).then_inc(roped_ready, 1)

            def turned(g, slot, t, banks):
                m = g * NU + t
                at = slice(t * P, (t + 1) * P)
                bank = banks[:, t % 2, :].rearrange("p (h n) -> p h n", h=4)
                dve.wait_ge(qkT_high, m + 1)
                dve.tensor_tensor(qkT_lo[:, slot, :, at], bank[:, 0:3, :], qkT_hi[:, slot, :, at],
                                  ALU.subtract).then_inc(qkT_split, 1)

            norm.dve_tile(dve, 0)
            for i in range(TILES + 2):
                if i + 1 < TILES:
                    norm.dve_tile(dve, i + 1)
                if i < TILES:
                    norm.dve_copy(dve, i)
                if i == 0:
                    split_low(0, 0, 0)
                    split_low(0, 0, 1)
                if 1 <= i <= TILES:
                    squared(i - 1, i - 1)
                if 2 <= i < TILES + 1:
                    rotate(i - 2, i - 2)
                if i >= 3:
                    turned(0, 0, i - 3, first_turns)
            core.dve_max(dve, 0, 0)
            core.dve_max(dve, 1, 1)
            split_low(1, 1, 0)
            split_low(1, 1, 1)

            def step(g, slot, first, last):
                for unit in range(NU):
                    n = g * NU + unit
                    core.dve_copy(dve, n, unit)
                    core.dve_rinv(dve, n, unit)
                    if unit == 0:
                        rotate(g * NU + TILES - 1, TILES - 1)
                    elif not last:
                        rotate(g * NU + NU + unit - 1, unit - 1)
                    if unit == 0:
                        turned(g, slot, TILES - 1, core.proj)
                    if not last:
                        squared(g * NU + NU + unit, unit)
                        if unit:
                            turned(g + 1, 1 - slot, unit - 1, core.proj)
                    core.dve_out(dve, g, n, unit, slot, first or (isinstance(g, int) and g < 2))
                    if not (last and unit >= NU - 2):
                        core.dve_max(dve, n + 2, (unit + 2) % NU)
                    if unit in (2, 4) and not (isinstance(g, int) and g >= GROUPS - 2):
                        split_low(g + 2, slot, unit // 4)

            loop_groups(dve, step)

        @block.tensor
        def _(pe):
            def project(g, slot, t):
                m = g * NU + t
                if isinstance(g, int) and g == 0:
                    pe.wait_ge(norm.copied_act, t + 1)
                    pe.wait_ge(norm.copied_dve, t + 1)
                    wait(pe, v_ready, m - 1)
                else:
                    pe.wait_ge(qkT_split, m - 1)
                at, out = slice(t * P, (t + 1) * P), core.proj[:, t % 2, :]
                for k in range(KD):
                    if t == 0 and k % HALF_K == 0:
                        pe.wait_ge(w_split, g * 2 + k // HALF_K + 1)
                    pe.matmul(out, xnT[:, k, at], w_hi[:, slot, k, :], start=(k == 0), stop=False)
                    pe.matmul(out, xnT[:, k, at], w_lo[:, slot, k, :], start=False, stop=False)
                    last = pe.matmul(out, xnT_lo[:, k, at], w_hi[:, slot, k, :], start=False, stop=(k == KD - 1))
                last.then_inc(proj_done, 1)

            def turn(g, t, banks):
                m = g * NU + t
                pe.wait_ge(roped_ready, m + 1)
                if banks is first_turns:
                    wait(pe, qkT_split, m - 1)
                else:
                    pe.wait_ge(v_ready, m + 1)
                for h in range(3):
                    last = pe.transpose(banks[:, t % 2, h * HD:(h + 1) * HD], normed[:, t % 2, h, :],
                                        shared.ident[:, :])
                last.then_inc(qkT_done, 1)

            def scores(g, slot, unit):
                tile, head = UNITS[unit]
                pe.wait_ge(qkT_split, g * NU + (2 if tile < PROMPT_TILES else TILES))
                core.pe_scores_of_parts(pe, g * NU + unit, unit, qkT_hi[:, slot, :, :], qkT_lo[:, slot, :, :],
                                        head, 2)

            for i in range(TILES + 2):
                if i < TILES:
                    norm.pe_tile(pe, i, shared.ident[:, :])
                if 1 <= i <= TILES:
                    project(0, 0, i - 1)
                if i == TILES + 1:
                    scores(0, 0, 0)
                    scores(0, 0, 1)
                if i >= 3:
                    turn(0, i - 3, first_turns)
            pe.wait_ge(qkT_split, TILES - 1)

            def step(g, slot, first, last):
                for unit in range(NU):
                    n = g * NU + unit
                    core.pe_turn(pe, n, unit, shared.ident[:, :])
                    if not last:
                        project(g + 1, 1 - slot, unit)
                    if unit == 0:
                        turn(g, TILES - 1, core.proj)
                    elif not last:
                        turn(g + 1, unit - 1, core.proj)
                    core.pe_pv(pe, n, unit, lambda t: V[:, slot, t, :])
                    if unit < NU - 2:
                        scores(g, slot, unit + 2)
                    elif not last:
                        scores(g + 1, 1 - slot, unit + 2 - NU)

            loop_groups(pe, step)
    s.end()


def output_block(nc, io, shared, layer):
    with ExitStack() as stack:
        s = Space(nc, stack, f"o{layer}_")
        o_dram, w_o = (io.o_a, shared.w_o_a) if layer == 0 else (io.o_b, shared.w_o_b)
        KO = o_dram.shape[1] // P
        HALVES = KO // KD
        SAMPLE_TILES = TILES - PROMPT_TILES
        ORDER = list(range(PROMPT_TILES, TILES)) + list(range(PROMPT_TILES))
        LAST_SAMPLE = SAMPLE_TILES - 1
        w_lo = shared.over_raw(nc, f"o{layer}_w_lo", [P, KO, D], SLOTS - KO // 2)
        w_hi_own = s.sb("w_hi_own", [P, KD, D], F32R)
        w_hi_raw = shared.over_raw(nc, f"o{layer}_w_hi", [P, KD, D], 0) if HALVES == 2 else None
        o_in = s.sb("o_in", [P, 2, KD * P])
        oT_hi = s.sb("oT_hi", [P, 2, KO, P], F32R)
        oT_lo = s.sb("oT_lo", [P, 2, KO, P], F32R)
        x = s.sb("x", [P, 2, D])
        xn = s.sb("xn", [P, 2, D])
        xnT = s.sb("xnT", [P, KD, P])
        junk = s.sb("squares", [P, D])
        gain = s.sb("gain", [P, D])
        w_r = s.sb("w_router", [P, KD, EXPERTS])
        ssq, mean, rstd = s.sb("ssq", [P, TILES]), s.sb("mean", [P, TILES]), s.sb("rstd", [P, TILES])
        half = s.sb("minus_half", [P, 1])
        logits = s.sb("logits", [P, TILES, EXPERTS])
        top = s.sb("top", [P, TILES])
        shifted = s.sb("shifted", [P, TILES, EXPERTS])
        expd = s.sb("expd", [P, TILES, EXPERTS])
        total, inv = s.sb("total", [P, TILES]), s.sb("inv", [P, TILES])
        aff = s.sb("aff", [P, TILES, EXPERTS])
        work = [s.sb("work_s", [EXPERTS, SAMPLE]), s.sb("work_p", [EXPERTS, PROMPT])]
        best = s.sb("best", [EXPERTS, CAP])
        best_at = s.sb("best_at", [EXPERTS, CAP], U32)
        chosen = s.sb("chosen", [EXPERTS, 2, CAP])
        oT_ps = s.psum("oT", [P, 2, 4, P])
        y_ps = s.psum("y", [P, 2, SAMPLE])
        xT_ps = s.psum("xT", [P, 2, 4, P])
        bank_a, bank_b = s.psum("router_a", [P, SAMPLE]), s.psum("router_b", [P, SAMPLE])
        logits_ps = [bank_a[:, 0:SAMPLE_TILES * EXPERTS].rearrange("p (t e) -> p t e", e=EXPERTS),
                     bank_b[:, 0:PROMPT_TILES * EXPERTS].rearrange("p (t e) -> p t e", e=EXPERTS)]
        affT_ps = [bank_b[0:EXPERTS, 0:SAMPLE], bank_a[0:EXPERTS, 0:PROMPT]]
        lists_ps = bank_b[0:CAP, 0:2 * EXPERTS].rearrange("p (w e) -> p w e", e=EXPERTS)
        TILES_OF = [slice(PROMPT_TILES, TILES), slice(0, PROMPT_TILES)]
        COUNT_OF = [SAMPLE_TILES, PROMPT_TILES]
        PLACES_OF = [slice(0, CAP_S), slice(CAP_S, CAP)]
        ROUNDS = [CAP_S // 8, CAP_P // 8]

        o_landed = [s.sem("o_landed0"), s.sem("o_landed1")]
        x_landed = [s.sem("x_landed0"), s.sem("x_landed1")]
        small_landed, w_high, w_split = s.sem("small_landed"), s.sem("w_high"), s.sem("w_split")
        oT_done, oT_high, oT_split, y_done = s.sem("oT_done"), s.sem("oT_high"), s.sem("oT_split"), s.sem("y_done")
        w_used = s.sem("w_used")
        x_ready, x_stored = s.sem("x_ready"), [s.sem("x_stored0"), s.sem("x_stored1")]
        ssq_ready, half_ready, mean_ready, rstd_ready = s.sem("ssq"), s.sem("half"), s.sem("mean"), s.sem("rstd")
        xn_ready, xn_stored = s.sem("xn_ready"), [s.sem("xn_stored0"), s.sem("xn_stored1")]
        xT_done, xT_copied, router_done, logits_ready = s.sem("xT_done"), s.sem("xT_copied"), s.sem("router_done"), s.sem("logits")
        chain, exp_ready, aff_ready = s.sem("softmax_steps"), s.sem("exp"), s.sem("aff")
        affT_done, chosen_ready, chosenT_done = s.sem("affT_done"), s.sem("chosen"), s.sem("chosenT_done")
        choice = [s.sem("choice_s"), s.sem("choice_p")]
        block = stack.enter_context(nc.Block())

        def rows(dram, i):
            return dram[ORDER[i] * P:(ORDER[i] + 1) * P]

        def w_hi(k):
            return w_hi_own[:, k % KD, :] if k >= KO - KD else w_hi_raw[:, k, :]

        @block.sync
        def _(sp):
            def load_o(i):
                for q in range(i * HALVES, (i + 1) * HALVES):
                    wait(sp, oT_done, q - 1)
                    h = q % HALVES
                    sp.dma_start(o_in[:, q % 2, :], rows(o_dram, i)[:, h * KD * P:(h + 1) * KD * P]
                                 ).then_inc(o_landed[q % 2], 16)

            def load_x(i):
                slot = i % 2
                if i >= 2:
                    sp.wait_ge(xn_ready, i - 1)
                    sp.wait_ge(ssq_ready, i - 1)
                    sp.wait_ge(x_stored[slot], 8 * (i - slot))
                src = token_rows(io.x_prompt, io.x_sample, ORDER[i]) if layer == 0 else rows(io.acc, i)
                sp.dma_start(x[:, slot, :], src).then_inc(x_landed[slot], 16)

            def store(i):
                slot = i % 2
                sp.wait_ge(x_ready, 2 * i + 2)
                sp.dma_start(rows(io.acc, i), x[:, slot, :]).then_inc(x_stored[slot], 16)
                sp.wait_ge(xn_ready, i + 1)
                sp.dma_start(rows(io.xn, i), xn[:, slot, :]).then_inc(xn_stored[slot], 16)

            load_o(0)
            load_x(0)
            load_x(1)
            sp.dma_start(gain[:, :], row_broadcast(io.g_ffn[layer])).then_inc(small_landed, 16)
            sp.dma_start(w_r[:, :, :], io.w_router[layer].rearrange("(k p) e -> p k e", p=P)).then_inc(small_landed, 16)
            load_o(1)
            for i in range(TILES):
                if i + 2 < TILES:
                    load_o(i + 2)
                if i == TILES - 1:
                    for quarter in range(4):
                        if quarter < 3:
                            sp.wait_ge(w_used, quarter + 1)
                        else:
                            sp.wait_ge(y_done, 2 * TILES)
                        if layer == 0:
                            shared.load_first(sp, io.w_down, layer, 8, quarter)
                        elif quarter < 2:
                            for j in (2 * quarter, 2 * quarter + 1):
                                shared.load_first(sp, io.w_gate, layer, 4, j)
                                shared.load_first(sp, io.w_up, layer, 0, j)
                        else:
                            shared.load_first(sp, io.w_down, layer, 8, 2 * quarter - 4)
                            shared.load_first(sp, io.w_down, layer, 8, 2 * quarter - 3)
                store(i)
                if i + 2 < TILES:
                    load_x(i + 2)
                    if layer == 0:
                        shared.load_first(sp, io.w_gate, layer, 4, i)
                        shared.load_first(sp, io.w_up, layer, 0, i)
            for slot in range(2):
                sp.wait_ge(x_stored[slot], 16 * TILES // 2)
                sp.wait_ge(xn_stored[slot], 16 * TILES // 2)

        @block.gpsimd
        def _(pool):
            pool.memset(half[:, :], -0.5).then_inc(half_ready, 1)
            pool.wait_ge(half_ready, 1)
            for i in range(TILES):
                pool.wait_ge(ssq_ready, i + 1)
                pool.tensor_scalar(mean[:, i:i + 1], ssq[:, i:i + 1], 1.0 / D, EPS,
                                   ALU.mult, ALU.add).then_inc(mean_ready, 1)
                pool.wait_ge(mean_ready, i + 1)
                pool.tensor_tensor(rstd[:, i:i + 1], mean[:, i:i + 1], half[:, :], ALU.pow).then_inc(rstd_ready, 1)

        @block.scalar
        def _(act):
            def split_high(k):
                act.activation(w_hi(k), w_o[:, k, :], ACT.Copy).then_inc(w_high, 1)

            def copy_oT(i):
                for h in range(HALVES):
                    act.wait_ge(oT_done, HALVES * i + h + 1)
                    wait(act, y_done, 2 * i - 2)
                    act.activation(oT_hi[:, i % 2, h * KD:(h + 1) * KD, :],
                                   oT_ps[:, :, :, :].rearrange("p b k n -> p (b k) n"), ACT.Copy).then_inc(oT_high, 1)

            def square(i):
                act.wait_ge(x_ready, 2 * i + 2)
                wait(act, ssq_ready, i)
                act.activation(junk[:, :], x[:, i % 2, :], ACT.Square,
                               accum_out=ssq[:, i:i + 1]).then_inc(ssq_ready, 1)

            def exp(part):
                act.wait_ge(chain, 4 * part + 2)
                act.activation(expd[:, TILES_OF[part], :], shifted[:, TILES_OF[part], :],
                               ACT.Exp).then_inc(exp_ready, 1)

            act.wait_ge(shared.w_o_landed, 16 * (layer + 1))
            for k in range(4):
                split_high(k)
            copy_oT(0)
            for k in range(4, KO):
                split_high(k)
            for i in range(TILES):
                if i:
                    square(i - 1)
                if i + 1 < TILES:
                    copy_oT(i + 1)
                if i == LAST_SAMPLE + 1:
                    exp(0)
            square(TILES - 1)
            exp(1)

        @block.vector
        def _(dve):
            def split_low(k):
                dve.wait_ge(w_high, k + 1)
                dve.tensor_tensor(w_lo[:, k, :], w_o[:, k, :], w_hi(k), ALU.subtract).then_inc(w_split, 1)

            def low_oT(i):
                for h in range(HALVES):
                    at = slice(h * KD, (h + 1) * KD)
                    dve.wait_ge(oT_high, HALVES * i + h + 1)
                    dve.tensor_tensor(oT_lo[:, i % 2, at, :], oT_ps[:, :, :, :].rearrange("p b k n -> p (b k) n"),
                                      oT_hi[:, i % 2, at, :], ALU.subtract).then_inc(oT_split, 1)

            def add(i):
                slot = i % 2
                dve.wait_ge(x_landed[slot], 16 * (i // 2 + 1))
                for n in range(2):
                    cols = slice(n * SAMPLE, (n + 1) * SAMPLE)
                    dve.wait_ge(y_done, 2 * i + n + 1)
                    dve.tensor_tensor(x[:, slot, cols], x[:, slot, cols], y_ps[:, n, :],
                                      ALU.add).then_inc(x_ready, 1)

            def normalise(i):
                slot = i % 2
                dve.wait_ge(x_ready, 2 * i + 2)
                dve.wait_ge(rstd_ready, i + 1)
                if i == 0:
                    dve.wait_ge(small_landed, 32)
                if i >= 2:
                    dve.wait_ge(xT_done, i - 1)
                    dve.wait_ge(xn_stored[slot], 16 * (i // 2))
                dve.scalar_tensor_tensor(out=xn[:, slot, :], in0=x[:, slot, :], scalar=rstd[:, i:i + 1],
                                         in1=gain[:, :], op0=ALU.mult, op1=ALU.mult).then_inc(xn_ready, 1)

            def copy_xT(i):
                dve.wait_ge(xT_done, i + 1)
                wait(dve, router_done, i)
                dve.tensor_copy(xnT[:, :, :], xT_ps[:, :, :, :].rearrange("p b k n -> p (b k) n")).then_inc(xT_copied, 1)

            def softmax(part):
                at, count, step = TILES_OF[part], COUNT_OF[part], 4 * part
                dve.wait_ge(router_done, SAMPLE_TILES if part == 0 else TILES)
                dve.tensor_copy(logits[:, at, :], logits_ps[part]).then_inc(logits_ready, 1)
                dve.wait_ge(logits_ready, part + 1)
                dve.tensor_reduce(top[:, at], logits[:, at, :], AX.X, ALU.max).then_inc(chain, 1)
                dve.wait_ge(chain, step + 1)
                dve.tensor_tensor(shifted[:, at, :], logits[:, at, :],
                                  top[:, at].unsqueeze(2).to_broadcast([P, count, EXPERTS]),
                                  ALU.subtract).then_inc(chain, 1)

            def softmax_end(part):
                at, count, step = TILES_OF[part], COUNT_OF[part], 4 * part
                dve.wait_ge(exp_ready, part + 1)
                dve.tensor_reduce(total[:, at], expd[:, at, :], AX.X, ALU.add).then_inc(chain, 1)
                dve.wait_ge(chain, step + 3)
                dve.reciprocal(inv[:, at], total[:, at]).then_inc(chain, 1)
                dve.wait_ge(chain, step + 4)
                dve.tensor_tensor(aff[:, at, :], expd[:, at, :],
                                  inv[:, at].unsqueeze(2).to_broadcast([P, count, EXPERTS]),
                                  ALU.mult).then_inc(aff_ready, 1)

            def copy_aff(part):
                dve.wait_ge(affT_done, part + 1)
                dve.tensor_copy(work[part][:, :], affT_ps[part]).then_inc(choice[part], 1)

            def choose(part, r):
                first = PLACES_OF[part].start + 8 * r
                at, open_ = slice(first, first + 8), work[part][:, :]
                dve.wait_ge(choice[part], 3 * r + 1)
                dve.max(best[:, at], open_).then_inc(choice[part], 1)
                dve.wait_ge(choice[part], 3 * r + 2)
                dve.max_index(best_at[:, at], best[:, at], open_).then_inc(choice[part], 1)
                dve.wait_ge(choice[part], 3 * r + 3)
                dve.match_replace(open_, best[:, at], open_, -1.0).then_inc(choice[part], 1)

            def list_choices(part):
                at = PLACES_OF[part]
                dve.wait_ge(choice[part], 3 * ROUNDS[part] + 1)
                dve.tensor_scalar(chosen[:, 0, at], best_at[:, at], float(PROMPT if part == 0 else 0), None,
                                  ALU.add).then_inc(chosen_ready, 1)
                dve.tensor_copy(chosen[:, 1, at], best[:, at]).then_inc(chosen_ready, 1)

            for k in range(4):
                split_low(k)
            low_oT(0)
            for k in range(4, KO):
                split_low(k)
            for i in range(LAST_SAMPLE + 2):
                if i:
                    add(i - 1)
                    normalise(i - 1)
                low_oT(i + 1)
                if i:
                    copy_xT(i - 1)
            softmax(0)
            softmax_end(0)
            add(LAST_SAMPLE + 1)
            normalise(LAST_SAMPLE + 1)
            copy_aff(0)
            BEFORE = [1, 3, 4, 5, 6, 6] if layer == 0 else [2, 5, 6, 7, 7, 7]
            for r in range(ROUNDS[0] + 1):
                if r == BEFORE[0]:
                    copy_xT(TILES - 2)
                if r == BEFORE[1]:
                    add(TILES - 1)
                if r == BEFORE[2]:
                    normalise(TILES - 1)
                if r == BEFORE[3]:
                    copy_xT(TILES - 1)
                if r == BEFORE[4]:
                    softmax(1)
                if r < ROUNDS[0]:
                    choose(0, r)
                if r == BEFORE[5]:
                    softmax_end(1)
            list_choices(0)
            copy_aff(1)
            for r in range(ROUNDS[1]):
                choose(1, r)
            list_choices(1)
            dve.wait_ge(chosenT_done, 1)
            dve.tensor_copy(shared.row_of[:, :], lists_ps[:, 0, :]).then_inc(shared.lists_ready, 1)
            dve.tensor_copy(shared.gate_of[:, :], lists_ps[:, 1, :]).then_inc(shared.lists_ready, 1)

        @block.tensor
        def _(pe):
            ident = shared.ident[:, :]

            def turn_o(i):
                for q in range(i * HALVES, (i + 1) * HALVES):
                    pe.wait_ge(o_landed[q % 2], 16 * (q // 2 + 1))
                    wait(pe, oT_split, q)
                    for k in range(KD):
                        last = pe.transpose(oT_ps[:, k // 4, k % 4, :], o_in[:, q % 2, k * P:(k + 1) * P], ident)
                    last.then_inc(oT_done, 1)

            def project(i, part):
                if part == 0:
                    pe.wait_ge(oT_split, HALVES * (i + 1))
                for n in range(2):
                    cols = slice(n * SAMPLE, (n + 1) * SAMPLE)
                    if part == 0:
                        wait(pe, x_ready, 2 * i - 1 + n)
                    for k in range(part * KO // 4, (part + 1) * KO // 4):
                        if i == 0:
                            pe.wait_ge(w_split, k + 1)
                        high, low = oT_hi[:, i % 2, k, :], oT_lo[:, i % 2, k, :]
                        pe.matmul(y_ps[:, n, :], high, w_hi(k)[:, cols], start=(k == 0), stop=False)
                        pe.matmul(y_ps[:, n, :], high, w_lo[:, k, cols], start=False, stop=False)
                        last = pe.matmul(y_ps[:, n, :], low, w_hi(k)[:, cols], start=False, stop=(k == KO - 1))
                    if part == 3:
                        last.then_inc(y_done, 1)
                    if i == TILES - 1 and n == 1 and part < 3:
                        last.then_inc(w_used, 1)

            def turn_x(i):
                pe.wait_ge(xn_ready, i + 1)
                wait(pe, xT_copied, i)
                for k in range(KD):
                    last = pe.transpose(xT_ps[:, k // 4, k % 4, :], xn[:, i % 2, k * P:(k + 1) * P], ident)
                last.then_inc(xT_done, 1)

            def route(i):
                part, place = (0, i) if i < SAMPLE_TILES else (1, i - SAMPLE_TILES)
                if i == 0:
                    pe.wait_ge(small_landed, 32)
                if i == SAMPLE_TILES:
                    pe.wait_ge(choice[0], 1)
                pe.wait_ge(xT_copied, i + 1)
                for k in range(KD):
                    last = pe.matmul(logits_ps[part][:, place, :], xnT[:, k, :], w_r[:, k, :], start=(k == 0),
                                     stop=(k == KD - 1))
                last.then_inc(router_done, 1)

            def turn_aff(part):
                pe.wait_ge(aff_ready, part + 1)
                if part == 1:
                    pe.wait_ge(logits_ready, 1)
                for t in range(COUNT_OF[part]):
                    last = pe.transpose(affT_ps[part][:, t * P:(t + 1) * P], aff[:, TILES_OF[part].start + t, :], ident)
                last.then_inc(affT_done, 1)

            turn_o(0)
            for i in range(TILES):
                project(i, 0)
                if i == LAST_SAMPLE + 2:
                    turn_aff(0)
                project(i, 1)
                if i + 1 < TILES:
                    turn_o(i + 1)
                if i:
                    turn_x(i - 1)
                project(i, 2)
                if i:
                    route(i - 1)
                project(i, 3)
            turn_x(TILES - 1)
            route(TILES - 1)
            turn_aff(1)
            pe.wait_ge(chosen_ready, 4)
            pe.wait_ge(logits_ready, 2)
            for what in range(2):
                last = pe.transpose(lists_ps[:, what, :], chosen[:, what, :], shared.ident[0:EXPERTS, 0:EXPERTS])
            last.then_inc(chosenT_done, 1)
    s.end()


def moe_block(nc, io, shared, layer):
    with ExitStack() as stack:
        s = Space(nc, stack, f"m{layer}_")
        raw = shared.raw
        hi = s.sb("w_hi", [P, SPLITS, 2, D], F32R)
        lo = s.sb("w_lo", [P, SPLITS, 2, D], F32R)
        xe = s.sb("xe", [CAP, D])
        xeT_hi = s.sb("xeT_hi", [P, 2, KD, CAP], F32R)
        xeT_lo = s.sb("xeT_lo", [P, 2, KD, CAP], F32R)
        silu = s.sb("silu", [CAP, FF])
        hid = s.sb("hid", [CAP, FF])
        hidT_hi = s.sb("hidT_hi", [P, KD, CAP], F32R)
        hidT_lo = s.sb("hidT_lo", [P, KD, CAP], F32R)
        ye = s.sb("ye", [CAP, D])
        row_gather = s.sb("row_gather", [CAP, 1], U32)
        row_scatter = s.sb("row_scatter", [CAP, 1], U32)
        gate_ps = s.psum("gate", [CAP, FF])
        up_ps = s.psum("up", [CAP, FF])
        down_ps = s.psum("down", [CAP, D])
        T_ps = s.psum("turned", [P, KD, P])

        hi_ready, lo_ready, split_used = s.sem("hi_ready"), s.sem("lo_ready"), s.sem("split_used")
        first_rows_ready, rows_ready, gathered = s.sem("first_rows_ready"), s.sem("rows_ready"), s.sem("gathered")
        scatter_rows_ready, scattered = s.sem("scatter_rows_ready"), s.sem("scattered")
        T_done, T_hi, T_lo = s.sem("T_done"), s.sem("T_hi"), s.sem("T_lo")
        silu_ready, hid_ready, ye_ready = s.sem("silu_ready"), s.sem("hid_ready"), s.sem("ye_ready")
        block = stack.enter_context(nc.Block())

        LAST = EXPERTS - 1

        def loop_experts(engine, step):
            step(0, 0)
            step(1, 1)
            with engine.Fori(1, EXPERTS // 2 - 1) as i:
                step(i * 2, 0)
                step(i * 2 + 1, 1)
            step(LAST - 1, 0)
            step(LAST, 1)

        def is_last(e):
            return isinstance(e, int) and e == LAST

        def pieces(e):
            slots = [0, 1, 2, 3, 8, 9, 10, 11] if is_last(e) else list(range(SLOTS))
            return list(enumerate(slots))

        def q_of(e, place):
            return e * SLOTS + 4 + place

        def wait_low(engine, e, place):
            engine.wait_ge(lo_ready, q_of(e, place) + 1)

        @block.sync
        def _(sp):
            def load(e, matrix, j, first_slot):
                src = matrix[layer].rearrange("e (c k p) n -> e c p k n", c=4, p=P)[bass.ds(e, 1), j]
                sp.dma_start(raw[:, first_slot + j, :].rearrange("p (k n) -> p k n", k=2),
                             src.rearrange("e p k n -> (e p) k n")).then_inc(shared.landed[first_slot + j], 16)

            for j in range(4):
                sp.wait_ge(lo_ready, j + 1)
                load(1, io.w_gate, j, 4)

            def step(e):
                for j in range(4):
                    wait_low(sp, e - 1, j)
                    load(e, io.w_up, j, 0)
                if not is_last(e):
                    for j in range(4):
                        wait_low(sp, e - 1, 4 + j)
                        load(e + 1, io.w_gate, j, 4)
                for j in range(4):
                    wait_low(sp, e - 1, 8 + j)
                    load(e, io.w_down, j, 8)

            with sp.Fori(1, LAST) as e:
                step(e)
            step(LAST)

        @block.gpsimd
        def _(pool):
            def gather(e, rows_ready, count):
                wait(pool, gathered, e * 16)
                wait(pool, T_done, e if isinstance(e, int) and e < 2 else e * 2 - 2)
                pool.tensor_copy(row_gather[:, :], shared.row_of[:, bass.ds(e, 1)]).then_inc(rows_ready, 1)
                pool.wait_ge(shared.lists_ready, 2 * layer + 2)
                pool.wait_ge(rows_ready, count)
                pool.indirect_dma_start(out=xe[:, :], out_offset=None, in_=io.xn,
                                        in_offset=bass.IndirectOffsetOnAxis(ap=row_gather[:, :], axis=0)
                                        ).then_inc(gathered, 16)

            def scatter(e):
                wait(pool, scattered, e * 16)
                pool.tensor_copy(row_scatter[:, :], shared.row_of[:, bass.ds(e, 1)]).then_inc(scatter_rows_ready, 1)
                pool.wait_ge(shared.lists_ready, 2 * layer + 2)
                pool.wait_ge(scatter_rows_ready, e + 1)
                pool.wait_ge(ye_ready, e + 1)
                pool.indirect_dma_start(out=io.acc, out_offset=bass.IndirectOffsetOnAxis(ap=row_scatter[:, :], axis=0),
                                        in_=ye[:, :], in_offset=None, compute_op=ALU.add).then_inc(scattered, 16)

            def step(e, ahead):
                if not (isinstance(e, int) and e == 0):
                    scatter(e - 1)
                if ahead:
                    if isinstance(e, int) and e == 0:
                        gather(2, first_rows_ready, 3)
                    else:
                        gather(e + 2, rows_ready, e)

            gather(0, first_rows_ready, 1)
            gather(1, first_rows_ready, 2)
            step(0, True)
            step(1, True)
            with pool.Fori(2, LAST - 1) as e:
                step(e, True)
            step(LAST - 1, False)
            step(LAST, False)
            scatter(LAST)
            pool.wait_ge(scattered, 16 * EXPERTS)

        @block.scalar
        def _(act):
            def high(q, split, slot, landed):
                act.wait_ge(shared.landed[slot], landed)
                wait(act, split_used, q + 1 - SPLITS)
                act.activation(hi[:, split, :, :].rearrange("p k n -> p (k n)"), raw[:, slot, :],
                               ACT.Copy).then_inc(hi_ready, 1)

            def turned(dst, n):
                act.wait_ge(T_done, n)
                act.activation(dst, T_ps[:, :, 0:CAP], ACT.Copy).then_inc(T_hi, 1)

            def gate_out(e, done):
                act.wait_ge(split_used, done)
                wait(act, hid_ready, e)
                act.activation(silu[:, :], gate_ps[:, :], ACT.Silu).then_inc(silu_ready, 1)

            def down_out(e, done):
                act.wait_ge(split_used, done)
                wait(act, scattered, e * 16)
                act.activation(ye[:, :], down_ps[:, :], ACT.Copy,
                               scale=shared.gate_of[:, bass.ds(e, 1)]).then_inc(ye_ready, 1)

            base = 16 * layer * EXPERTS
            for j in range(4):
                if j == 2:
                    turned(xeT_hi[:, 0, :, :], 1)
                high(j, j % SPLITS, 4 + j, base + 16)

            def step(e, parity):
                for place, slot in pieces(e):
                    ahead = 1 if 4 <= slot < 8 else 0
                    high(q_of(e, place), (4 + place) % SPLITS, slot, (e + ahead) * 16 + base + 16)
                    if place == 2:
                        if isinstance(e, int) and e == 0:
                            gate_out(0, 4)
                    if place == 3 and not is_last(e):
                        turned(xeT_hi[:, 1 - parity, :, :], e * 2 + 2)
                    if place == 3 and not (isinstance(e, int) and e == 0):
                        down_out(e - 1, q_of(e, 0))
                    if place == (5 if is_last(e) else 8):
                        turned(hidT_hi[:, :, :], e * 2 + (2 if is_last(e) else 3))
                    if place == 10:
                        gate_out(e + 1, q_of(e, 8))
                if is_last(e):
                    down_out(e, q_of(e, 8))

            loop_experts(act, step)

        @block.vector
        def _(dve):
            def low(q, split, slot):
                dve.wait_ge(hi_ready, q + 1)
                wait(dve, split_used, q + 1 - SPLITS)
                dve.tensor_tensor(lo[:, split, :, :].rearrange("p k n -> p (k n)"), raw[:, slot, :],
                                  hi[:, split, :, :].rearrange("p k n -> p (k n)"),
                                  ALU.subtract).then_inc(lo_ready, 1)

            def turned(dst, high_part, n):
                dve.wait_ge(T_hi, n)
                dve.tensor_tensor(dst, T_ps[:, :, 0:CAP], high_part, ALU.subtract).then_inc(T_lo, 1)

            for j in range(4):
                if j == 1:
                    turned(xeT_lo[:, 0, :, :], xeT_hi[:, 0, :, :], 1)
                low(j, j % SPLITS, 4 + j)

            def step(e, parity):
                for place, slot in pieces(e):
                    low(q_of(e, place), (4 + place) % SPLITS, slot)
                    if place == 3 and not is_last(e):
                        turned(xeT_lo[:, 1 - parity, :, :], xeT_hi[:, 1 - parity, :, :], e * 2 + 2)
                    if place == 5:
                        dve.wait_ge(silu_ready, e + 1)
                        dve.wait_ge(split_used, q_of(e, 4))
                        wait(dve, T_done, 2 * e + 1)
                        dve.tensor_tensor(hid[:, :], silu[:, :], up_ps[:, :], ALU.mult).then_inc(hid_ready, 1)
                    if place == (5 if is_last(e) else 8):
                        turned(hidT_lo[:, :, :], hidT_hi[:, :, :], e * 2 + (2 if is_last(e) else 3))

            loop_experts(dve, step)

        @block.tensor
        def _(pe):
            def turn(src, n):
                wait(pe, T_lo, n)
                for k in range(KD):
                    last = pe.transpose(T_ps[:, k, 0:CAP], src[:, k * P:(k + 1) * P], shared.ident[0:CAP, 0:CAP])
                last.then_inc(T_done, 1)

            def products(out, left_hi, left_lo, j, split, q):
                for half in range(2):
                    cols = slice(half * SAMPLE, (half + 1) * SAMPLE)
                    for kk in range(2):
                        k = 2 * j + kk
                        pe.matmul(out[:, cols], left_hi[:, k, :], hi[:, split, kk, cols], start=(k == 0), stop=False)
                        pe.matmul(out[:, cols], left_hi[:, k, :], lo[:, split, kk, cols], start=False, stop=False)
                        last = pe.matmul(out[:, cols], left_lo[:, k, :], hi[:, split, kk, cols], start=False,
                                         stop=(k == KD - 1))
                last.then_inc(split_used, 1)

            pe.wait_ge(gathered, 16)
            turn(xe, 0)
            pe.wait_ge(T_lo, 1)
            for j in range(4):
                pe.wait_ge(lo_ready, j + 1)
                products(gate_ps, xeT_hi[:, 0], xeT_lo[:, 0], j, j % SPLITS, j)

            def step(e, parity):
                for place, slot in pieces(e):
                    split = (4 + place) % SPLITS
                    if slot == 0:
                        wait(pe, hid_ready, e)
                    if slot == 4:
                        pe.wait_ge(silu_ready, e + 1)
                        pe.wait_ge(T_lo, e * 2 + 2)
                    if slot == 8:
                        if not (isinstance(e, int) and e == 0):
                            pe.wait_ge(ye_ready, e)
                        if is_last(e):
                            pe.wait_ge(hid_ready, e + 1)
                            turn(hid, e * 2 + 1)
                        pe.wait_ge(T_lo, e * 2 + (2 if is_last(e) else 3))
                    if slot == 1 and not is_last(e):
                        pe.wait_ge(gathered, e * 16 + 32)
                        turn(xe, e * 2 + 1)
                    if slot == 6:
                        pe.wait_ge(hid_ready, e + 1)
                        turn(hid, e * 2 + 2)
                    wait_low(pe, e, place)
                    q = q_of(e, place)
                    if slot < 4:
                        products(up_ps, xeT_hi[:, parity], xeT_lo[:, parity], slot, split, q)
                    elif slot < 8:
                        products(gate_ps, xeT_hi[:, 1 - parity], xeT_lo[:, 1 - parity], slot - 4, split, q)
                    else:
                        products(down_ps, hidT_hi, hidT_lo, slot - 8, split, q)

            loop_experts(pe, step)
    s.end()


def final_block(nc, io, shared):
    with ExitStack() as stack:
        s = Space(nc, stack, "f_")
        x = s.sb("x", [P, TILES, D])
        y = s.sb("y", [P, TILES, D])
        gain = s.sb("gain", [P, D])
        ssq, mean, rstd = s.sb("ssq", [P, TILES]), s.sb("mean", [P, TILES]), s.sb("rstd", [P, TILES])
        half = s.sb("minus_half", [P, 1])
        gain_landed, x_landed = s.sem("gain_landed"), [s.sem(f"x_landed{t}") for t in range(TILES)]
        half_ready, ssq_ready, mean_ready = s.sem("half_ready"), s.sem("ssq_ready"), s.sem("mean_ready")
        rstd_ready, y_ready, stored = s.sem("rstd_ready"), s.sem("y_ready"), s.sem("stored")
        block = stack.enter_context(nc.Block())

        @block.sync
        def _(sp):
            sp.dma_start(gain[:, :], row_broadcast(io.g_final)).then_inc(gain_landed, 16)
            for t in range(TILES):
                sp.dma_start(x[:, t, :], io.acc[t * P:(t + 1) * P, :]).then_inc(x_landed[t], 16)
            for t in range(TILES):
                sp.wait_ge(y_ready, t + 1)
                sp.dma_start(token_rows(io.y_prompt, io.y_sample, t), y[:, t, :]).then_inc(stored, 16)
            sp.wait_ge(stored, 16 * TILES)

        @block.scalar
        def _(act):
            for t in range(TILES):
                act.wait_ge(x_landed[t], 16)
                act.activation(y[:, t, :], x[:, t, :], ACT.Square, accum_out=ssq[:, t:t + 1]).then_inc(ssq_ready, 1)

        @block.gpsimd
        def _(pool):
            pool.memset(half[:, :], -0.5).then_inc(half_ready, 1)
            pool.wait_ge(half_ready, 1)
            for t in range(TILES):
                pool.wait_ge(ssq_ready, t + 1)
                pool.tensor_scalar(mean[:, t:t + 1], ssq[:, t:t + 1], 1.0 / D, EPS,
                                   ALU.mult, ALU.add).then_inc(mean_ready, 1)
                pool.wait_ge(mean_ready, t + 1)
                pool.tensor_tensor(rstd[:, t:t + 1], mean[:, t:t + 1], half[:, :], ALU.pow).then_inc(rstd_ready, 1)

        @block.vector
        def _(dve):
            dve.wait_ge(gain_landed, 16)
            for t in range(TILES):
                dve.wait_ge(rstd_ready, t + 1)
                dve.scalar_tensor_tensor(out=y[:, t, :], in0=x[:, t, :], scalar=rstd[:, t:t + 1], in1=gain[:, :],
                                         op0=ALU.mult, op1=ALU.mult).then_inc(y_ready, 1)
    s.end()


class Tensors:

    def __init__(self, t):
        self.x_prompt, self.x_sample, self.g_attn_a = t["x_prompt"], t["x_sample"], t["g_attn_a"]
        self.w_in_a, self.g_q_a, self.w_uq_a = t["w_in_a"], t["g_q_a"], t["w_uq_a"]
        self.g_kv_a, self.w_ukv_a, self.w_o_a = t["g_kv_a"], t["w_ukv_a"], t["w_o_a"]
        self.g_attn_b, self.w_qkv_b, self.g_qn_b = t["g_attn_b"], t["w_qkv_b"], t["g_qn_b"]
        self.g_kn_b, self.w_o_b, self.g_ffn = t["g_kn_b"], t["w_o_b"], t["g_ffn"]
        self.w_router, self.w_gate, self.w_up = t["w_router"], t["w_gate"], t["w_up"]
        self.w_down, self.g_final, self.rope_a_tok = t["w_down"], t["g_final"], t["rope_a_tok"]
        self.rope_a_T, self.rope_b, self.ident = t["rope_a_T"], t["rope_b"], t["ident"]
        self.y_prompt, self.y_sample, self.acc = t["y_prompt"], t["y_sample"], t["acc"]
        self.xn, self.o_a, self.o_b = t["xn"], t["o_a"], t["o_b"]


class Shared:

    def __init__(self, nc, stack, io):
        s = Space(nc, stack, "s_")
        self.io = io
        self.raw = s.sb("raw", [P, SLOTS, SLOT])
        self.raw_at = nc.sbuf_base - SLOTS * SLOT * 4
        self.ident = s.sb("ident", [P, P])
        self.row_of = s.sb("row_of", [CAP, EXPERTS], U32)
        self.gate_of = s.sb("gate_of", [CAP, EXPERTS])
        self.ident_landed = s.sem("ident_landed")
        self.w_o_landed = s.sem("w_o_landed")
        self.lists_ready = s.sem("lists_ready")
        self.landed = [s.sem(f"landed{j}") for j in range(SLOTS)]
        arena = self.raw.rearrange("p s n -> p (s n)")
        self.w_o_a = arena[:, (SLOTS - 4) * SLOT:].rearrange("p (k n) -> p k n", n=D)
        self.w_o_b = arena[:, (SLOTS - 8) * SLOT:].rearrange("p (k n) -> p k n", n=D)

    def over_raw(self, nc, name, shape, first_slot):
        return nc.alloc_sbuf_tensor_at(name, shape, F32R, offset=self.raw_at + first_slot * SLOT * 4)

    def load_first(self, sp, matrix, layer, first_slot, j):
        src = matrix[layer, 0].rearrange("(c k p) n -> c p k n", c=4, p=P)
        sp.dma_start(self.raw[:, first_slot + j, :].rearrange("p (k n) -> p k n", k=2),
                     src[j]).then_inc(self.landed[first_slot + j], 16)


def build(nc, io):
    with ExitStack() as stack:
        shared = Shared(nc, stack, io)
        mla_block(nc, io, shared)
        output_block(nc, io, shared, 0)
        moe_block(nc, io, shared, 0)
        gqa_block(nc, io, shared)
        output_block(nc, io, shared, 1)
        moe_block(nc, io, shared, 1)
        final_block(nc, io, shared)


def rope_constants():
    def angles(positions, d):
        inv = np.float32(THETA) ** -(np.arange(d // 2, dtype=np.float32) * np.float32(2.0) / np.float32(d))
        a = positions.astype(np.float32)[:, None] * inv[None, :].astype(np.float32)
        c, s = np.cos(a).astype(np.float32), np.sin(a).astype(np.float32)
        return np.concatenate([c, c], 1), np.concatenate([-s, s], 1)

    pos = np.concatenate([np.arange(PROMPT), np.arange(SAMPLE)])
    ca, sa = angles(pos, DR)
    tok = np.stack([ca, sa], 1).reshape(TILES, P, 2, DR).transpose(1, 0, 2, 3)
    turned = np.concatenate([ca.T, sa.T], 0)
    cr, sr = angles(pos // GRID_W, HD // 2)
    cc, sc = angles(pos % GRID_W, HD // 2)
    b = np.stack([np.concatenate([cr, cc], 1), np.concatenate([sr, sc], 1)], 1)
    b = b.reshape(TILES, P, 2, HD).transpose(1, 0, 2, 3)
    return {"rope_a_tok": np.ascontiguousarray(tok), "rope_a_T": np.ascontiguousarray(turned),
            "rope_b": np.ascontiguousarray(b), "ident": np.eye(P, dtype=np.float32)}


INPUTS = ["x_prompt", "x_sample", "g_attn_a", "w_in_a", "g_q_a", "w_uq_a", "g_kv_a", "w_ukv_a", "w_o_a",
          "g_attn_b", "w_qkv_b", "g_qn_b", "g_kn_b", "w_o_b", "g_ffn", "w_router", "w_gate", "w_up",
          "w_down", "g_final"]


def kernel(**inputs):
    import concourse.bacc as bacc
    from concourse.bass_utils import run_bass_kernel_spmd

    nc = bacc.Bacc("TRN2", target_bir_lowering=False, num_devices=1)
    arrays, io = {}, {}
    host = {name: np.ascontiguousarray(inputs[name]) for name in INPUTS} | rope_constants()
    for name, a in host.items():
        arrays[f"in_{name}"] = a
        io[name] = nc.dram_tensor(f"in_{name}", a.shape, mybir.dt.from_np(a.dtype), kind="ExternalInput").ap()
    for name, rows in (("y_prompt", PROMPT), ("y_sample", SAMPLE)):
        io[name] = nc.dram_tensor(f"out_{name}", (1, rows, D), F32, kind="ExternalOutput").ap()
    io["acc"] = nc.dram_tensor("acc", (N, D), F32, kind="Internal").ap()
    io["xn"] = nc.dram_tensor("xn", (N, D), F32, kind="Internal").ap()
    io["o_a"] = nc.dram_tensor("o_a", (N, HEADS * DV), F32, kind="Internal").ap()
    io["o_b"] = nc.dram_tensor("o_b", (N, HEADS * HD), F32, kind="Internal").ap()
    build(nc, Tensors(io))
    r = run_bass_kernel_spmd(nc, [arrays], core_ids=[0])
    return r.results[0]["out_y_prompt"], r.results[0]["out_y_sample"]
```
